# Optimizing a Trainium2 kernel written in Bass

```python
import math
import jax, jax.numpy as jnp
from jax import lax
import numpy as np

D_MODEL = 1024
BATCH = 1
SEQ = 256
DEPTH = 2

MEM_LEN = 256
XA_HEADS = 4
XA_HEAD_DIM = D_MODEL // XA_HEADS
D_FF = 256 * ((8 * D_MODEL // 3 + 255) // 256)
BRANCH_W = D_MODEL // 2
S5_GROUP = 16
S5_GROUPS = BRANCH_W // S5_GROUP
S5_STATE = 64
LRU_HEADS = 8
LRU_HEAD_DIM = BRANCH_W // LRU_HEADS
LRU_CONV = 4
LRU_C = 8.0
RW_HEAD_DIM = 64
RW_HEADS = BRANCH_W // RW_HEAD_DIM
RW_DECAY_RANK = 64
RW_A_RANK = 64
RW_GATE_RANK = 128
RW_COLS = 3 * BRANCH_W + RW_DECAY_RANK + RW_A_RANK + RW_GATE_RANK
N_BRANCH = 3
IN_COLS = BRANCH_W + 2 * BRANCH_W + RW_COLS + N_BRANCH * D_MODEL
IN_SPLITS = [BRANCH_W, 2 * BRANCH_W, 3 * BRANCH_W, 3 * BRANCH_W + RW_COLS]
RW_SPLITS = [BRANCH_W, 2 * BRANCH_W, 3 * BRANCH_W, 3 * BRANCH_W + RW_DECAY_RANK,
             3 * BRANCH_W + RW_DECAY_RANK + RW_A_RANK]
ALPHA = (2 * DEPTH) ** 0.25
BETA = (8 * DEPTH) ** -0.25
LN_EPS = 1e-5
RW_GN_EPS = 64e-5

kernel_name = "hybrid_s5_rglru_rwkv7_deepnorm_trunk"

F32 = jnp.float32

def layer_norm(x, g, b):
    xf = x.astype(F32)
    mu = jnp.mean(xf, -1, keepdims=True)
    var = jnp.mean(jnp.square(xf - mu), -1, keepdims=True)
    return ((xf - mu) * lax.rsqrt(var + LN_EPS) * g + b).astype(x.dtype)

def swiglu(x, wg, wu, wd):
    return (jax.nn.silu(x @ wg) * (x @ wu)) @ wd

def _lin_op(e1, e2):
    a1, b1 = e1
    a2, b2 = e2
    return a1 * a2, a2 * b1 + b2

def token_shift(z):
    return jnp.pad(z, ((0, 0), (1, 0), (0, 0)))[:, :-1]

def s5_branch(u, lam_re, lam_im, log_dt, b_re, b_im, c_re, c_im, d, glu_w1, glu_w2):
    bsz, seq, _ = u.shape
    uf = u.astype(F32).reshape(bsz, seq, S5_GROUPS, S5_GROUP)
    lam = lax.complex(lam_re.astype(F32), lam_im.astype(F32))
    dt = jnp.exp(log_dt.astype(F32))[:, None]
    lam_bar = jnp.exp(lam * dt)
    b_mat = lax.complex(b_re.astype(F32), b_im.astype(F32))
    c_mat = lax.complex(c_re.astype(F32), c_im.astype(F32))
    b_bar = ((lam_bar - 1.0) / lam)[..., None] * b_mat
    bu = jnp.einsum('bsgc,gpc->bsgp', uf.astype(jnp.complex64), b_bar)
    a_el = jnp.broadcast_to(lam_bar, (1, seq, S5_GROUPS, S5_STATE))
    _, states = lax.associative_scan(_lin_op, (a_el, bu), axis=1)
    y = jnp.real(jnp.einsum('bsgp,gcp->bsgc', states, c_mat))
    y = y + d.astype(F32).reshape(S5_GROUPS, S5_GROUP) * uf
    y = jax.nn.gelu(y.reshape(bsz, seq, BRANCH_W)).astype(u.dtype)
    return (y @ glu_w1) * jax.nn.sigmoid(y @ glu_w2)

def causal_depthwise_conv(x, w, b):
    ch = x.shape[-1]
    out = lax.conv_general_dilated(
        x, w[:, None, :].astype(x.dtype), window_strides=(1,), padding=[(LRU_CONV - 1, 0)],
        dimension_numbers=('NWC', 'WIO', 'NWC'), feature_group_count=ch)
    return out + b

def rglru_branch(zx, zy, conv_w, conv_b, wa, ba, wx, bx, lam, w_out):
    bsz, seq, _ = zx.shape
    xc = causal_depthwise_conv(zx, conv_w, conv_b)
    xh = xc.reshape(bsz, seq, LRU_HEADS, LRU_HEAD_DIM)
    gate_r = jax.nn.sigmoid((jnp.einsum('bshi,hij->bshj', xh, wa).reshape(bsz, seq, BRANCH_W) + ba).astype(F32))
    gate_i = jax.nn.sigmoid((jnp.einsum('bshi,hij->bshj', xh, wx).reshape(bsz, seq, BRANCH_W) + bx).astype(F32))
    log_a = -LRU_C * gate_r * jax.nn.softplus(-lam.astype(F32))
    a = jnp.exp(log_a)
    mult = jnp.sqrt(-jnp.expm1(2.0 * log_a))
    b_in = mult * gate_i * xc.astype(F32)
    _, h = lax.associative_scan(_lin_op, (a, b_in), axis=1)
    y = (h * jax.nn.gelu(zy.astype(F32))).astype(zx.dtype)
    return y @ w_out

def rwkv7_scan(r, w, k, v, a, b):
    bsz, _, h, n = r.shape

    def step(state, inp):
        r_t, w_t, k_t, v_t, a_t, b_t = inp
        sa = jnp.einsum('bhvk,bhk->bhv', state, a_t)
        state = (state * w_t[:, :, None, :] + sa[..., None] * b_t[:, :, None, :]
                 + v_t[..., None] * k_t[:, :, None, :])
        return state, jnp.einsum('bhvk,bhk->bhv', state, r_t)

    xs = tuple(jnp.moveaxis(t, 1, 0) for t in (r, w, k, v, a, b))
    _, ys = lax.scan(step, jnp.zeros((bsz, h, n, n), F32), xs)
    return jnp.moveaxis(ys, 0, 1)

def rwkv7_branch(z, mu, w0, w_up, a0, a_up, g_up, k_k, k_a, r_k, ln_g, ln_b, w_out):
    bsz, seq, _ = z.shape
    z = z + mu * (token_shift(z) - z)
    r, k, v, wd, ad, gd = jnp.split(z, RW_SPLITS, axis=-1)
    w_log = -jax.nn.softplus(-(w0 + jnp.tanh(wd) @ w_up).astype(F32)) - 0.5
    decay = jnp.exp(-jnp.exp(w_log))
    a = jax.nn.sigmoid((a0 + ad @ a_up).astype(F32))
    g = jax.nn.sigmoid(gd) @ g_up

    def heads(t):
        return t.astype(F32).reshape(bsz, seq, RW_HEADS, RW_HEAD_DIM)

    kk = heads(k * k_k)
    kk = kk * lax.rsqrt(jnp.sum(kk * kk, -1, keepdims=True) + 1e-12)
    k = k.astype(F32) * (1.0 + (a - 1.0) * k_a)
    rh, kh, vh, ah, wh = heads(r), heads(k), heads(v), heads(a), heads(decay)
    y = rwkv7_scan(rh, wh, kh, vh, -kk, kk * ah)
    y_mu = jnp.mean(y, -1, keepdims=True)
    y_var = jnp.mean(jnp.square(y - y_mu), -1, keepdims=True)
    y = ((y - y_mu) * lax.rsqrt(y_var + RW_GN_EPS)).reshape(bsz, seq, BRANCH_W) * ln_g + ln_b
    bonus = jnp.sum(rh * kh * r_k, -1, keepdims=True) * vh
    y = (y + bonus.reshape(bsz, seq, BRANCH_W)) * g
    return y.astype(z.dtype) @ w_out

def cross_attention(x, mem, wq, wkv, wo):
    bsz, seq, _ = x.shape
    q = (x @ wq).reshape(bsz, seq, XA_HEADS, XA_HEAD_DIM)
    k, v = jnp.split(mem @ wkv, 2, axis=-1)
    k = k.reshape(bsz, -1, XA_HEADS, XA_HEAD_DIM)
    v = v.reshape(bsz, -1, XA_HEADS, XA_HEAD_DIM)
    s = jnp.einsum('bshd,bmhd->bhsm', q, k).astype(F32) * (XA_HEAD_DIM ** -0.5)
    p = jax.nn.softmax(s, axis=-1).astype(x.dtype)
    o = jnp.einsum('bhsm,bmhd->bshd', p, v).reshape(bsz, seq, D_MODEL)
    return o @ wo

def setup_inputs(seed: int = 0) -> dict:
    key = jax.random.key(seed)
    ks = iter(jax.random.split(key, 64))
    L, D, F, W = DEPTH, D_MODEL, D_FF, BRANCH_W
    G, P, C = S5_GROUPS, S5_STATE, S5_GROUP

    def nrm(shape, scale):
        return jax.random.normal(next(ks), shape, F32) * scale

    def unif(shape, lo, hi):
        return jax.random.uniform(next(ks), shape, F32, lo, hi)

    def gain(shape):
        return 1.0 + nrm(shape, 0.02)

    lru_s = unif((L, W), 0.9, 0.999) ** (1.0 / LRU_C)
    inp = {}
    inp['x'] = nrm((BATCH, SEQ, D), 1.0)
    inp['mem'] = nrm((BATCH, MEM_LEN, D), 1.0)
    inp['ffn1_wg'] = nrm((L, D, F), D ** -0.5)
    inp['ffn1_wu'] = nrm((L, D, F), D ** -0.5)
    inp['ffn1_wd'] = nrm((L, F, D), BETA * F ** -0.5)
    inp['ln1_g'] = gain((L, D))
    inp['ln1_b'] = nrm((L, D), 0.01)
    inp['w_in'] = nrm((L, D, IN_COLS), D ** -0.5)
    inp['s5_lam_re'] = -0.5 + nrm((L, G, P), 0.01)
    inp['s5_lam_im'] = math.pi * jnp.arange(P, dtype=F32) + nrm((L, G, P), 0.01)
    inp['s5_log_dt'] = unif((L, G), math.log(1e-3), math.log(1e-1))
    inp['s5_b_re'] = nrm((L, G, P, C), (2 * C) ** -0.5)
    inp['s5_b_im'] = nrm((L, G, P, C), (2 * C) ** -0.5)
    inp['s5_c_re'] = nrm((L, G, C, P), (2 * P) ** -0.5)
    inp['s5_c_im'] = nrm((L, G, C, P), (2 * P) ** -0.5)
    inp['s5_d'] = nrm((L, W), 1.0)
    inp['s5_glu_w1'] = nrm((L, W, D), W ** -0.5)
    inp['s5_glu_w2'] = nrm((L, W, D), W ** -0.5)
    inp['lru_conv_w'] = nrm((L, LRU_CONV, W), LRU_CONV ** -0.5)
    inp['lru_conv_b'] = nrm((L, W), 0.01)
    inp['lru_wa'] = nrm((L, LRU_HEADS, LRU_HEAD_DIM, LRU_HEAD_DIM), LRU_HEAD_DIM ** -0.5)
    inp['lru_ba'] = nrm((L, W), 0.01)
    inp['lru_wx'] = nrm((L, LRU_HEADS, LRU_HEAD_DIM, LRU_HEAD_DIM), LRU_HEAD_DIM ** -0.5)
    inp['lru_bx'] = nrm((L, W), 0.01)
    inp['lru_lambda'] = jnp.log(lru_s) - jnp.log1p(-lru_s)
    inp['lru_w_out'] = nrm((L, W, D), W ** -0.5)
    inp['rw_mu'] = unif((L, RW_COLS), 0.0, 1.0)
    inp['rw_w0'] = jnp.linspace(-6.0, -1.0, W, dtype=F32) + nrm((L, W), 0.1)
    inp['rw_w_up'] = nrm((L, RW_DECAY_RANK, W), 0.1 * RW_DECAY_RANK ** -0.5)
    inp['rw_a0'] = nrm((L, W), 0.1)
    inp['rw_a_up'] = nrm((L, RW_A_RANK, W), 0.1 * RW_A_RANK ** -0.5)
    inp['rw_g_up'] = nrm((L, RW_GATE_RANK, W), RW_GATE_RANK ** -0.5)
    inp['rw_k_k'] = 0.85 + nrm((L, W), 0.02)
    inp['rw_k_a'] = gain((L, W))
    inp['rw_r_k'] = nrm((L, RW_HEADS, RW_HEAD_DIM), 0.1)
    inp['rw_ln_g'] = gain((L, W))
    inp['rw_ln_b'] = nrm((L, W), 0.01)
    inp['rw_w_out'] = nrm((L, W, D), W ** -0.5)
    inp['mix_w_out'] = nrm((L, D, D), BETA * D ** -0.5)
    inp['ln2_g'] = gain((L, D))
    inp['ln2_b'] = nrm((L, D), 0.01)
    inp['xa_wq'] = nrm((L, D, D), D ** -0.5)
    inp['xa_wkv'] = nrm((L, D, 2 * D), D ** -0.5)
    inp['xa_wo'] = nrm((L, D, D), BETA * D ** -0.5)
    inp['ln3_g'] = gain((L, D))
    inp['ln3_b'] = nrm((L, D), 0.01)
    inp['ffn2_wg'] = nrm((L, D, F), D ** -0.5)
    inp['ffn2_wu'] = nrm((L, D, F), D ** -0.5)
    inp['ffn2_wd'] = nrm((L, F, D), BETA * F ** -0.5)
    inp['ln4_g'] = gain((L, D))
    inp['ln4_b'] = nrm((L, D), 0.01)
    return inp

def reference(x, mem, ffn1_wg, ffn1_wu, ffn1_wd, ln1_g, ln1_b, w_in,
              s5_lam_re, s5_lam_im, s5_log_dt, s5_b_re, s5_b_im, s5_c_re, s5_c_im, s5_d,
              s5_glu_w1, s5_glu_w2,
              lru_conv_w, lru_conv_b, lru_wa, lru_ba, lru_wx, lru_bx, lru_lambda, lru_w_out,
              rw_mu, rw_w0, rw_w_up, rw_a0, rw_a_up, rw_g_up, rw_k_k, rw_k_a, rw_r_k,
              rw_ln_g, rw_ln_b, rw_w_out,
              mix_w_out, ln2_g, ln2_b,
              xa_wq, xa_wkv, xa_wo, ln3_g, ln3_b,
              ffn2_wg, ffn2_wu, ffn2_wd, ln4_g, ln4_b):
    bsz, seq, _ = x.shape
    for l in range(DEPTH):
        x = layer_norm(ALPHA * x + 0.5 * swiglu(x, ffn1_wg[l], ffn1_wu[l], ffn1_wd[l]), ln1_g[l], ln1_b[l])
        z = x @ w_in[l]
        z_s5, z_lx, z_ly, z_rw, z_gate = jnp.split(z, IN_SPLITS, axis=-1)
        y_s5 = s5_branch(z_s5, s5_lam_re[l], s5_lam_im[l], s5_log_dt[l], s5_b_re[l], s5_b_im[l],
                         s5_c_re[l], s5_c_im[l], s5_d[l], s5_glu_w1[l], s5_glu_w2[l])
        y_lru = rglru_branch(z_lx, z_ly, lru_conv_w[l], lru_conv_b[l], lru_wa[l], lru_ba[l],
                             lru_wx[l], lru_bx[l], lru_lambda[l], lru_w_out[l])
        y_rw = rwkv7_branch(z_rw, rw_mu[l], rw_w0[l], rw_w_up[l], rw_a0[l], rw_a_up[l], rw_g_up[l],
                            rw_k_k[l], rw_k_a[l], rw_r_k[l], rw_ln_g[l], rw_ln_b[l], rw_w_out[l])
        gates = jax.nn.sigmoid(z_gate.reshape(bsz, seq, N_BRANCH, D_MODEL))
        merged = gates[:, :, 0] * y_s5 + gates[:, :, 1] * y_lru + gates[:, :, 2] * y_rw
        x = layer_norm(ALPHA * x + merged @ mix_w_out[l], ln2_g[l], ln2_b[l])
        x = layer_norm(ALPHA * x + cross_attention(x, mem, xa_wq[l], xa_wkv[l], xa_wo[l]), ln3_g[l], ln3_b[l])
        x = layer_norm(ALPHA * x + 0.5 * swiglu(x, ffn2_wg[l], ffn2_wu[l], ffn2_wd[l]), ln4_g[l], ln4_b[l])
    return x


_drawn_inputs = setup_inputs


def setup_inputs(seed=0):
    import zlib

    import numpy as np

    out = dict(_drawn_inputs(seed))
    spreads = {}
    factors = {'ln1_b': 3.478,
     's5_lam_re': 64.0,
     's5_lam_im': 64.0,
     's5_log_dt': 64.0,
     's5_b_re': 64.0,
     's5_b_im': 64.0,
     's5_c_re': 64.0,
     's5_c_im': 64.0,
     'lru_conv_b': 8.0,
     'lru_ba': 200.0,
     'lru_bx': 64.0,
     'rw_w_up': 8.0,
     'rw_a0': 8.0,
     'rw_a_up': 8.0,
     'rw_k_k': 130.291,
     'rw_k_a': 8.0,
     'rw_ln_g': 8.0,
     'rw_ln_b': 35.707,
     'ln2_b': 3.469,
     'ln3_b': 3.683,
     'ln4_b': 3.533}
    for name, (base, spread) in spreads.items():
        noise = np.random.default_rng([zlib.crc32(name.encode()), seed]).standard_normal(out[name].shape)
        drawn = base * np.exp(spread * noise) if base else spread * noise
        out[name] = __import__('jax').numpy.asarray(drawn.astype(out[name].dtype))
    for name, factor in factors.items():
        out[name] = (out[name] * factor).astype(out[name].dtype)
    return out
```

```python
from contextlib import ExitStack

import concourse.bass as bass
import numpy as np
from concourse import mybir

ALU = mybir.AluOpType
ACT = mybir.ActivationFunctionType
AX = mybir.AxisListType
F32 = mybir.dt.float32
F32R = mybir.dt.float32r

P = 128
D = 1024
T = 256
M = 256
L = 2
F = 2816
W = 512
NF = F // P
ND = D // P
NW = W // P
NT = T // P
NS = 16
C = 64
NC = T // C
NQ = NW * NC
XH = 4
RW0 = 3 * W
RWT = 14
GATE0 = RW0 + RWT * P
ALPHA = (2 * L) ** 0.25
LN_EPS = 1e-5
GN_EPS = 64e-5
RAW = 3
SPLIT = 2
PIECE = 1024
EDEC = float(np.exp(-0.5))
MAGIC = 1.5 * 2.0 ** 23
TWO_PI = 2.0 * np.pi
PI_A = 6.28125
PI_B = float(np.float32(TWO_PI - PI_A).view(np.uint32) & np.uint32(0xFFFFF000)) and float(
    np.array([np.float32(TWO_PI - PI_A).view(np.uint32) & np.uint32(0xFFFFF000)], np.uint32).view(np.float32)[0])
PI_C = float(TWO_PI - PI_A - PI_B)

ROWS_A = [("lam_re", NS), ("lam_im", NS), ("log_dt", NS), ("s5_d", NW), ("conv_w", 4 * NW), ("conv_b", NW),
          ("ba", NW), ("bx", NW), ("lam", NW), ("mu", RWT), ("w0", NW), ("a0", NW), ("k_k", NW), ("k_a", NW),
          ("r_k", NW), ("gn_g", NW), ("gn_b", NW)]
ROWS_B = [(f"ln{n}_{x}", ND) for n in range(4) for x in "gb"]

CONST = [("ident", P), ("heads", P), ("maskG", P), ("strict", C)] + \
        [(f"off{b}", C) for b in (1, 2, 4, 8, 16, 32)] + \
        [("eye2", C), ("time", T), ("reset", T), ("half_state", 2), ("half_chan", 2), ("cols", 8)]


def columns(rows, start=0):
    at, where = start, {}
    for name, n in rows:
        where[name] = (at, n)
        at += n
    return where, at


CCOL, NCONST = columns(CONST)
PCOL_A, NA = columns(ROWS_A)
PCOL_B, NB = columns(ROWS_B, P)


def constants():
    c = np.zeros((P, NCONST), np.float32)

    def put(name, value):
        a, n = CCOL[name]
        c[:, a:a + n] = value

    p, j = np.arange(P)[:, None], np.arange(P)[None, :]
    i, jc = p % C, np.arange(C)[None, :]
    put("ident", p == j)
    put("heads", p // C == j // C)
    s, t, is_k, is_r = p % C, j % C, p >= C, j >= C
    put("maskG", np.where(is_r, s <= t, is_k & (s < t)))
    put("strict", jc < i)
    for b in (1, 2, 4, 8, 16, 32):
        put(f"off{b}", (i // (2 * b) == jc // (2 * b)) & (i % (2 * b) >= b) & (jc % (2 * b) < b))
    put("eye2", i == jc)
    put("time", np.arange(T)[None, :])
    put("reset", np.arange(T)[None, :] % C != 0)
    put("half_state", p // C == np.arange(2)[None, :])
    put("half_chan", (p // 16) % 2 == np.arange(2)[None, :])
    put("cols", np.array([np.pi / 2, 1e-12, GN_EPS, -0.5, LN_EPS / ALPHA ** 2, 1.0, 0.0, 0.0], np.float32)[None, :])
    return c


def ffn_items(i):
    out = []
    for j in range(NF // 2):
        out += [(f"g{i}", j), (f"u{i}", j)]
        if i == 0 and j == 0:
            out.append(("rowsT", 0))
        if i == 0 and j == 7:
            out.append(("bcT", 0))
        if j >= 1:
            out.append((f"d{i}", j - 1))
    return out + [(f"d{i}", NF // 2 - 1)]


def plan():
    zs = [("z", j) for j in (0, 1, 6, 7, 8, 9, 10, 11, 12, 2, 3, 4, 5)]
    mid = [("gate", j) for j in range(4)] + [("w1", 0), ("w2", 0), ("w1", 1), ("w2", 1)]
    mid += [("gate", j) for j in range(4, 8)] + [("lru", 0), ("lru", 1)] + [("gate", j) for j in range(8, 12)]
    mid += [("memT", 0)] + [("k", j) for j in range(4)] + [("v", 0), ("rw", 0), ("rw", 1), ("v", 1)]
    mid += [("mix", j) for j in range(4)] + [("v", 2), ("v", 3)]
    out = ffn_items(0) + [("lnT", 0)] + zs + mid + [("lnT", 1)] + [("q", j) for j in range(4)]
    return out + [("wo", j) for j in range(4)] + [("lnT", 2)] + ffn_items(1) + [("lnT", 3)]


BANKS_OF = {"rowsT": 1, "memT": 4, "bcT": 4, "lnT": 4, "g0": 1, "u0": 1, "g1": 1, "u1": 1, "z": 1, "gate": 1, "w1": 2, "w2": 2,
            "lru": 2, "rw": 2, "k": 1, "v": 1, "q": 1}
NOT_WEIGHTS = ("rowsT", "bcT", "memT", "lnT")
PLAN = plan()
FFN_KINDS = "gud"
PIECES = [(kind, j, m) for kind, j in PLAN if kind not in NOT_WEIGHTS for m in range(2)]
INDEX = {x: n for n, x in enumerate(PIECES)}
PLAIN = ("w1", "w2", "lru", "rw")
SPLIT_AT = {}
LO_AT = {}
for _n, _x in enumerate(PIECES):
    if _x[0] not in PLAIN:
        _who = "pool" if _x[0] == "gate" else "dve"
        SPLIT_AT[_n] = len(SPLIT_AT)
        LO_AT[_n] = (_who, sum(w == _who for w, _ in LO_AT.values()))
SPLITS = list(SPLIT_AT)
ROTA = [(x, b) for x in PLAN for b in range(BANKS_OF.get(x[0], 0))]
ROTA_AT = {x: n for n, x in enumerate(ROTA)}
ZORD = [x[1] for x in PLAN if x[0] == "z"]


def trunk(nc, io, consts, out):
    with ExitStack() as ctx:
        cursor = [(nc.sbuf_base + 63) // 32 * 32]

        def sb(name, n, dtype=F32):
            t = nc.alloc_sbuf_tensor_at(name, [P, n], dtype, offset=cursor[0])
            cursor[0] += 4 * n
            return t, cursor[0] - 4 * n

        def rounded(name, place, at, *dims):
            n = 1
            for d in dims:
                n *= d
            return view(nc.alloc_sbuf_tensor_at(name, [P, n], F32R, offset=place + 4 * at), 0, *dims)

        def sem(name):
            s = nc.alloc_semaphore(name)
            sems.append(s)
            return s

        sems = []

        raw, _ = sb("ring_raw", RAW * PIECE)
        ring_hi, _ = sb("ring_hi", SPLIT * PIECE, F32R)
        ring_lo, _ = sb("ring_lo", SPLIT * PIECE, F32R)
        xtok_t, _ = sb("x_tok", NT * D)
        xTh_t, _ = sb("xT_hi", ND * T, F32R)
        xTl_t, _ = sb("xT_lo", ND * T, F32R)
        reg_a, a_at = sb("region_a", 6144)
        reg_r, r_at = sb("region_r", 8192)
        reg_z, _ = sb("region_z", 4 * T + RWT * (T + 1) + 4 * (T + 3) + 4 * T + 6)
        work, w_at = sb("work", 12288)
        cst, _ = sb("constants", (NCONST + 7) // 8 * 8)
        pcol, _ = sb("param_columns", 2 * P)
        small, _ = sb("small", 512)
        wgate, _ = sb("lru_gate_weights", 2 * NW * P)
        ups, _ = sb("up_weights", 2 * W)
        bT, _ = sb("s5_b", 2 * NW * P)
        cT, _ = sb("s5_c", 2 * NW * P)

        def view(region, at, *dims):
            n = 1
            for d in dims:
                n *= d
            v = region[:, at:at + n]
            if len(dims) == 1:
                return v
            names = "abcd"[:len(dims)]
            return v.rearrange(f"p ({' '.join(names)}) -> p {' '.join(names)}",
                               **{x: d for x, d in zip(names[1:], dims[1:])})

        def const(name):
            a, n = CCOL[name]
            return cst[:, a:a + n]

        def ccol(k):
            a = CCOL["cols"][0]
            return cst[:, a + k:a + k + 1]

        HALF_PI, TINY, GNE, NEG_HALF, LNE, ONE, ZERO = (ccol(k) for k in range(7))
        ident = const("ident")

        def pc(name, k=0, n=1):
            a = (PCOL_A if name in PCOL_A else PCOL_B)[name][0]
            return pcol[:, a + k:a + k + n]

        xtok = view(xtok_t, 0, NT, D)
        xT = [view(xTh_t, 0, ND, T), view(xTl_t, 0, ND, T)]
        hT = [rounded("hT_hi", a_at, 0, NF, T), rounded("hT_lo", w_at, 6144, NF, T)]
        gates = view(reg_a, 0, ND, T)
        merged = view(reg_a, 2048, ND, T)
        BK = view(reg_a, 4096, NW, NC, 2, C)
        attn_p = view(reg_a, 0, XH, NT, M)
        attn_pT = view(reg_a, 2048, XH, 2, T)
        oT = [rounded("oT_hi", a_at, 4096, ND, T), rounded("oT_lo", w_at, 8192, ND, T)]
        cosT = view(reg_r, 0, NS, T)
        sinT = view(reg_r, 4096, NS, T)
        G = view(reg_r, 0, NQ * 2, P)
        BKtok = view(reg_r, 4096, NQ, P)
        SV = view(reg_r, 6144, NC, 8, C)
        memT = [rounded("memT_hi", r_at, 0, ND, M), rounded("memT_lo", r_at, 2048, ND, M)]
        kmT = view(reg_r, 4096, ND, M)
        vm = view(reg_r, 6144, 2, D)
        zu = view(reg_z, 0, NW, T)
        zrw = view(reg_z, 1024, RWT, T + 1)
        V_AT = 1024 + 8 * (T + 1)
        LX_AT = 1024 + RWT * (T + 1)
        lx = view(reg_z, LX_AT, NW, T + 3)
        ly = view(reg_z, LX_AT + NW * (T + 3), NW, T)
        memtok = view(reg_z, LX_AT, 2, D)
        b_raw = [view(reg_z, 256 * i, NS, 16) for i in range(2)]
        c_raw = [view(reg_z, 512 + 256 * i, NW, C) for i in range(2)]
        b_bd = [view(reg_z, 1024 + 512 * i, NW, P) for i in range(2)]
        c_bd = [view(reg_z, 2048 + 512 * i, NW, P) for i in range(2)]
        rot = [view(reg_z, 3072 + 1024 * i, 4, T) for i in range(3)]
        prow = view(reg_z, 6144, 2, P)
        Wst = view(reg_z, 1024, NQ, C)
        Ysb = view(reg_z, 2048, NQ, C)
        tmpB = view(reg_z, 3072, NQ, C)
        yT = view(reg_z, 1024, NW, T)
        AR = view(work, 0, NW, NC, 2, C)
        gRW = view(work, 2048, NW, T)
        bonus = view(work, 3072, NW, T)
        wk = [view(work, 4096 + 1024 * i, NW, T) for i in range(8)]
        W_bd = view(work, 4096, NQ, P)
        M_bd = view(work, 6144, NQ, P)
        X_bd = view(work, 8192, NQ, P)
        Usb = view(work, 10240, NW, C)
        S0 = [view(work, 10496 + 256 * i, NW, C) for i in range(2)]
        lnbc = view(work, 0, 2, D)
        sil = [view(work, 4096 + 512 * i, 512) for i in range(2)]
        htmp = [view(work, 5120 + 512 * i, 512) for i in range(2)]
        bt_tmp = [view(work, 11776 + 256 * i, NS, 16) for i in range(2)]
        xf = view(work, 6144, ND, T)
        qT = view(work, 4096, ND, T)
        merged_r = [rounded("merged_hi", w_at, 7168, ND, T), rounded("merged_lo", w_at, 9216, ND, T)]
        s5m = view(work, 0, 2, 2, T)
        s5v = view(work, 1024, 2, T)
        s5z = [view(work, 1536 + 512 * i, 2, T) for i in range(2)]
        s5n = view(work, 2560, 2, 2, T)
        s5s = [view(work, 3584 + 512 * i, 2, T) for i in range(2)]
        mtmp = view(work, 11264, NW, T)
        col = {}
        at = [0]

        def small_cols(name, n):
            col[name] = small[:, at[0]:at[0] + n]
            at[0] += n
            return col[name]

        stats = [small_cols(f"stats{t}", 12) for t in range(NT)]
        mv = [small_cols(f"mv{t}", 2) for t in range(NT)]
        vare = [small_cols(f"vare{t}", 1) for t in range(NT)]
        rstd = [small_cols(f"rstd{t}", 1) for t in range(NT)]
        dt_, xr, rho, th, em, den = (small_cols(n, NS) for n in ("dt", "xr", "rho", "th", "em", "den"))
        ang, rnd, phi, s1, c1, aab = (small_cols(n, NS) for n in ("ang", "rnd", "phi", "s1", "c1", "aab"))
        nre, nim, fr, fi, t1, t2 = (small_cols(n, NS) for n in ("nre", "nim", "fr", "fi", "t1", "t2"))
        dt_raw = small_cols("dt_raw", 2)
        u_, w_, w2_, pl = (small_cols(n, NW) for n in ("u", "w", "w2", "pl"))
        sp8, sp8n, omka, alam = (small_cols(n, NW) for n in ("sp8", "sp8n", "omka", "alam"))
        pC = small_cols("pC", NQ).rearrange("p (t c) -> p t c", t=NW)
        nmax, rsum, rinv = (small_cols(n, 2 * XH) for n in ("nmax", "rsum", "rinv"))
        assert at[0] <= 512

        banks = [ctx.enter_context(nc.psum_tensor(f"bank{b}", [P, 512], F32)) for b in range(8)]

        def bank(b, *dims):
            names = "abcd"[:len(dims)]
            if len(dims) <= 1:
                return banks[b][:, :]
            return banks[b][:, :].rearrange(f"p ({' '.join(names)}) -> p {' '.join(names)}",
                                            **{x: d for x, d in zip(names[1:], dims[1:])})

        def rota(kind, j, b=0):
            return ROTA_AT[((kind, j), b)] % 4

        s_pre = nc.alloc_semaphore("prologue_loaded")
        s_preT = nc.alloc_semaphore("prologue_turned")
        s_preX = nc.alloc_semaphore("prologue_split")
        s_preA = nc.alloc_semaphore("prologue_act")
        s_preD = nc.alloc_semaphore("prologue_dve")
        s_zero = nc.alloc_semaphore("zeros_written")
        s_end = nc.alloc_semaphore("layer_ended")
        s_go = {e: nc.alloc_semaphore(f"next_layer_{e}") for e in ("pe", "act", "dve", "pool")}
        s_out = nc.alloc_semaphore("output_stored")

        s_w = [sem(f"weights_loaded{i}") for i in range(RAW)]
        s_piece = sem("piece_multiplied")
        s_hi = sem("weights_hi")
        s_lo = {"dve": sem("weights_lo_dve"), "pool": sem("weights_lo_pool")}
        s_hh = sem("hidden_hi")
        s_hl = sem("hidden_lo")
        s_xTp = sem("xT_lo_from_pool")
        s_mh = sem("merged_hi")
        s_ml = sem("merged_lo")
        s_memTl = sem("memory_lo")
        s_oh = sem("o_hi")
        s_par = sem("parameters_loaded")
        s_raw = sem("s5_matrices_loaded")
        s_lnw = sem("ln_weights_loaded")
        s_memld = sem("memory_loaded")
        s_rowsT = sem("parameter_rows_turned")
        s_pcol = sem("parameter_columns")
        s_silu = sem("silu_done")
        s_h = sem("hidden_done")
        s_lny = sem("ln_residual_read")
        s_lnv = sem("ln_variance")
        s_lnr = sem("ln_rstd")
        s_lnx = sem("ln_normalised")
        s_lnT = sem("ln_turned")
        s_xTa = sem("xT_from_act")
        s_xTd = sem("xT_from_dve")
        s_xg = sem("x_tok_gain_applied")
        s_p1 = sem("prep_dve")
        s_p2 = sem("prep_act")
        s_p3 = sem("prep_pool")
        s_bcT = sem("bc_turned")
        s_bce = sem("bc_evac_act")
        s_rot = sem("rotation_dve")
        s_rots = sem("rotation_act")
        s_z = sem("z_evacuated")
        s_bu = sem("s5_bu")
        s_fwd = sem("s5_rotated")
        s_scan = sem("s5_scanned")
        s_back = sem("s5_rotated_back")
        s_y5 = sem("s5_y")
        s_y5d = sem("s5_y_plus_du")
        s_ys5 = sem("s5_gelu")
        s_conv = sem("lru_conv")
        s_lg = sem("lru_gates_product")
        s_lga = sem("lru_gates_act")
        s_lq = sem("lru_square")
        s_lm = sem("lru_multiplier")
        s_yl = sem("lru_y")
        s_shift = sem("rwkv_shifted")
        s_lora_in = sem("rwkv_lora_input")
        s_lora = sem("rwkv_lora_product")
        s_lora_a = sem("rwkv_lora_act")
        s_kk = sem("rwkv_kk")
        s_sq = sem("rwkv_kk_squared")
        s_ss = sem("rwkv_kk_sums")
        s_nrm = sem("rwkv_kk_norm")
        s_dec = sem("rwkv_decay_sums")
        s_exp = sem("rwkv_exponentials")
        s_ex = sem("rwkv_exponentials_used")
        s_rk = sem("rwkv_rk")
        s_rks = sem("rwkv_rk_scaled")
        s_bon = sem("rwkv_bonus_sums")
        s_ops = sem("rwkv_operands")
        s_tok = sem("rwkv_turned")
        s_toke = sem("rwkv_turned_evac_act")
        s_tokv = sem("rwkv_turned_evac_dve")
        s_G = sem("rwkv_G")
        s_Ge = sem("rwkv_G_masked")
        s_N = sem("rwkv_N")
        s_Nb = sem("rwkv_N_masked")
        s_Wb = sem("rwkv_W_dve")
        s_Wp = sem("rwkv_W_pool")
        s_tmp = sem("rwkv_W_step")
        s_T = sem("rwkv_solve_turned")
        s_Ta = sem("rwkv_solve_evac_act")
        s_Td = sem("rwkv_solve_evac_dve")
        s_Y = sem("rwkv_Y")
        s_Ye = sem("rwkv_Y_evac")
        s_WY = sem("rwkv_WY")
        s_U = sem("rwkv_U")
        s_Ue = sem("rwkv_U_evac")
        s_Sa = sem("rwkv_Sa")
        s_Sae = sem("rwkv_Sa_evac")
        s_Sn = sem("rwkv_state_product")
        s_S = sem("rwkv_state")
        s_y = sem("rwkv_y")
        s_ye = sem("rwkv_y_evac")
        s_mean = sem("rwkv_mean")
        s_yc = sem("rwkv_centred")
        s_ysq = sem("rwkv_centred_squared")
        s_var = sem("rwkv_variance")
        s_gnr = sem("rwkv_std")
        s_yrw = sem("rwkv_gated")
        s_gact = sem("gates_activated")
        s_glu = sem("glu_sigmoid")
        s_m = sem("merged_banks_read")
        s_acc0 = sem("token_tile_0_multiplied")
        s_bonr = sem("rwkv_bonus_read")
        s_dtx = sem("log_dt_rows_spread")
        s_zz = sem("row_zeros_written")
        s_kv = sem("memory_kv_evac")
        s_memT = sem("memory_turned")
        s_memTe = sem("memory_turned_evac")
        s_q = sem("q_evac")
        s_sc = sem("scores")
        s_mx = sem("score_max")
        s_ex2 = sem("softmax_exp")
        s_pn = sem("softmax_normalised")
        s_pT = sem("p_turned")
        s_pTe = sem("p_turned_evac")
        s_o = sem("o_product")
        s_oe = sem("o_evac")
        c_act, c_dve, c_pool = sem("act_chain"), sem("dve_chain"), sem("pool_chain")

        CLEAR = range(sems[0].num, sems[-1].num + 1)
        assert [s.num for s in sems] == list(CLEAR)

        def released(item, b):
            kind, j = item
            if kind in ("g0", "u0"):
                return s_h, j + 1
            if kind in ("g1", "u1"):
                return s_h, NF // 2 + j + 1
            if kind == "rowsT":
                return s_pcol, 1
            if kind == "bcT":
                return (s_bce, b + 1)
            if kind == "memT":
                return s_memTl, b + 1
            if kind == "lnT":
                return (s_xTa, 2 * j + b + 1) if b < 2 else (s_xTd, 2 * j + b - 1)
            if kind == "z":
                return s_z, ZORD.index(j) + 1
            if kind == "gate":
                return s_gact, j + 1
            if kind == "w2":
                return s_glu, 2 * j + b + 1
            if kind == "w1":
                return s_m, 2 * j + b + 1
            if kind == "lru":
                return s_m, 4 + 2 * j + b + 1
            if kind == "rw":
                return s_m, 8 + 2 * j + b + 1
            if kind == "k":
                return s_kv, j + 1
            if kind == "v":
                return s_kv, 4 + j + 1
            if kind == "q":
                return s_q, j + 1
            raise KeyError(kind)

        def source(l, kind, j, m):
            def rows(w, k0, nk, c0, n):
                part = w[l, bass.ds(k0 * P, nk * P), bass.ds(c0, n)]
                return part.rearrange("(k p) n -> p k n", p=P), nk, n
            if kind in PLAIN:
                w = {"w1": "s5_glu_w1", "w2": "s5_glu_w2", "lru": "lru_w_out", "rw": "rw_w_out"}[kind]
                return rows(io[w], 0, NW, 512 * j + 256 * m, 256)
            if kind in ("d0", "d1", "mix", "wo"):
                w = {"d0": "ffn1_wd", "d1": "ffn2_wd", "mix": "mix_w_out", "wo": "xa_wo"}[kind]
                return rows(io[w], j * 2 + m, 1, 0, D)
            w, c0 = {"g0": ("ffn1_wg", 0), "u0": ("ffn1_wu", 0), "g1": ("ffn2_wg", 0), "u1": ("ffn2_wu", 0),
                     "z": ("w_in", 0), "gate": ("w_in", GATE0), "k": ("xa_wkv", 0), "v": ("xa_wkv", D),
                     "q": ("xa_wq", 0)}[kind]
            return rows(io[w], 0, ND, j * 256 + (c0 + P * m), P)

        def slot(ring, i, nk, cols):
            return ring[:, i * PIECE:i * PIECE + nk * cols].rearrange("p (k n) -> p k n", k=nk)

        def loaded(eng, n):
            eng.wait_ge(s_w[n % RAW], 16 * (n // RAW + 1))

        def raw_flat(n):
            return raw[:, (n % RAW) * PIECE:(n % RAW + 1) * PIECE]

        def split_flat(ring, f):
            return ring[:, (f % SPLIT) * PIECE:(f % SPLIT + 1) * PIECE]

        def split_index(kind, j, m=1, ahead=0):
            return min(SPLIT_AT[INDEX[(kind, j, m)]] + ahead, len(SPLITS) - 1)

        def done_chunk(eng, kind, j):
            eng.wait_ge(s_piece, INDEX[(kind, j, 1)] + 1)

        class Steps:

            def __init__(self, eng, chain):
                self.eng, self.chain, self.n = eng, chain, {}

            def mark(self, ins, s):
                ins.then_inc(s, 1)
                self.n[s.name] = self.n.get(s.name, 0) + 1
                return self.n[s.name]

            def then(self, ins, s=None):
                s = s or self.chain
                self.eng.wait_ge(s, self.mark(ins, s))

        def layer_end(eng, who):
            eng.drain().then_inc(s_end, 1)
            eng.wait_ge(s_go[who], 1)
            eng.sem_clear(s_go[who])

        block = ctx.enter_context(nc.Block())

        @block.sync
        def _(sp):
            sp.dma_start(cst[:, 0:NCONST], consts).then_inc(s_pre, 16)
            sp.dma_start(xtok, io["x"][0].rearrange("(t p) d -> p t d", p=P)).then_inc(s_pre, 16)
            with sp.Fori(0, L) as l:
                def piece(n, step=0):
                    kind, j, m = PIECES[n]
                    if n >= RAW and n - RAW in LO_AT:
                        who, i = LO_AT[n - RAW]
                        sp.wait_ge(s_lo[who], 2 * len(FFN_KINDS) * step + i + 1)
                    elif n >= RAW:
                        sp.wait_ge(s_piece, n - RAW + 1)
                    src, nk, cols = source(l, kind, j + step, m)
                    sp.dma_start(slot(raw, n % RAW, nk, cols), src).then_inc(s_w[n % RAW], 16)

                def ffn(i):
                    n0 = INDEX[(f"g{i}", 0, 0)]
                    for n in range(n0, n0 + 4):
                        piece(n)
                    with sp.Fori(0, NF // 2 - 1) as step:
                        for n in range(n0 + 4, n0 + 4 + 2 * len(FFN_KINDS)):
                            piece(n, step)
                    n = INDEX[(f"d{i}", NF // 2 - 1, 0)]
                    piece(n)
                    piece(n + 1)

                ffn(0)
                for n in range(INDEX[("d0", NF // 2 - 1, 1)] + 1, INDEX[("g1", 0, 0)]):
                    piece(n)
                ffn(1)
                sp.wait_ge(s_end, 4)
                sp.sem_clear(CLEAR)
                sp.sem_clear(s_end)
                sp.drain()
                for who in ("pe", "act", "dve", "pool"):
                    sp.sem_inc(s_go[who], 1)
            sp.dma_start(out[0].rearrange("(t p) d -> p t d", p=P), xtok).then_inc(s_out, 16)
            sp.wait_ge(s_out, 16)

        @block.tensor
        def _(pe):
            mm = nc.tensor.matmul

            def claim(kind, j, b=0):
                r = ROTA_AT[((kind, j), b)]
                if r >= 4:
                    s, v = released(*ROTA[r - 4])
                    pe.wait_ge(s, v)
                return banks[r % 4]

            def take(kind, j, m):
                n = INDEX[(kind, j, m)]
                who, i = LO_AT[n]
                pe.wait_ge(s_lo[who], i + 1)
                _, nk, cols = source(0, kind, j, m)
                return [slot(ring, SPLIT_AT[n] % SPLIT, nk, cols) for ring in (ring_hi, ring_lo)]

            def mm3(o, a, b, first, last):
                mm(o, a[0], b[0], start=first, stop=False)
                mm(o, a[0], b[1], start=False, stop=False)
                return mm(o, a[1], b[0], start=False, stop=last)

            def half_chunk(kind, j, m, src):
                if kind in PLAIN:
                    n = INDEX[(kind, j, m)]
                    loaded(pe, n)
                    w, o = slot(raw, n % RAW, NW, 256), claim(kind, j, m)
                    for c in range(2):
                        for k in range(NW):
                            last = mm(o[:, c * T:(c + 1) * T], w[:, k, c * P:(c + 1) * P], src[:, k, :],
                                      start=(k == 0), stop=(k == NW - 1))
                else:
                    if m == 0:
                        claim(kind, j)
                    o = banks[rota(kind, j)]
                    w = take(kind, j, m)
                    for k in range(ND):
                        last = mm3(o[:, m * T:(m + 1) * T], [x[:, k, :] for x in w], [x[:, k, :] for x in src],
                                   k == 0, k == ND - 1)
                last.then_inc(s_piece, 1)

            def by_channel(kind, j, src):
                for m in range(2):
                    half_chunk(kind, j, m, src)

            def by_token(kind, j, src, first, last_chunk):
                for m in range(2):
                    w = take(kind, j, m)
                    end = last_chunk and m == 1
                    for t in range(NT):
                        for h in range(2):
                            last = mm3(banks[4 + 2 * t + h][:, :], [x[:, 2 * j + m, t * P:(t + 1) * P] for x in src],
                                       [x[:, 0, 512 * h:512 * (h + 1)] for x in w], first and m == 0, end)
                        if end and t == 0:
                            last.then_inc(s_acc0, 1)
                    last.then_inc(s_piece, 1)

            def ffn(i):
                for kind, j in ffn_items(i):
                    if kind[0] in "gu":
                        by_channel(kind, j, xT)
                    elif kind == "rowsT":
                        o = claim("rowsT", 0)
                        pe.wait_ge(s_par, 16 * N_PAR_DMA)
                        pe.wait_ge(s_dtx, 1)
                        nc.tensor.transpose(o[:, 0:NA], prow[0:NA, 0, :], ident[0:NA, 0:NA])
                        nc.tensor.transpose(o[:, P:P + NB - P], prow[0:NB - P, 1, :], ident[0:NB - P, 0:NB - P])\
                            .then_inc(s_rowsT, 1)
                    elif kind == "bcT":
                        pe.wait_ge(s_p3, 4)
                        for b, src in enumerate(b_bd + c_bd):
                            o = claim("bcT", 0, b)
                            for t in range(NW):
                                last = nc.tensor.transpose(o[:, t * P:(t + 1) * P], src[:, t, :], ident)
                            last.then_inc(s_bcT, 1)
                    else:
                        if i == 1 and j == 0:
                            pe.wait_ge(s_lny, 3 * NT)
                        pe.wait_ge(s_hl, i * (NF // 2) + j + 1)
                        by_token(kind, j, hT, j == 0, j == NF // 2 - 1)

            def ln_turn(n):
                os = [claim("lnT", n, b) for b in range(4)]
                for t in range(NT):
                    pe.wait_ge(s_lnx, NT * n + t + 1)
                    for d in range(ND):
                        last = nc.tensor.transpose(os[d // 2][:, (d % 2) * T + t * P:(d % 2) * T + (t + 1) * P],
                                                   xtok[:, t, d * P:(d + 1) * P], ident)
                    last.then_inc(s_lnT, 1)

            def wait_xT(n):
                pe.wait_ge(s_xTa, 2 * n + 2)
                pe.wait_ge(s_xTd, 2 * n + 2)
                pe.wait_ge(s_xTp, 2 * n + 2)

            pe.wait_ge(s_pre, 32)
            for t in range(NT):
                for d in range(ND):
                    last = nc.tensor.transpose(banks[d // 2][:, (d % 2) * T + t * P:(d % 2) * T + (t + 1) * P],
                                               xtok[:, t, d * P:(d + 1) * P], ident)
            last.then_inc(s_preT, 1)
            pe.wait_ge(s_preX, 2)

            with pe.Fori(0, L) as l:
                ffn(0)
                ln_turn(0)
                wait_xT(0)

                zq = list(ZORD)

                def z_chunk():
                    by_channel("z", zq.pop(0), xT)

                def s5_in(s):
                    t, q = s // 4, s % 4
                    if s == 0:
                        pe.wait_ge(s_z, 2)
                        pe.wait_ge(s_bce, 4)
                        pe.wait_ge(s_lny, 2)
                    if s >= 2:
                        pe.wait_ge(s_fwd, s - 1)
                    o = bank(4 + s % 2, 2, T)
                    for i in range(2):
                        last = mm(o[:, i, :], view(bT, 512 * i, NW, P)[32 * q:32 * q + 32, t, :],
                                  zu[32 * q:32 * q + 32, t, :], start=True, stop=True)
                    last.then_inc(s_bu, 1)

                def s5_out(s):
                    t, q = s // 4, s % 4
                    if q == 0 and t >= 2:
                        pe.wait_ge(s_y5d, t - 1)
                    pe.wait_ge(s_back, s + 1)
                    o = banks[6 + t % 2][32 * q:32 * q + 32, 0:T]
                    for i in range(2):
                        last = mm(o, view(cT, 512 * i, NW, P)[:, t, 32 * q:32 * q + 32], s5s[s % 2][:, i, :],
                                  start=(i == 0), stop=(i == 1))
                    last.then_inc(s_y5, 1)

                z_chunk()
                z_chunk()
                s5_in(0)
                s5_in(1)
                for s in range(NS):
                    if s % 2 == 0:
                        z_chunk()
                    if s >= 1:
                        s5_out(s - 1)
                    if s + 2 < NS:
                        s5_in(s + 2)
                while zq:
                    z_chunk()
                s5_out(NS - 1)

                def gate(j):
                    by_channel("gate", j, xT)

                gate(0)
                gate(1)
                pe.wait_ge(s_conv, NW)
                pe.wait_ge(s_y5d, NW)
                pe.wait_ge(s_fwd, NS)
                for g in range(2):
                    for t in range(NW):
                        last = mm(bank(4 + 2 * g + t // 2, 2, T)[:, t % 2, :], view(wgate, 512 * g, NW, P)[:, t, :],
                                  wk[1][:, t, :], start=True, stop=True)
                    last.then_inc(s_lg, 1)
                gate(2)
                pe.wait_ge(s_lora_in, 2)
                pe.wait_ge(s_shift, RWT)
                for t in range(NW):
                    if t % 2 == 0:
                        pe.wait_ge(s_lga, 8)
                    last = mm(bank(4 + t // 2, 2, T)[:, t % 2, :], ups[0:C, t * P:(t + 1) * P],
                              wk[7][0:C, 0, :], start=True, stop=True)
                last.then_inc(s_lora, 1)
                for t in range(NW):
                    last = mm(bank(6 + t // 2, 2, T)[:, t % 2, :], ups[C:P, t * P:(t + 1) * P],
                              zrw[C:P, 12, 1:T + 1], start=True, stop=True)
                last.then_inc(s_lora, 1)
                gate(3)
                pe.wait_ge(s_lora_a, 4)
                for t in range(NW):
                    last = mm(bank(4 + t // 2, 2, T)[:, t % 2, :], ups[:, W + t * P:W + (t + 1) * P],
                              wk[7][:, 1, :], start=True, stop=True)
                last.then_inc(s_lora, 1)
                pe.wait_ge(s_lora_a, 8)
                pe.wait_ge(s_sq, 1)
                for h in range(2):
                    last = mm(banks[6 + h][:, :], const("heads"), wk[6][:, 2 * h:2 * h + 2, :], start=True, stop=True)
                last.then_inc(s_ss, 1)
                def glu(j):
                    if j == 0:
                        pe.wait_ge(s_ys5, NW)
                    by_channel("w1", j, zu)
                    by_channel("w2", j, zu)

                glu(0)
                pe.wait_ge(s_lora_a, 10)
                pe.wait_ge(s_rks, NW)
                for h in range(2):
                    last = mm(banks[4 + h][:, :], const("heads"), wk[7][:, 2 * h:2 * h + 2, :], start=True, stop=True)
                last.then_inc(s_bon, 1)
                pe.wait_ge(s_ops, 1)
                pe.wait_ge(s_nrm, 1)
                pe.wait_ge(s_bonr, 1)
                for q in range(NQ):
                    last = nc.tensor.transpose(banks[4 + q // 4][:, (q % 4) * P:(q % 4 + 1) * P],
                                               BK[:, q // NC, q % NC, :, :], ident)
                last.then_inc(s_tok, 1)
                pe.wait_ge(s_toke, 2)
                pe.wait_ge(s_tokv, 2)
                for q in range(NQ):
                    t, c = q // NC, q % NC
                    a = V_AT + t * (T + 1) + 1 + C * c - C
                    last = nc.tensor.transpose(banks[4 + q // 4][:, (q % 4) * P:(q % 4 + 1) * P],
                                               reg_z[:, a:a + P], ident)
                last.then_inc(s_tok, 1)
                for g in range(4):
                    if g == 0:
                        pe.wait_ge(s_toke, 4)
                        pe.wait_ge(s_tokv, 4)
                    if g >= 2:
                        pe.wait_ge(s_Ge, 2 * (g - 1))
                    for i in range(4):
                        q = 4 * g + i
                        for par in range(2):
                            r = slice(C * par, C * par + C)
                            last = mm(banks[4 + 2 * (g % 2) + par][:, i * P:(i + 1) * P], BK[r, q // NC, q % NC, :, :],
                                      AR[r, q // NC, q % NC, :, :], start=True, stop=True)
                    last.then_inc(s_G, 1)
                glu(1)
                pe.wait_ge(s_Ge, 8)
                for q in range(NQ):
                    for par in range(2):
                        r = slice(C * par, C * par + C)
                        last = mm(banks[4 + 2 * par + q // 8][r, (q % 8) * C:(q % 8 + 1) * C],
                                  AR[r, q // NC, q % NC, 0, :], BK[r, q // NC, q % NC, 0, :], start=True, stop=True)
                last.then_inc(s_N, 1)
                gate(4)

                def turn_pairs(src):
                    for q in range(NQ):
                        last = nc.tensor.transpose(banks[4 + q // 4][:, (q % 4) * P:(q % 4 + 1) * P], src[:, q, :],
                                                   ident)
                    last.then_inc(s_T, 1)

                pe.wait_ge(s_Nb, 8)
                turn_pairs(W_bd)
                fill = [("gate", 5, xT), ("gate", 6, xT), ("gate", 7, xT), ("lru", 0, ly), ("lru", 1, ly)]
                pe.wait_ge(s_Wb, 1)
                pe.wait_ge(s_Wp, 1)
                pe.wait_ge(s_Ta, 1)
                pe.wait_ge(s_Td, 1)
                turn_pairs(W_bd)
                for i in range(5):
                    if i == 3:
                        pe.wait_ge(s_yl, NW)
                    pe.wait_ge(s_Ta, i + 2)
                    pe.wait_ge(s_Td, i + 2)
                    for q in range(NQ):
                        last = mm(banks[4 + q // 8][:, (q % 8) * C:(q % 8 + 1) * C], M_bd[:, q, :], Wst[:, q, :],
                                  start=True, stop=True)
                    last.then_inc(s_Y, 1)
                    kind, j, src = fill[i]
                    half_chunk(kind, j, 0, src)
                    pe.wait_ge(s_Ye, i + 1)
                    for q in range(NQ):
                        last = mm(banks[6 + q // 8][:, (q % 8) * C:(q % 8 + 1) * C], X_bd[:, q, :], Ysb[:, q, :],
                                  start=True, stop=True)
                    last.then_inc(s_WY, 1)
                    half_chunk(kind, j, 1, src)
                    pe.wait_ge(s_Wb, i + 2)
                    pe.wait_ge(s_Wp, i + 2)
                    turn_pairs(W_bd)

                pe.wait_ge(s_Ta, 7)
                pe.wait_ge(s_Td, 7)
                for c in range(NC):
                    if c >= 1:
                        pe.wait_ge(s_ye, 2 * c)
                    for h in range(8):
                        t, par = h // 2, h % 2
                        q = t * NC + c
                        r = slice(C * par, C * par + C)
                        last = mm(banks[4 + par][r, t * C:(t + 1) * C], G[:, 2 * q + par, 0:C], SV[:, c, h, :],
                                  start=(t == 0), stop=(c == 0), skip_group_check=True)
                    if c >= 1:
                        pe.wait_ge(s_S, c)
                        for h in range(8):
                            t, par = h // 2, h % 2
                            r = slice(C * par, C * par + C)
                            last = mm(banks[4 + par][r, t * C:(t + 1) * C], AR[r, t, c, 0, :], S0[c % 2][r, t, :],
                                      start=False, stop=True, skip_group_check=True)
                    last.then_inc(s_U, 1)
                    half_chunk("gate", 8 + c, 0, xT)
                    pe.wait_ge(s_Ue, 2 * (c + 1))
                    for h in range(8):
                        t, par = h // 2, h % 2
                        last = mm(banks[6][0:C, h * C:(h + 1) * C], X_bd[:, t * NC + c, C * par:C * par + C],
                                  Usb[:, t, :], start=True, stop=True)
                    last.then_inc(s_Sa, 1)
                    half_chunk("gate", 8 + c, 1, xT)
                    pe.wait_ge(s_Sae, c + 1)
                    if c < NC - 1:
                        for h in range(8):
                            t, par = h // 2, h % 2
                            r = slice(C * par, C * par + C)
                            last = mm(banks[7][r, t * C:(t + 1) * C], BKtok[:, t * NC + c, C * par:C * par + C],
                                      SV[:, c, h, :], start=True, stop=True)
                        last.then_inc(s_Sn, 1)
                    for h in range(8):
                        t, par = h // 2, h % 2
                        q = t * NC + c
                        r = slice(C * par, C * par + C)
                        o = banks[4 + par][r, 256 + t * C:256 + (t + 1) * C]
                        last = mm(o, SV[:, c, h, :], G[:, 2 * q + par, C:P], start=(t == 0), stop=(c == 0),
                                  skip_group_check=True)
                    if c >= 1:
                        for h in range(8):
                            t, par = h // 2, h % 2
                            r = slice(C * par, C * par + C)
                            last = mm(banks[4 + par][r, 256 + t * C:256 + (t + 1) * C], S0[c % 2][r, t, :],
                                      AR[r, t, c, 1, :], start=False, stop=True, skip_group_check=True)
                    last.then_inc(s_y, 1)
                pe.wait_ge(s_ye, 2 * NC)
                for h in range(2):
                    last = mm(banks[4 + h][:, :], const("heads"), yT[:, 2 * h:2 * h + 2, :], start=True, stop=True)
                last.then_inc(s_mean, 1)
                pe.wait_ge(s_memld, 16)
                os = [claim("memT", 0, b) for b in range(4)]
                for b in range(4):
                    for d in (2 * b, 2 * b + 1):
                        for t in range(2):
                            last = nc.tensor.transpose(os[b][:, (d % 2) * M + t * P:(d % 2) * M + (t + 1) * P],
                                                       memtok[:, t, d * P:(d + 1) * P], ident)
                    last.then_inc(s_memT, 1)
                pe.wait_ge(s_memTl, 4)

                def memory_values(j):
                    claim("v", j)
                    o = banks[rota("v", j)]
                    for m in range(2):
                        w = take("v", j, m)
                        for t in range(2):
                            for k in range(ND):
                                last = mm3(o[:, t * 256 + m * P:t * 256 + (m + 1) * P],
                                           [x[:, k, t * P:(t + 1) * P] for x in memT], [x[:, k, :] for x in w],
                                           k == 0, k == ND - 1)
                        last.then_inc(s_piece, 1)

                by_channel("k", 0, memT)
                pe.wait_ge(s_ysq, 1)
                for h in range(2):
                    last = mm(banks[6 + h][:, :], const("heads"), wk[1][:, 2 * h:2 * h + 2, :], start=True, stop=True)
                last.then_inc(s_var, 1)
                for j in range(1, 4):
                    by_channel("k", j, memT)
                memory_values(0)
                pe.wait_ge(s_yrw, 1)
                by_channel("rw", 0, wk[0])
                by_channel("rw", 1, wk[0])
                memory_values(1)
                pe.wait_ge(s_gnr, 1)
                for j in range(4):
                    pe.wait_ge(s_ml, j + 1)
                    by_token("mix", j, merged_r, j == 0, j == 3)
                memory_values(2)
                memory_values(3)
                ln_turn(1)
                wait_xT(1)

                def scores(h):
                    pe.wait_ge(s_q, h + 1)
                    if h == 0:
                        pe.wait_ge(s_kv, 8)
                    for t in range(NT):
                        for d in range(2):
                            last = mm(banks[4 + h][:, t * M:(t + 1) * M], qT[:, 2 * h + d, t * P:(t + 1) * P],
                                      kmT[:, 2 * h + d, :], start=(d == 0), stop=(d == 1))
                    last.then_inc(s_sc, 1)

                def turn_p(h):
                    pe.wait_ge(s_pn, h + 1)
                    for t in range(NT):
                        for m in range(2):
                            last = nc.tensor.transpose(banks[4 + h][:, m * T + t * P:m * T + (t + 1) * P],
                                                       attn_p[:, h, t, m * P:(m + 1) * P], ident)
                    last.then_inc(s_pT, 1)

                def values(h):
                    pe.wait_ge(s_pTe, h + 1)
                    for d in range(2):
                        for m in range(2):
                            last = mm(banks[4 + h][:, d * T:(d + 1) * T], vm[:, m, (2 * h + d) * P:(2 * h + d + 1) * P],
                                      attn_pT[:, h, m, :], start=(m == 0), stop=(m == 1))
                    last.then_inc(s_o, 1)

                by_channel("q", 0, xT)
                by_channel("q", 1, xT)
                scores(0)
                by_channel("q", 2, xT)
                scores(1)
                turn_p(0)
                by_channel("q", 3, xT)
                scores(2)
                turn_p(1)
                values(0)
                scores(3)
                turn_p(2)
                values(1)
                turn_p(3)
                values(2)
                values(3)
                pe.wait_ge(s_oe, XH)
                for j in range(4):
                    by_token("wo", j, oT, j == 0, j == 3)
                ln_turn(2)
                wait_xT(2)
                ffn(1)
                ln_turn(3)
                layer_end(pe, "pe")

        @block.scalar
        def _(act):
            st = Steps(act, c_act)

            def f(o, i, func, **kw):
                return nc.scalar.activation(o, i, func, **kw)

            hi_at = [0]

            def hi_to(kind, j, m=1, ahead=0):
                while hi_at[0] <= split_index(kind, j, m, ahead):
                    i = hi_at[0]
                    if i >= SPLIT:
                        act.wait_ge(s_piece, SPLITS[i - SPLIT] + 1)
                    loaded(act, SPLITS[i])
                    st.mark(f(split_flat(ring_hi, i), raw_flat(SPLITS[i]), ACT.Copy), s_hi)
                    hi_at[0] += 1

            def ln(n):
                act.wait_ge(s_lnT, NT * n + NT)
                for b in range(2):
                    src = bank(rota("lnT", n, b), 2, T)
                    for m in range(2):
                        d = 2 * b + m
                        ins = f(xf[:, d, :], src[:, m, :], ACT.Identity, scale=pc(f"ln{n}_g", d), bias=pc(f"ln{n}_b", d))
                    st.then(ins)
                    st.mark(f(xT[0][:, 2 * b:2 * b + 2, :], xf[:, 2 * b:2 * b + 2, :], ACT.Copy), s_xTa)

            def silu(i, j):
                hi_to(f"u{i}", j, 0)
                done_chunk(act, f"g{i}", j)
                if i * (NF // 2) + j >= 2:
                    act.wait_ge(s_h, i * (NF // 2) + j - 1)
                st.mark(f(sil[j % 2], banks[rota(f"g{i}", j)][:, :], ACT.Silu), s_silu)

            def hidden_hi(i, j):
                hi_to(f"u{i}", j, 1, ahead=1)
                act.wait_ge(s_h, i * (NF // 2) + j + 1)
                st.mark(f(hT[0][:, 2 * j:2 * j + 2, :].rearrange("p a t -> p (a t)"), htmp[j % 2], ACT.Copy), s_hh)

            def rotation(q):
                act.wait_ge(s_rot, 4 * q + 1)
                sl = slice(4 * q, 4 * q + 4)
                st.mark(f(sinT[:, sl, :], rot[0], ACT.Sin, scale=float(np.pi)), s_rots)
                act.wait_ge(s_rot, 4 * q + 2)
                st.mark(f(cosT[:, sl, :], rot[1], ACT.Sin, scale=-float(np.pi), bias=HALF_PI), s_rots)

            act.wait_ge(s_preT, 1)
            for b in range(2):
                ins = f(xf[:, 2 * b:2 * b + 2, :], bank(b, 2, T), ACT.Copy)
            ins.then_inc(s_preA, 1)
            act.wait_ge(s_preA, 1)
            f(xT[0][:, 0:4, :], xf[:, 0:4, :], ACT.Copy).then_inc(s_preA, 1)

            with act.Fori(0, L) as l:
                def rows(row, n, src, k=0):
                    act.dma_start(prow[row:row + n, k, :], src).then_inc(s_par, 16)
                    count[0] += 1

                count = [0]
                src = {"lam_re": "s5_lam_re", "lam_im": "s5_lam_im", "s5_d": "s5_d", "conv_w": "lru_conv_w",
                       "conv_b": "lru_conv_b", "ba": "lru_ba", "bx": "lru_bx", "lam": "lru_lambda", "mu": "rw_mu",
                       "w0": "rw_w0", "a0": "rw_a0", "k_k": "rw_k_k", "k_a": "rw_k_a", "r_k": "rw_r_k",
                       "gn_g": "rw_ln_g", "gn_b": "rw_ln_b"}
                for name, (r0, n) in PCOL_A.items():
                    if name == "log_dt":
                        act.dma_start(dt_raw[r0:r0 + n, :], io["s5_log_dt"][l].rearrange("(s g) -> s g", g=2))\
                            .then_inc(s_par, 16)
                        count[0] += 1
                        continue
                    a = io[src[name]][l]
                    if name in ("lam_re", "lam_im", "r_k"):
                        rows(r0, n, a.rearrange("(n h) c -> n (h c)", n=n))
                    elif name == "conv_w":
                        rows(r0, n, a.rearrange("j (t c) -> (j t) c", c=P))
                    else:
                        rows(r0, n, a.rearrange("(n c) -> n c", c=P))
                for name, (r0, n) in PCOL_B.items():
                    a = io[f"ln{int(name[2]) + 1}_{name[-1]}"][l]
                    rows(r0 - P, n, a.rearrange("(n c) -> n c", c=P), k=1)
                assert count[0] == N_PAR_DMA
                act.wait_ge(s_zero, 1)
                for par in range(2):
                    for g, name in enumerate(("lru_wa", "lru_wx")):
                        act.dma_start(view(wgate, 512 * g, NW, P)[C * par:C * par + C, :, C * par:C * par + C],
                                      io[name][l].rearrange("(t h) i j -> h i t j", h=2)[par]).then_inc(s_raw, 16)
                for g, name in enumerate(("s5_b_re", "s5_b_im")):
                    for h in range(2):
                        act.dma_start(b_raw[g][64 * h:64 * h + 64],
                                      io[name][l].rearrange("(s h) q c -> h q s c", h=2)[h]).then_inc(s_raw, 16)
                for g, name in enumerate(("s5_c_re", "s5_c_im")):
                    act.dma_start(c_raw[g], io[name][l].rearrange("(t g) c q -> (g c) t q", t=NW)).then_inc(s_raw, 16)
                act.dma_start(ups[0:C, 0:W], io["rw_w_up"][l]).then_inc(s_raw, 16)
                act.dma_start(ups[C:P, 0:W], io["rw_a_up"][l]).then_inc(s_raw, 16)
                act.dma_start(ups[:, W:2 * W], io["rw_g_up"][l]).then_inc(s_raw, 16)

                def prep1():
                    act.wait_ge(s_pcol, 1)
                    st.mark(f(dt_, pc("log_dt", 0, NS), ACT.Exp), s_p2)
                    act.wait_ge(s_p1, 1)
                    st.mark(f(u_, alam, ACT.Exp, scale=-1.0), s_p2)

                def prep2():
                    act.wait_ge(s_p1, 2)
                    st.mark(f(rho, xr, ACT.Exp), s_p2)
                    st.mark(f(th, xr, ACT.Tanh, scale=0.5), s_p2)

                def prep3():
                    act.wait_ge(s_p1, 3)
                    st.mark(f(s1, ang, ACT.Sin, scale=0.5), s_p2)
                    st.mark(f(c1, aab, ACT.Sin, scale=-0.5, bias=HALF_PI), s_p2)

                def prep_evac():
                    for b in range(4):
                        dst = view(bT if b < 2 else cT, 512 * (b % 2), 512)
                        act.wait_ge(s_bcT, b + 1)
                        ins = f(dst, banks[rota("bcT", 0, b)][:, :], ACT.Copy, scale=-1.0 if b == 3 else 1.0)
                        st.mark(ins, s_bce)

                steps = {2: [prep1, prep2, prep3], 4: [lambda: rotation(0)], 5: [lambda: rotation(1)],
                         6: [lambda: rotation(2)], 7: [lambda: rotation(3)], 8: [prep_evac]}
                for j in range(NF // 2):
                    if j in steps:
                        hi_to("g0", j)
                    for g in steps.get(j, ()):
                        g()
                    silu(0, j)
                    hidden_hi(0, j)
                def ln_weights(n):
                    if n:
                        act.wait_ge(s_xg, 2 * NT * n)
                    if n == 1:
                        act.wait_ge(s_yrw, 1)
                    for k, x in enumerate("gb"):
                        act.dma_start(lnbc[:, k, :], io[f"ln{n + 1}_{x}"][l].unsqueeze(0).to_broadcast([P, D]))\
                            .then_inc(s_lnw, 16)

                ln_weights(0)
                hi_to("z", ZORD[0])
                ln(0)

                dst = {0: zu[:, 0:2, :], 1: zu[:, 2:4, :], 2: lx[:, 0:2, 3:], 3: lx[:, 2:4, 3:],
                       4: ly[:, 0:2, :], 5: ly[:, 2:4, :]}
                dst.update({6 + k: zrw[:, 2 * k:2 * k + 2, 1:] for k in range(7)})
                act.wait_ge(s_bce, 4)
                act.wait_ge(s_rot, 16)
                for j in ZORD:
                    hi_to("z", j, ahead=1)
                    done_chunk(act, "z", j)
                    func = ACT.Gelu_apprx_tanh if j in (4, 5) else ACT.Copy
                    st.mark(f(dst[j], bank(rota("z", j), 2, T), func), s_z)
                hi_to("gate", 0)
                for t in range(NW):
                    act.wait_ge(s_y5d, t + 1)
                    st.mark(f(zu[:, t, :], zu[:, t, :], ACT.Gelu_apprx_tanh), s_ys5)
                def gate_evac(j):
                    done_chunk(act, "gate", j)
                    if j >= 4:
                        act.wait_ge(s_m, j - 3)
                    st.mark(f(gates[:, 2 * (j % 4):2 * (j % 4) + 2, :], bank(rota("gate", j), 2, T), ACT.Sigmoid),
                            s_gact)

                hi_to("gate", 1, 0)
                gate_evac(0)
                hi_to("gate", 1)
                for g in range(2):
                    act.wait_ge(s_lg, g + 1)
                    for t in range(NW):
                        st.mark(f(wk[2 + g][:, t, :], bank(4 + 2 * g + t // 2, 2, T)[:, t % 2, :], ACT.Sigmoid,
                                  bias=pc("bx" if g else "ba", t)), s_lga)
                    hi_to("gate", 2, g)
                act.wait_ge(s_shift, RWT)
                st.mark(f(wk[7][:, 1, :], zrw[:, 13, 1:], ACT.Sigmoid), s_lora_in)
                st.mark(f(wk[7][0:C, 0, :], zrw[0:C, 12, 1:], ACT.Tanh), s_lora_in)
                gate_evac(1)
                act.wait_ge(s_lga, 8)
                for t in range(NW):
                    f(wk[4][:, t, :], wk[2][:, t, :], ACT.Exp, scale=sp8n[:, t:t + 1])
                    st.mark(f(wk[5][:, t, :], wk[2][:, t, :], ACT.Tanh, scale=sp8[:, t:t + 1]), s_lga)
                hi_to("gate", 3)
                act.wait_ge(s_lq, 1)
                st.mark(f(wk[5], wk[5], ACT.Sqrt), s_lm)
                act.wait_ge(s_yl, NW)
                for g in range(2):
                    act.wait_ge(s_lora, g + 1)
                    for t in range(NW):
                        st.mark(f(wk[1 + g][:, t, :], bank(4 + 2 * g + t // 2, 2, T)[:, t % 2, :], ACT.Sigmoid,
                                  bias=pc("a0" if g else "w0", t)), s_lora_a)
                act.wait_ge(s_kk, 1)
                st.mark(f(wk[6], wk[4], ACT.Square), s_sq)
                gate_evac(2)
                act.wait_ge(s_lora, 3)
                for h in range(2):
                    st.mark(f(gRW[:, 2 * h:2 * h + 2, :], bank(4 + h, 2, T), ACT.Copy), s_lora_a)
                act.wait_ge(s_ss, 1)
                for h in range(2):
                    ins = f(wk[5][:, 2 * h:2 * h + 2, :], bank(6 + h, 2, T), ACT.Sqrt, bias=TINY)
                st.mark(ins, s_nrm)
                gate_evac(3)
                act.wait_ge(s_dec, 1)
                st.mark(f(wk[6], wk[3], ACT.Exp, scale=EDEC), s_exp)
                st.mark(f(wk[0], wk[1], ACT.Exp, scale=-EDEC), s_exp)
                act.wait_ge(s_ex, 1)
                st.mark(f(wk[0], wk[3], ACT.Exp, scale=-EDEC), s_exp)
                act.wait_ge(s_rk, 1)
                act.wait_ge(s_lora, 3)
                for t in range(NW):
                    st.mark(f(wk[7][:, t, :], wk[7][:, t, :], ACT.Copy, scale=pc("r_k", t)), s_rks)

                def glu_sigmoid(j):
                    done_chunk(act, "w2", j)
                    for b in range(2):
                        if j:
                            act.wait_ge(s_m, b + 1)
                        else:
                            act.wait_ge(s_bon, 1)
                        st.mark(f(mtmp[:, 2 * b:2 * b + 2, :], bank(rota("w2", j, b), 2, T), ACT.Sigmoid), s_glu)

                glu_sigmoid(0)
                act.wait_ge(s_tok, 1)
                act.wait_ge(s_back, NS)
                for b in range(2):
                    st.mark(f(BKtok[:, 4 * b:4 * b + 4, :], bank(4 + b, 4, P), ACT.Copy), s_toke)
                act.wait_ge(s_tok, 2)
                for b in range(2):
                    st.mark(f(SV[C:P, :, 2 * b:2 * b + 2, :], bank(4 + b, 4, 2, C)[C:P], ACT.Copy), s_toke)
                glu_sigmoid(1)
                hi_to("gate", 5, 0)
                gate_evac(4)

                def turned(dst, n):
                    act.wait_ge(s_T, n)
                    for b in range(2):
                        ins = f(dst[:, 4 * b:4 * b + 4, :], bank(4 + b, 4, P), ACT.Copy)
                    st.mark(ins, s_Ta)

                turned(M_bd, 1)
                turned(X_bd, 2)
                for i in range(5):
                    act.wait_ge(s_Y, i + 1)
                    for b in range(2):
                        ins = f(Ysb[:, 8 * b:8 * b + 8, :], bank(4 + b, 8, C), ACT.Copy)
                    st.mark(ins, s_Ye)
                    if i < 3:
                        hi_to("gate", 5 + i)
                    if i < 2:
                        hi_to("gate", 6 + i, 0)
                    if i < 3:
                        gate_evac(5 + i)
                    if i == 4:
                        hi_to("gate", 8)
                    turned(X_bd, i + 3)
                act.dma_start(memtok, io["mem"][0].rearrange("(t p) d -> p t d", p=P)).then_inc(s_memld, 16)
                for c in range(NC):
                    hi_to("gate", 8 + c)
                    act.wait_ge(s_Sa, c + 1)
                    st.mark(f(SV[0:C, c, :, :], bank(6, 8, C)[0:C], ACT.Copy), s_Sae)
                    hi_to("gate", 8 + c, ahead=1)
                    gate_evac(8 + c)
                    act.wait_ge(s_y, c + 1)
                    for par in range(2):
                        r = slice(C * par, C * par + C)
                        st.mark(f(yT[r, :, C * c:C * c + C], bank(4 + par, 2, NW, C)[r, 1], ACT.Copy), s_ye)
                hi_to("k", 0)
                for b in range(4):
                    act.wait_ge(s_memT, b + 1)
                    st.mark(f(memT[0][:, 2 * b:2 * b + 2, :], bank(rota("memT", 0, b), 2, M), ACT.Copy), s_memTe)

                def k_evac(j):
                    done_chunk(act, "k", j)
                    st.mark(f(kmT[:, 2 * j:2 * j + 2, :], bank(rota("k", j), 2, M), ACT.Copy), s_kv)

                def v_evac(j):
                    done_chunk(act, "v", j)
                    st.mark(f(vm[:, :, 256 * j:256 * j + 256], bank(rota("v", j), 2, 256), ACT.Copy), s_kv)

                def merged_hi(j):
                    act.wait_ge(s_m, 8 + j + 1)
                    st.mark(f(merged_r[0][:, 2 * j:2 * j + 2, :], merged[:, 2 * j:2 * j + 2, :], ACT.Copy), s_mh)

                act.wait_ge(s_yc, 1)
                st.mark(f(wk[1], wk[0], ACT.Square), s_ysq)
                hi_to("k", 0, ahead=1)
                act.wait_ge(s_var, 1)
                for h in range(2):
                    ins = f(wk[2][:, 2 * h:2 * h + 2, :], bank(6 + h, 2, T), ACT.Sqrt, bias=GNE, scale=1.0 / C)
                st.mark(ins, s_gnr)
                k_evac(0)
                for j in range(1, 4):
                    hi_to("k", j, ahead=1)
                    k_evac(j)
                hi_to("v", 0)
                v_evac(0)
                ln_weights(1)
                hi_to("v", 1, 0)
                merged_hi(0)
                merged_hi(1)
                hi_to("v", 1)
                merged_hi(2)
                merged_hi(3)
                hi_to("v", 1, ahead=1)
                v_evac(1)
                hi_to("v", 2, ahead=1)
                v_evac(2)
                hi_to("v", 3, ahead=1)
                v_evac(3)
                hi_to("q", 0)
                ln(1)
                def softmax_exp(h):
                    act.wait_ge(s_mx, h + 1)
                    for t in range(NT):
                        k = NT * h + t
                        ins = f(attn_p[:, h, t, :], banks[4 + h][:, t * M:(t + 1) * M], ACT.Exp, bias=nmax[:, k:k + 1],
                                scale=1.0 / 16.0, accum_out=rsum[:, k:k + 1])
                    st.mark(ins, s_ex2)

                def q_evac(j):
                    done_chunk(act, "q", j)
                    st.mark(f(qT[:, 2 * j:2 * j + 2, :], bank(rota("q", j), 2, T), ACT.Copy), s_q)

                def p_evac(h):
                    act.wait_ge(s_pT, h + 1)
                    st.mark(f(attn_pT[:, h, :, :], bank(4 + h, 2, T), ACT.Copy), s_pTe)

                def o_hi(h):
                    act.wait_ge(s_o, h + 1)
                    st.mark(f(oT[0][:, 2 * h:2 * h + 2, :], bank(4 + h, 2, T), ACT.Copy), s_oh)

                hi_to("q", 1, 0)
                q_evac(0)
                hi_to("q", 2, 0)
                q_evac(1)
                hi_to("q", 2)
                softmax_exp(0)
                hi_to("q", 3, 0)
                q_evac(2)
                hi_to("q", 3)
                softmax_exp(1)
                hi_to("wo", 0, 0)
                p_evac(0)
                q_evac(3)
                hi_to("wo", 0)
                softmax_exp(2)
                p_evac(1)
                o_hi(0)
                softmax_exp(3)
                p_evac(2)
                o_hi(1)
                p_evac(3)
                o_hi(2)
                o_hi(3)
                ln_weights(2)
                hi_to("g1", 0)
                ln(2)
                for j in range(NF // 2):
                    silu(1, j)
                    hidden_hi(1, j)
                ln_weights(3)
                hi_to("d1", NF // 2 - 1)
                ln(3)
                layer_end(act, "act")

        @block.vector
        def _(dve):
            st = Steps(dve, c_dve)
            v = nc.vector
            tt, ts, stt = v.tensor_tensor, v.tensor_scalar, v.scalar_tensor_tensor

            lo_at = [0]

            def lo_to(kind, j, m=1, ahead=0):
                while lo_at[0] <= split_index(kind, j, m, ahead):
                    i = lo_at[0]
                    if LO_AT[SPLITS[i]][0] == "dve":
                        dve.wait_ge(s_hi, i + 1)
                        st.mark(tt(split_flat(ring_lo, i), raw_flat(SPLITS[i]), split_flat(ring_hi, i), ALU.subtract),
                                s_lo["dve"])
                    lo_at[0] += 1

            def ln(n, kind, j, scale, after):
                if n:
                    dve.wait_ge(s_xg, 2 * NT * n)
                for t in range(NT):
                    if t == 0:
                        dve.wait_ge(s_acc0, n + 1)
                    else:
                        done_chunk(dve, kind, j)
                    for h in range(2):
                        x = xtok[:, t, 512 * h:512 * h + 512]
                        ins = stt(x, banks[4 + 2 * t + h][:, :], scale, x, ALU.mult, ALU.add)
                        if h == 1:
                            st.then(ins, s_lny)
                        else:
                            st.then(ins)
                    for h in range(2):
                        st.then(v.bn_stats(stats[t][:, 6 * h:6 * h + 6], xtok[:, t, 512 * h:512 * h + 512]))
                    st.then(v.bn_aggr(mv[t], stats[t]))
                    st.mark(ts(vare[t], mv[t][:, 1:2], LNE, None, ALU.add), s_lnv)
                    if t < len(after):
                        lo_to(*after[t])
                for t in range(NT):
                    dve.wait_ge(s_lnr, NT * n + t + 1)
                    st.mark(ts(xtok[:, t, :], xtok[:, t, :], mv[t][:, 0:1], rstd[t], ALU.subtract, ALU.mult), s_lnx)
                for piece in after[NT:]:
                    lo_to(*piece)
                dve.wait_ge(s_lnT, NT * n + NT)
                for b in range(2, 4):
                    src, sl = bank(rota("lnT", n, b), 2, T), slice(2 * b, 2 * b + 2)
                    for m in range(2):
                        d = 2 * b + m
                        ins = ts(xf[:, d, :], src[:, m, :], pc(f"ln{n}_g", d), pc(f"ln{n}_b", d), ALU.mult, ALU.add)
                    st.then(ins)
                    st.then(v.tensor_copy(xT[0][:, sl, :], xf[:, sl, :]))
                    st.mark(tt(xT[1][:, sl, :], xf[:, sl, :], xT[0][:, sl, :], ALU.subtract), s_xTd)

            def hidden(i, j):
                lo_to(f"u{i}", j, 1, 1)
                dve.wait_ge(s_silu, i * (NF // 2) + j + 1)
                if i * (NF // 2) + j >= 2:
                    dve.wait_ge(s_hl, i * (NF // 2) + j - 1)
                done_chunk(dve, f"u{i}", j)
                st.mark(tt(htmp[j % 2], sil[j % 2], banks[rota(f"u{i}", j)][:, :], ALU.mult), s_h)

            dve.wait_ge(s_preT, 1)
            for b in range(2, 4):
                ins = v.tensor_copy(xf[:, 2 * b:2 * b + 2, :], bank(b, 2, T))
            ins.then_inc(s_preD, 1)
            dve.wait_ge(s_preD, 1)
            v.tensor_copy(xT[0][:, 4:8, :], xf[:, 4:8, :]).then_inc(s_preD, 1)
            dve.wait_ge(s_preD, 2)
            tt(xT[1][:, 4:8, :], xf[:, 4:8, :], xT[0][:, 4:8, :], ALU.subtract).then_inc(s_preX, 1)

            def prep():
                dve.wait_ge(s_rowsT, 1)
                o = banks[rota("rowsT", 0)]
                v.tensor_copy(pcol[:, 0:NA], o[:, 0:NA])
                st.then(v.tensor_copy(pcol[:, P:NB], o[:, P:NB]), s_pcol)
                lre, lim, lam = pc("lam_re", 0, NS), pc("lam_im", 0, NS), pc("lam", 0, NW)
                st.then(stt(alam, lam, -1.0, lam, ALU.mult, ALU.max), s_p1)
                dve.wait_ge(s_p2, 1)
                st.then(tt(ang, lim, dt_, ALU.mult))
                st.then(tt(xr, lre, dt_, ALU.mult), s_p1)
                st.then(ts(rnd, ang, 1.0 / TWO_PI, MAGIC, ALU.mult, ALU.add))
                st.then(ts(rnd, rnd, MAGIC, None, ALU.subtract))
                for part in (PI_A, PI_B, PI_C):
                    st.then(stt(ang, rnd, -part, ang, ALU.mult, ALU.add))
                st.then(stt(aab, ang, -1.0, ang, ALU.mult, ALU.max), s_p1)
                st.then(ts(phi, ang, 1.0 / TWO_PI, None, ALU.mult))
                lo_to("g0", 2)
                dve.wait_ge(s_p2, 2)
                st.then(ts(w_, u_, 2.0, None, ALU.add))
                st.then(v.reciprocal(w_, w_))
                st.then(tt(w_, w_, u_, ALU.mult))
                st.then(tt(w2_, w_, w_, ALU.mult))
                st.then(ts(pl, w2_, 1.0 / 19.0, None, ALU.mult))
                for k in range(17, 1, -2):
                    st.then(stt(pl, pl, 1.0 / k, w2_, ALU.add, ALU.mult))
                st.then(stt(pl, pl, 1.0, w_, ALU.add, ALU.mult))
                lo_to("u0", 2, 0)
                st.then(ts(u_, lam, -1.0, 0.0, ALU.mult, ALU.max))
                st.then(stt(pl, pl, 2.0, u_, ALU.mult, ALU.add))
                v.tensor_scalar(sp8, pl, 8.0, None, ALU.mult)
                v.tensor_scalar(sp8n, pl, -8.0, None, ALU.mult)
                st.then(ts(omka, pc("k_a", 0, NW), -1.0, 1.0, ALU.mult, ALU.add))
                dve.wait_ge(s_p2, 6)
                st.then(stt(em, rho, 1.0, th, ALU.add, ALU.mult))
                st.then(tt(t1, s1, s1, ALU.mult))
                st.then(ts(t2, t1, -2.0, 1.0, ALU.mult, ALU.add))
                st.then(tt(t2, em, t2, ALU.mult))
                st.then(stt(nre, t1, -2.0, t2, ALU.mult, ALU.add))
                st.then(stt(t1, s1, 2.0, c1, ALU.mult, ALU.mult))
                st.then(tt(nim, rho, t1, ALU.mult))
                st.then(tt(t1, lre, lre, ALU.mult))
                st.then(tt(t2, lim, lim, ALU.mult))
                st.then(tt(den, t1, t2, ALU.add))
                lo_to("u0", 2)
                st.then(v.reciprocal(den, den))
                st.then(tt(t1, nre, lre, ALU.mult))
                st.then(tt(t2, nim, lim, ALU.mult))
                st.then(tt(t1, t1, t2, ALU.add))
                st.then(tt(fr, t1, den, ALU.mult))
                st.then(tt(t1, nim, lre, ALU.mult))
                st.then(tt(t2, nre, lim, ALU.mult))
                st.then(tt(t1, t1, t2, ALU.subtract))
                st.then(tt(fi, t1, den, ALU.mult), s_p1)

            def rotation(q):
                sl = slice(4 * q, 4 * q + 4)
                time = const("time").unsqueeze(1).to_broadcast([P, 4, T])
                turns = phi[:, sl].unsqueeze(2).to_broadcast([P, 4, T])
                st.then(tt(rot[0], time, turns, ALU.mult))
                st.then(ts(rot[1], rot[0], MAGIC, None, ALU.add))
                lo_to("g0", q + 4)
                st.then(ts(rot[1], rot[1], MAGIC, None, ALU.subtract))
                st.then(tt(rot[0], rot[0], rot[1], ALU.subtract), s_rot)
                st.then(stt(rot[1], rot[0], -1.0, rot[0], ALU.mult, ALU.max), s_rot)
                lo_to("u0", q + 4, 0)
                dve.wait_ge(s_rots, 2 * q + 2)
                st.then(stt(rot[2], sinT[:, sl, :], -2.0, sinT[:, sl, :], ALU.mult, ALU.mult))
                st.then(stt(sinT[:, sl, :], sinT[:, sl, :], 2.0, cosT[:, sl, :], ALU.mult, ALU.mult), s_rot)
                st.then(ts(cosT[:, sl, :], rot[2], 1.0, None, ALU.add), s_rot)

            with dve.Fori(0, L) as l:
                st.n.clear()
                for j in range(NF // 2):
                    lo_to("g0", j, 0)
                    if j == 2:
                        prep()
                    if j in (4, 5, 6, 7):
                        rotation(j - 4)
                    hidden(0, j)
                lo_to("z", ZORD[0], 0)
                ln(0, "d0", NF // 2 - 1, 0.5 / ALPHA, [("z", ZORD[0], 0), ("z", ZORD[0])])

                def s5_forward(s):
                    dve.wait_ge(s_bu, s + 1)
                    src = bank(4 + s % 2, 2, T)
                    cs = cosT[:, s:s + 1, :].to_broadcast([P, 2, T])
                    sn = sinT[:, s:s + 1, :].to_broadcast([P, 2, T])
                    tt(s5m[:, 0, :, :], src, cs, ALU.mult)
                    st.then(tt(s5m[:, 1, :, :], src, sn, ALU.mult), s_fwd)
                    tt(s5v[:, 0, :], s5m[:, 0, 0, :], s5m[:, 1, 1, :], ALU.add)
                    st.then(tt(s5v[:, 1, :], s5m[:, 0, 1, :], s5m[:, 1, 0, :], ALU.subtract))
                    if s >= 2:
                        dve.wait_ge(s_back, s - 1)
                    for i in range(2):
                        ins = v.tensor_tensor_scan(s5z[s % 2][:, i, :], rho[:, s:s + 1].to_broadcast([P, T]),
                                                   s5v[:, i, :], 0.0, ALU.mult, ALU.add)
                    st.then(ins, s_scan)

                def s5_skip(t):
                    dve.wait_ge(s_y5, 4 * t + 4)
                    st.then(stt(zu[:, t, :], zu[:, t, :], pc("s5_d", t), banks[6 + t % 2][:, 0:T], ALU.mult, ALU.add),
                            s_y5d)

                dve.wait_ge(s_xg, 2 * NT)
                lo_to("z", ZORD[1])
                for s in range(NS):
                    lo_to("z", ZORD[2 + s // 2], s % 2)
                    s5_forward(s)
                    if s >= 6 and s % 4 == 2:
                        s5_skip((s - 6) // 4)

                def shift(a, n):
                    before = wk[6][:, 0:n, :]
                    st.then(tt(before, zrw[:, a:a + n, 0:T], zrw[:, a:a + n, 1:T + 1], ALU.subtract))
                    for t in range(n):
                        ins = stt(zrw[:, a + t, 1:T + 1], before[:, t, :], pc("mu", a + t), zrw[:, a + t, 1:T + 1],
                                  ALU.mult, ALU.add)
                        st.then(ins, s_shift)

                xc = wk[1]

                def convolve(t):
                    st.then(ts(xc[:, t, :], lx[:, t, 0:T], pc("conv_w", t), pc("conv_b", t), ALU.mult, ALU.add))
                    for k in range(1, 4):
                        ins = stt(xc[:, t, :], lx[:, t, k:k + T], pc("conv_w", 4 * k + t), xc[:, t, :], ALU.mult, ALU.add)
                        if k == 3:
                            st.then(ins, s_conv)
                        else:
                            st.then(ins)

                dve.wait_ge(s_z, 9)
                dve.wait_ge(s_zz, 2)
                lo_to("z", ZORD[10], 0)
                shift(12, 2)
                lo_to("z", ZORD[10])
                shift(4, 4)
                lo_to("z", ZORD[11], 0)
                dve.wait_ge(s_z, 11)
                convolve(0)
                lo_to("z", ZORD[11])
                convolve(1)
                convolve(2)
                lo_to("z", ZORD[12], 0)
                convolve(3)
                lo_to("z", ZORD[12])
                s5_skip(NW - 1)
                shift(0, 4)
                shift(8, 4)
                dve.wait_ge(s_lga, 12)
                a_, th_, gi_, h_ = wk[4], wk[5], wk[3], wk[6]
                st.then(tt(h_, a_, a_, ALU.mult))
                st.then(stt(th_, h_, 1.0, th_, ALU.add, ALU.mult), s_lq)
                st.then(tt(gi_, gi_, xc, ALU.mult))
                dve.wait_ge(s_lm, 1)
                st.then(tt(gi_, gi_, th_, ALU.mult))
                for t in range(NW):
                    st.then(v.tensor_tensor_scan(h_[:, t, :], a_[:, t, :], gi_[:, t, :], 0.0, ALU.mult, ALU.add))
                    st.then(tt(ly[:, t, :], h_[:, t, :], ly[:, t, :], ALU.mult), s_yl)

                r_, k_, v_ = (zrw[:, a:a + 4, 1:T + 1] for a in (0, 4, 8))
                sw, ra, dec, kk, rn, rk = wk[1], wk[2], wk[3], wk[4], wk[5], wk[7]
                for t in range(NW):
                    ins = ts(kk[:, t, :], k_[:, t, :], pc("k_k", t), None, ALU.mult)
                st.then(ins, s_kk)
                dve.wait_ge(s_lora_a, 4)
                for t in range(NW):
                    ins = v.tensor_tensor_scan(dec[:, t, :], const("reset"), sw[:, t, :], 0.0, ALU.mult, ALU.add)
                st.then(ins)
                st.then(tt(sw, dec, sw, ALU.subtract), s_dec)
                dve.wait_ge(s_lora_a, 8)
                dve.wait_ge(s_lora, 3)
                for t in range(NW):
                    ins = ts(rk[:, t, :], ra[:, t, :], pc("k_a", t), omka[:, t:t + 1], ALU.mult, ALU.add)
                st.then(ins)
                st.then(tt(k_, k_, rk, ALU.mult))
                st.then(tt(rk, r_, k_, ALU.mult), s_rk)
                dve.wait_ge(s_nrm, 1)
                st.then(v.reciprocal(rn, rn))
                st.then(tt(kk, kk, rn, ALU.mult))
                st.then(stt(ra, kk, -1.0, ra, ALU.mult, ALU.mult))
                def split(x):
                    return x.rearrange("p t (c s) -> p t c s", c=NC)

                dve.wait_ge(s_exp, 1)
                dve.wait_ge(s_y5d, NW)
                eN = wk[6]
                for t in range(NW):
                    tt(BK[:, t, :, 0, :], ra[:, t, :].rearrange("p (c s) -> p c s", c=NC),
                       eN[:, t, :].rearrange("p (c s) -> p c s", c=NC), ALU.mult)
                    tt(BK[:, t, :, 1, :], k_[:, t, :].rearrange("p (c s) -> p c s", c=NC),
                       eN[:, t, :].rearrange("p (c s) -> p c s", c=NC), ALU.mult)
                dve.wait_ge(s_exp, 2)
                for t in range(NW):
                    ins = tt(AR[:, t, :, 0, :], kk[:, t, :].rearrange("p (c s) -> p c s", c=NC),
                             wk[0][:, t, :].rearrange("p (c s) -> p c s", c=NC), ALU.mult)
                st.then(ins, s_ex)
                dve.wait_ge(s_exp, 3)
                for t in range(NW):
                    ins = tt(AR[:, t, :, 1, :], r_[:, t, :].rearrange("p (c s) -> p c s", c=NC),
                             wk[0][:, t, :].rearrange("p (c s) -> p c s", c=NC), ALU.mult)
                st.then(v.tensor_copy(pC, split(wk[0])[:, :, :, C - 1]), s_ops)
                dve.wait_ge(s_bon, 1)
                for h in range(2):
                    ins = tt(bonus[:, 2 * h:2 * h + 2, :], bank(4 + h, 2, T), v_[:, 2 * h:2 * h + 2, :], ALU.mult)
                st.then(ins, s_bonr)

                def merge(k):
                    j, b = (k % 4) // 2, k % 2
                    sl = slice(2 * (k % 4), 2 * (k % 4) + 2)
                    tmp = mtmp[:, 2 * b:2 * b + 2, :]
                    if k < 4:
                        dve.wait_ge(s_gact, k + 1)
                        dve.wait_ge(s_glu, k + 1)
                        done_chunk(dve, "w1", j)
                        st.then(tt(tmp, tmp, bank(rota("w1", j, b), 2, T), ALU.mult))
                        st.then(tt(merged[:, sl, :], tmp, gates[:, sl, :], ALU.mult), s_m)
                        return
                    kind = "lru" if k < 8 else "rw"
                    dve.wait_ge(s_gact, k + 1)
                    done_chunk(dve, kind, j)
                    st.then(tt(tmp, gates[:, sl, :], bank(rota(kind, j, b), 2, T), ALU.mult))
                    st.then(tt(merged[:, sl, :], merged[:, sl, :], tmp, ALU.add), s_m)

                dve.wait_ge(s_tok, 1)
                dve.wait_ge(s_back, NS)
                for b in range(2, 4):
                    st.mark(v.tensor_copy(BKtok[:, 4 * b:4 * b + 4, :], bank(4 + b, 4, P)), s_tokv)
                dve.wait_ge(s_tok, 2)
                for b in range(2, 4):
                    st.mark(v.tensor_copy(SV[C:P, :, 2 * b:2 * b + 2, :], bank(4 + b, 4, 2, C)[C:P]), s_tokv)
                merge(0)
                merge(1)
                G4 = G.rearrange("p (q h) s -> p q h s", h=2)
                for g in range(4):
                    dve.wait_ge(s_G, g + 1)
                    for par in range(2):
                        st.mark(tt(G4[:, 4 * g:4 * g + 4, par, :], bank(4 + 2 * (g % 2) + par, 4, P),
                                   const("maskG").unsqueeze(1).to_broadcast([P, 4, P]), ALU.mult), s_Ge)
                merge(2)
                merge(3)
                dve.wait_ge(s_N, 1)
                dve.wait_ge(s_p3, 5)
                for par in range(2):
                    r = slice(C * par, C * par + C)
                    for hf in range(2):
                        src = bank(4 + 2 * par + hf, 8, C)[r]
                        for name, dst in (("strict", W_bd[r, 8 * hf:8 * hf + 8, C * par:C * par + C]),
                                          ("off1", Wst[r, 8 * hf:8 * hf + 8, :])):
                            m = const(name)[r].unsqueeze(1).to_broadcast([C, 8, C])
                            ins = tt(dst, src, m, ALU.mult)
                            st.mark(ins, s_Nb)
                dve.wait_ge(s_Nb, 8)
                st.then(tt(Wst, Wst, const("eye2").unsqueeze(1).to_broadcast([P, NQ, C]), ALU.add), s_tmp)
                dve.wait_ge(s_T, 1)
                st.mark(v.tensor_copy(W_bd[0:C, :, 0:C], Wst[0:C]), s_Wb)

                def turned(dst, n):
                    dve.wait_ge(s_T, n)
                    for b in range(2, 4):
                        ins = v.tensor_copy(dst[:, 4 * b:4 * b + 4, :], bank(4 + b, 4, P))
                    st.then(ins, s_Td)

                turned(M_bd, 1)
                turned(X_bd, 2)
                for i in range(5):
                    dve.wait_ge(s_WY, i + 1)
                    for b in range(2):
                        m = const(f"off{2 << i}").unsqueeze(1).to_broadcast([P, 8, C])
                        ins = tt(tmpB[:, 8 * b:8 * b + 8, :], bank(6 + b, 8, C), m, ALU.mult)
                    st.then(ins, s_tmp)
                    st.then(tt(W_bd[0:C, :, 0:C], Wst[0:C], tmpB[0:C], ALU.add), s_Wb)
                    dve.wait_ge(s_Wp, i + 2)
                    st.then(tt(Wst, Wst, tmpB, ALU.add))
                    turned(X_bd, i + 3)
                    if i == 4:
                        for k in range(4, 8):
                            merge(k)
                for c in range(NC):
                    dve.wait_ge(s_U, c + 1)
                    for par in range(2):
                        r = slice(C * par, C * par + C)
                        st.mark(v.tensor_copy(Usb[r], bank(4 + par, 2, NW, C)[r, 0]), s_Ue)
                    if c < NC - 1:
                        dve.wait_ge(s_Sn, c + 1)
                        pcb = pC[:, :, c:c + 1].to_broadcast([P, NW, C])
                        src, new = bank(7, 2, NW, C)[:, 0], S0[(c + 1) % 2]
                        if c:
                            st.then(tt(new, src, S0[c % 2], ALU.add))
                            st.then(tt(new, new, pcb, ALU.mult), s_S)
                        else:
                            st.then(tt(new, src, pcb, ALU.mult), s_S)
                lo_to("k", 0)
                dve.wait_ge(s_mean, 1)
                yc, sd = wk[0], wk[2]
                for h in range(2):
                    ins = stt(yc[:, 2 * h:2 * h + 2, :], bank(4 + h, 2, T), -1.0 / C, yT[:, 2 * h:2 * h + 2, :],
                              ALU.mult, ALU.add)
                st.then(ins, s_yc)
                for b in range(4):
                    dve.wait_ge(s_memTe, b + 1)
                    sl = slice(2 * b, 2 * b + 2)
                    st.mark(tt(memT[1][:, sl, :], bank(rota("memT", 0, b), 2, M), memT[0][:, sl, :], ALU.subtract),
                            s_memTl)
                lo_to("k", 0, 1, 1)
                dve.wait_ge(s_gnr, 1)
                for h in range(2):
                    st.then(v.reciprocal(sd[:, 2 * h:2 * h + 2, :], sd[:, 2 * h:2 * h + 2, :]))
                    lo_to("k", 1, 1, h)
                st.then(tt(yc, yc, sd, ALU.mult))
                for t in range(NW):
                    ins = ts(yc[:, t, :], yc[:, t, :], pc("gn_g", t), pc("gn_b", t), ALU.mult, ALU.add)
                st.then(ins)
                lo_to("k", 2)
                st.then(tt(yc, yc, bonus, ALU.add))
                st.then(tt(yc, yc, gRW, ALU.mult), s_yrw)

                def merged_lo(j):
                    dve.wait_ge(s_mh, j + 1)
                    sl = slice(2 * j, 2 * j + 2)
                    st.mark(tt(merged_r[1][:, sl, :], merged[:, sl, :], merged_r[0][:, sl, :], ALU.subtract), s_ml)

                lo_to("v", 1, 0)
                for j in range(2):
                    merge(8 + 2 * j)
                    merge(9 + 2 * j)
                    merged_lo(2 * j)
                    merged_lo(2 * j + 1)
                    lo_to("v", 1, 1, j)
                lo_to("v", 2, 0)
                ln(1, "mix", 3, 1.0 / ALPHA, [("v", 2), ("v", 3, 0), ("v", 3), ("q", 0)])

                def score_max(h):
                    dve.wait_ge(s_sc, h + 1)
                    k = slice(NT * h, NT * h + NT)
                    st.then(v.tensor_reduce(nmax[:, k], bank(4 + h, NT, M), AX.X, ALU.max))
                    st.then(ts(nmax[:, k], nmax[:, k], -1.0 / 16.0, None, ALU.mult), s_mx)

                def normalise(h):
                    dve.wait_ge(s_ex2, h + 1)
                    k = slice(NT * h, NT * h + NT)
                    st.then(v.reciprocal(rinv[:, k], rsum[:, k]))
                    for t in range(NT):
                        ins = ts(attn_p[:, h, t, :], attn_p[:, h, t, :], rinv[:, NT * h + t:NT * h + t + 1], None,
                                 ALU.mult)
                    st.then(ins, s_pn)

                def o_evac(h):
                    dve.wait_ge(s_o, h + 1)
                    dve.wait_ge(s_oh, h + 1)
                    sl = slice(2 * h, 2 * h + 2)
                    st.mark(tt(oT[1][:, sl, :], bank(4 + h, 2, T), oT[0][:, sl, :], ALU.subtract), s_oe)

                lo_to("q", 2, 0)
                score_max(0)
                lo_to("q", 3, 0)
                score_max(1)
                lo_to("q", 3)
                normalise(0)
                lo_to("wo", 0, 0)
                score_max(2)
                normalise(1)
                lo_to("wo", 0)
                o_evac(0)
                score_max(3)
                normalise(2)
                o_evac(1)
                normalise(3)
                o_evac(2)
                o_evac(3)
                lo_to("g1", 0, 0)
                ln(2, "wo", 3, 1.0 / ALPHA, [("g1", 0, 0), ("g1", 0)])
                for j in range(NF // 2):
                    hidden(1, j)
                lo_to("d1", NF // 2 - 1)
                ln(3, "d1", NF // 2 - 1, 0.5 / ALPHA, [])
                layer_end(dve, "dve")

        @block.gpsimd
        def _(pool):
            st = Steps(pool, c_pool)
            g = nc.gpsimd
            tt = g.tensor_tensor
            g.memset(wgate[:, :], 0.0).then_inc(s_zero, 1)

            def ln(n):
                for t in range(NT):
                    pool.wait_ge(s_lnv, NT * n + t + 1)
                    st.mark(tt(rstd[t], vare[t], NEG_HALF, ALU.pow), s_lnr)
                pool.wait_ge(s_lnw, 32 * (n + 1))
                for b in range(2):
                    pool.wait_ge(s_xTa, 2 * n + b + 1)
                    sl = slice(2 * b, 2 * b + 2)
                    st.mark(tt(xT[1][:, sl, :], xf[:, sl, :], xT[0][:, sl, :], ALU.subtract), s_xTp)
                for t in range(NT):
                    pool.wait_ge(s_lnT, NT * n + t + 1)
                    st.then(tt(xtok[:, t, :], xtok[:, t, :], lnbc[:, 0, :], ALU.mult), s_xg)
                    st.then(tt(xtok[:, t, :], xtok[:, t, :], lnbc[:, 1, :], ALU.add), s_xg)

            def gate_lo(j, m):
                n = INDEX[("gate", j, m)]
                i = SPLIT_AT[n]
                pool.wait_ge(s_hi, i + 1)
                st.then(tt(split_flat(ring_lo, i), raw_flat(n), split_flat(ring_hi, i), ALU.subtract), s_lo["pool"])

            def hidden_lo(i, j):
                pool.wait_ge(s_hh, i * (NF // 2) + j + 1)
                hi, lo = (x[:, 2 * j:2 * j + 2, :].rearrange("p a t -> p (a t)") for x in hT)
                st.mark(tt(lo, htmp[j % 2], hi, ALU.subtract), s_hl)

            pool.wait_ge(s_preA, 2)
            tt(xT[1][:, 0:4, :], xf[:, 0:4, :], xT[0][:, 0:4, :], ALU.subtract).then_inc(s_preX, 1)
            pool.wait_ge(s_preX, 2)

            with pool.Fori(0, L) as l:
                st.n.clear()
                pool.wait_ge(s_zero, 1)
                pool.wait_ge(s_par, 16 * N_PAR_DMA)
                r0 = PCOL_A["log_dt"][0]
                g.tensor_copy(prow[r0:r0 + NS, 0, :].rearrange("s (g q) -> s g q", g=2),
                              dt_raw[r0:r0 + NS, :].unsqueeze(2).to_broadcast([NS, 2, 64])).then_inc(s_dtx, 1)
                pool.wait_ge(s_dtx, 1)
                for j in range(2):
                    hidden_lo(0, j)
                pool.wait_ge(s_raw, 16 * 13)
                pool.wait_ge(s_p1, 4)
                half_s, half_c = const("half_state"), const("half_chan")
                frb, fib = (x.unsqueeze(2).to_broadcast([P, NS, 16]) for x in (fr, fi))
                for i in range(2):
                    a, b = (frb, fib) if i == 0 else (fib, frb)
                    st.then(tt(bt_tmp[0], b_raw[0], a, ALU.mult))
                    st.then(tt(bt_tmp[1], b_raw[1], b, ALU.mult))
                    st.then(tt(bt_tmp[0], bt_tmp[0], bt_tmp[1], ALU.subtract if i == 0 else ALU.add))
                    for h in range(2):
                        dst = b_bd[i].rearrange("p t (s h c) -> p (t s) h c", s=4, h=2)[:, :, h, :]
                        ins = tt(dst, bt_tmp[0], half_s[:, h:h + 1].unsqueeze(2).to_broadcast([P, NS, 16]), ALU.mult)
                    st.then(ins, s_p3)
                    hidden_lo(0, 2 + i)
                for i in range(2):
                    for h in range(2):
                        ins = tt(c_bd[i][:, :, 64 * h:64 * h + 64], c_raw[i],
                                 half_c[:, h:h + 1].unsqueeze(2).to_broadcast([P, NW, C]), ALU.mult)
                    st.then(ins, s_p3)
                    hidden_lo(0, 4 + i)
                for j in range(6, NF // 2):
                    hidden_lo(0, j)
                ln(0)
                pool.wait_ge(s_bce, 4)
                pool.wait_ge(s_rot, 16)
                st.then(g.memset(zrw[:, :, 0:1], 0.0), s_zz)
                st.then(g.memset(lx[:, :, 0:3], 0.0), s_zz)
                for s in range(NS):
                    pool.wait_ge(s_scan, s + 1)
                    z = s5z[s % 2]
                    cs = cosT[:, s:s + 1, :].to_broadcast([P, 2, T])
                    sn = sinT[:, s:s + 1, :].to_broadcast([P, 2, T])
                    tt(s5n[:, 0, :, :], z, cs, ALU.mult)
                    st.then(tt(s5n[:, 1, :, :], z, sn, ALU.mult))
                    if s >= 2:
                        pool.wait_ge(s_y5, s - 1)
                    tt(s5s[s % 2][:, 0, :], s5n[:, 0, 0, :], s5n[:, 1, 1, :], ALU.subtract)
                    st.then(tt(s5s[s % 2][:, 1, :], s5n[:, 0, 1, :], s5n[:, 1, 0, :], ALU.add), s_back)
                for j in range(4):
                    for m in range(2):
                        gate_lo(j, m)
                pool.wait_ge(s_ops, 1)
                st.then(g.memset(W_bd[0:C, :, C:P], 0.0))
                st.then(g.memset(W_bd[C:P, :, 0:C], 0.0), s_p3)
                gate_lo(4, 0)
                gate_lo(4, 1)
                for i in range(6):
                    if i == 5:
                        gate_lo(8, 0)
                    pool.wait_ge(s_tmp, i + 1)
                    r = slice(C, P)
                    if i == 0:
                        pool.wait_ge(s_T, 1)
                        st.then(g.tensor_copy(W_bd[r, :, C:P], Wst[r]), s_Wp)
                    else:
                        st.then(tt(W_bd[r, :, C:P], Wst[r], tmpB[r], ALU.add), s_Wp)
                    if i < 3:
                        gate_lo(5 + i, 0)
                        gate_lo(5 + i, 1)
                gate_lo(8, 1)
                for j in range(9, 12):
                    gate_lo(j, 0)
                    gate_lo(j, 1)
                ln(1)
                ln(2)
                for j in range(NF // 2):
                    hidden_lo(1, j)
                ln(3)
                layer_end(pool, "pool")


N_PAR_DMA = len(ROWS_A) + len(ROWS_B)
_INS = ['x', 'mem', 'ffn1_wg', 'ffn1_wu', 'ffn1_wd', 'ln1_g', 'ln1_b', 'w_in', 's5_lam_re', 's5_lam_im', 's5_log_dt',
        's5_b_re', 's5_b_im', 's5_c_re', 's5_c_im', 's5_d', 's5_glu_w1', 's5_glu_w2', 'lru_conv_w', 'lru_conv_b',
        'lru_wa', 'lru_ba', 'lru_wx', 'lru_bx', 'lru_lambda', 'lru_w_out', 'rw_mu', 'rw_w0', 'rw_w_up', 'rw_a0',
        'rw_a_up', 'rw_g_up', 'rw_k_k', 'rw_k_a', 'rw_r_k', 'rw_ln_g', 'rw_ln_b', 'rw_w_out', 'mix_w_out', 'ln2_g',
        'ln2_b', 'xa_wq', 'xa_wkv', 'xa_wo', 'ln3_g', 'ln3_b', 'ffn2_wg', 'ffn2_wu', 'ffn2_wd', 'ln4_g', 'ln4_b']


def kernel(**inputs):
    import concourse.bacc as _bacc
    from concourse.bass_utils import run_bass_kernel_spmd as _run

    nc = _bacc.Bacc("TRN2", target_bir_lowering=False, num_devices=1)
    arrays, io = {}, {}
    for name in _INS:
        a = np.ascontiguousarray(inputs[name])
        arrays[f"in_{name}_dram"] = a
        io[name] = nc.dram_tensor(f"in_{name}_dram", a.shape, mybir.dt.from_np(a.dtype), kind="ExternalInput").ap()
    c = constants()
    arrays["constants_dram"] = c
    consts = nc.dram_tensor("constants_dram", c.shape, F32, kind="ExternalInput").ap()
    out = nc.dram_tensor("out_0_dram", (1, T, D), F32, kind="ExternalOutput").ap()
    trunk(nc, io, consts, out)
    r = _run(nc, [arrays], core_ids=[0])
    return r.results[0]["out_0_dram"]
```

```python
from contextlib import ExitStack

import concourse.bass as bass
import numpy as np
from concourse import mybir

ALU = mybir.AluOpType
ACT = mybir.ActivationFunctionType
AX = mybir.AxisListType
F32 = mybir.dt.float32
F32R = mybir.dt.float32r

P = 128
D = 1024
T = 256
M = 256
L = 2
F = 2816
W = 512
NF = F // P
ND = D // P
NW = W // P
NT = T // P
NS = 16
C = 64
NC = T // C
NQ = NW * NC
XH = 4
RW0 = 3 * W
RWT = 14
GATE0 = RW0 + RWT * P
ALPHA = (2 * L) ** 0.25
LN_EPS = 1e-5
GN_EPS = 64e-5
RAW = 3
SPLIT = 2
PIECE = 1024
EDEC = float(np.exp(-0.5))
MAGIC = 1.5 * 2.0 ** 23
TWO_PI = 2.0 * np.pi
PI_A = 6.28125
PI_B = float(np.float32(TWO_PI - PI_A).view(np.uint32) & np.uint32(0xFFFFF000)) and float(
    np.array([np.float32(TWO_PI - PI_A).view(np.uint32) & np.uint32(0xFFFFF000)], np.uint32).view(np.float32)[0])
PI_C = float(TWO_PI - PI_A - PI_B)

ROWS_A = [("lam_re", NS), ("lam_im", NS), ("log_dt", NS), ("s5_d", NW), ("conv_w", 4 * NW), ("conv_b", NW),
          ("ba", NW), ("bx", NW), ("lam", NW), ("mu", RWT), ("w0", NW), ("a0", NW), ("k_k", NW), ("k_a", NW),
          ("r_k", NW), ("gn_g", NW), ("gn_b", NW)]
ROWS_B = [(f"ln{n}_{x}", ND) for n in range(4) for x in "gb"]

CONST = [("ident", P), ("heads", P), ("maskG", P), ("strict", C)] + \
        [(f"off{b}", C) for b in (1, 2, 4, 8, 16, 32)] + \
        [("eye2", C), ("time", T), ("reset", T), ("half_state", 2), ("half_chan", 2), ("cols", 8)]


def columns(rows, start=0):
    at, where = start, {}
    for name, n in rows:
        where[name] = (at, n)
        at += n
    return where, at


CCOL, NCONST = columns(CONST)
PCOL_A, NA = columns(ROWS_A)
PCOL_B, NB = columns(ROWS_B, P)


def constants():
    c = np.zeros((P, NCONST), np.float32)

    def put(name, value):
        a, n = CCOL[name]
        c[:, a:a + n] = value

    p, j = np.arange(P)[:, None], np.arange(P)[None, :]
    i, jc = p % C, np.arange(C)[None, :]
    put("ident", p == j)
    put("heads", p // C == j // C)
    s, t, is_k, is_r = p % C, j % C, p >= C, j >= C
    put("maskG", np.where(is_r, s <= t, is_k & (s < t)))
    put("strict", jc < i)
    for b in (1, 2, 4, 8, 16, 32):
        put(f"off{b}", (i // (2 * b) == jc // (2 * b)) & (i % (2 * b) >= b) & (jc % (2 * b) < b))
    put("eye2", i == jc)
    put("time", np.arange(T)[None, :])
    put("reset", np.arange(T)[None, :] % C != 0)
    put("half_state", p // C == np.arange(2)[None, :])
    put("half_chan", (p // 16) % 2 == np.arange(2)[None, :])
    put("cols", np.array([np.pi / 2, 1e-12, GN_EPS, -0.5, LN_EPS / ALPHA ** 2, 1.0, 0.0, 0.0], np.float32)[None, :])
    return c


def ffn_items(i):
    out = []
    for j in range(NF // 2):
        out += [(f"g{i}", j), (f"u{i}", j)]
        if i == 0 and j == 1:
            out.append(("rowsT", 0))
        if i == 0 and j == 8:
            out.append(("bcT", 0))
        if j >= 1:
            out.append((f"d{i}", j - 1))
    return out + [(f"d{i}", NF // 2 - 1)]


def plan():
    zs = [("z", j) for j in (0, 1, 6, 7, 8, 9, 10, 11, 12, 2, 3, 4, 5)]
    mid = [("gate", j) for j in range(4)] + [("w1", 0), ("w2", 0), ("w1", 1), ("w2", 1)]
    mid += [("gate", j) for j in range(4, 8)] + [("lru", 0), ("lru", 1)] + [("gate", j) for j in range(8, 12)]
    mid += [("memT", 0)] + [("k", j) for j in range(4)] + [("v", 0), ("rw", 0), ("rw", 1), ("v", 1)]
    mid += [("mix", j) for j in range(4)] + [("v", 2), ("v", 3)]
    out = ffn_items(0) + [("lnT", 0)] + zs + mid + [("lnT", 1)] + [("q", j) for j in range(4)] + [("attn", h) for h in range(XH)]
    return out + [("wo", j) for j in range(4)] + [("lnT", 2)] + ffn_items(1) + [("lnT", 3)]


BANKS_OF = {"rowsT": 1, "memT": 4, "bcT": 4, "lnT": 4, "g0": 1, "u0": 1, "g1": 1, "u1": 1, "z": 1, "gate": 1, "w1": 2, "w2": 2,
            "lru": 2, "rw": 2, "k": 1, "v": 1, "q": 1, "attn": 1}
NOT_WEIGHTS = ("attn", "rowsT", "bcT", "memT", "lnT")
PLAN = plan()
FFN_KINDS = "gud"
PIECES = [(kind, j, m) for kind, j in PLAN if kind not in NOT_WEIGHTS for m in range(2)]
INDEX = {x: n for n, x in enumerate(PIECES)}
PLAIN = ("w1", "w2", "lru", "rw")
SPLIT_AT = {}
LO_AT = {}
for _n, _x in enumerate(PIECES):
    if _x[0] not in PLAIN:
        _who = "pool" if _x[0] == "gate" else "dve"
        SPLIT_AT[_n] = len(SPLIT_AT)
        LO_AT[_n] = (_who, sum(w == _who for w, _ in LO_AT.values()))
SPLITS = list(SPLIT_AT)
ROTA = [(x, b) for x in PLAN for b in range(BANKS_OF.get(x[0], 0))]
ROTA_AT = {x: n for n, x in enumerate(ROTA)}
ZORD = [x[1] for x in PLAN if x[0] == "z"]


def trunk(nc, io, consts, out):
    with ExitStack() as ctx:
        cursor = [(nc.sbuf_base + 63) // 32 * 32]

        def sb(name, n, dtype=F32):
            t = nc.alloc_sbuf_tensor_at(name, [P, n], dtype, offset=cursor[0])
            cursor[0] += 4 * n
            return t, cursor[0] - 4 * n

        def rounded(name, place, at, *dims):
            n = 1
            for d in dims:
                n *= d
            return view(nc.alloc_sbuf_tensor_at(name, [P, n], F32R, offset=place + 4 * at), 0, *dims)

        def sem(name):
            s = nc.alloc_semaphore(name)
            sems.append(s)
            return s

        sems = []

        raw, _ = sb("ring_raw", RAW * PIECE)
        ring_hi, _ = sb("ring_hi", SPLIT * PIECE, F32R)
        ring_lo, _ = sb("ring_lo", SPLIT * PIECE, F32R)
        xtok_t, _ = sb("x_tok", NT * D)
        xTh_t, _ = sb("xT_hi", ND * T, F32R)
        xTl_t, _ = sb("xT_lo", ND * T, F32R)
        reg_a, a_at = sb("region_a", 6144)
        reg_r, r_at = sb("region_r", 8192)
        reg_z, _ = sb("region_z", 4 * T + RWT * (T + 1) + 4 * (T + 3) + 4 * T + 6)
        work, w_at = sb("work", 12288)
        cst, _ = sb("constants", (NCONST + 7) // 8 * 8)
        pcol, _ = sb("param_columns", 2 * P)
        small, _ = sb("small", 512)
        wgate, _ = sb("lru_gate_weights", 2 * NW * P)
        ups, _ = sb("up_weights", 2 * W)
        bT, _ = sb("s5_b", 2 * NW * P)
        cT, _ = sb("s5_c", 2 * NW * P)

        def view(region, at, *dims):
            n = 1
            for d in dims:
                n *= d
            v = region[:, at:at + n]
            if len(dims) == 1:
                return v
            names = "abcd"[:len(dims)]
            return v.rearrange(f"p ({' '.join(names)}) -> p {' '.join(names)}",
                               **{x: d for x, d in zip(names[1:], dims[1:])})

        def const(name):
            a, n = CCOL[name]
            return cst[:, a:a + n]

        def ccol(k):
            a = CCOL["cols"][0]
            return cst[:, a + k:a + k + 1]

        HALF_PI, TINY, GNE, NEG_HALF, LNE, ONE, ZERO = (ccol(k) for k in range(7))
        ident = const("ident")

        def pc(name, k=0, n=1):
            a = (PCOL_A if name in PCOL_A else PCOL_B)[name][0]
            return pcol[:, a + k:a + k + n]

        xtok = view(xtok_t, 0, NT, D)
        xT = [view(xTh_t, 0, ND, T), view(xTl_t, 0, ND, T)]
        hT = [rounded("hT_hi", a_at, 0, NF, T), rounded("hT_lo", w_at, 6144, NF, T)]
        gates = view(reg_a, 0, ND, T)
        merged = view(reg_a, 2048, ND, T)
        BK = view(reg_a, 4096, NW, NC, 2, C)
        attn_p = view(reg_a, 0, XH, NT, M)
        attn_pT = view(reg_a, 2048, XH, 2, T)
        oT = [rounded("oT_hi", a_at, 4096, ND, T), rounded("oT_lo", w_at, 8192, ND, T)]
        cosT = view(reg_r, 0, NS, T)
        sinT = view(reg_r, 4096, NS, T)
        G = view(reg_r, 0, NQ * 2, P)
        BKtok = view(reg_r, 4096, NQ, P)
        SV = view(reg_r, 6144, NC, 8, C)
        memT = [rounded("memT_hi", r_at, 0, ND, M), rounded("memT_lo", r_at, 2048, ND, M)]
        kmT = view(reg_r, 4096, ND, M)
        vm = view(reg_r, 6144, 2, D)
        zu = view(reg_z, 0, NW, T)
        zrw = view(reg_z, 1024, RWT, T + 1)
        V_AT = 1024 + 8 * (T + 1)
        LX_AT = 1024 + RWT * (T + 1)
        lx = view(reg_z, LX_AT, NW, T + 3)
        ly = view(reg_z, LX_AT + NW * (T + 3), NW, T)
        memtok = view(reg_z, LX_AT, 2, D)
        b_raw = [view(reg_z, 256 * i, NS, 16) for i in range(2)]
        c_raw = [view(reg_z, 512 + 256 * i, NW, C) for i in range(2)]
        b_bd = [view(reg_z, 1024 + 512 * i, NW, P) for i in range(2)]
        c_bd = [view(reg_z, 2048 + 512 * i, NW, P) for i in range(2)]
        rot = [view(reg_z, 3072 + 1024 * i, 4, T) for i in range(3)]
        prow = view(reg_z, 6144, 2, P)
        Wst = view(reg_z, 1024, NQ, C)
        Ysb = view(reg_z, 2048, NQ, C)
        tmpB = view(reg_z, 3072, NQ, C)
        yT = view(reg_z, 1024, NW, T)
        AR = view(work, 0, NW, NC, 2, C)
        gRW = view(work, 2048, NW, T)
        bonus = view(work, 3072, NW, T)
        wk = [view(work, 4096 + 1024 * i, NW, T) for i in range(8)]
        W_bd = view(work, 4096, NQ, P)
        M_bd = view(work, 6144, NQ, P)
        X_bd = view(work, 8192, NQ, P)
        Usb = view(work, 10240, NW, C)
        S0 = [view(work, 10496 + 256 * i, NW, C) for i in range(2)]
        lnbc = view(work, 0, 2, D)
        sil = [view(work, 4096 + 512 * i, 512) for i in range(2)]
        htmp = [view(work, 5120 + 512 * i, 512) for i in range(2)]
        bt_tmp = [view(work, 11776 + 256 * i, NS, 16) for i in range(2)]
        xf = view(work, 6144, ND, T)
        qT = view(work, 4096, ND, T)
        merged_r = [rounded("merged_hi", w_at, 7168, ND, T), rounded("merged_lo", w_at, 9216, ND, T)]
        s5m = view(work, 0, 2, 2, T)
        s5v = view(work, 1024, 2, T)
        s5z = [view(work, 1536 + 512 * i, 2, T) for i in range(2)]
        s5n = view(work, 2560, 2, 2, T)
        s5s = [view(work, 3584 + 512 * i, 2, T) for i in range(2)]
        kk = view(work, 3072, NW, T)
        kk_sq = view(work, 0, NW, T)
        kk_norm = view(work, 1024, NW, T)
        mtmp = view(work, 11264, NW, T)
        col = {}
        at = [0]

        def small_cols(name, n):
            col[name] = small[:, at[0]:at[0] + n]
            at[0] += n
            return col[name]

        stats = [small_cols(f"stats{t}", 12) for t in range(NT)]
        mv = [small_cols(f"mv{t}", 2) for t in range(NT)]
        vare = [small_cols(f"vare{t}", 1) for t in range(NT)]
        nbias = [small_cols(f"nbias{t}", 1) for t in range(NT)]
        rstd = [small_cols(f"rstd{t}", 1) for t in range(NT)]
        dt_, xr, rho, th, em, den = (small_cols(n, NS) for n in ("dt", "xr", "rho", "th", "em", "den"))
        ang, rnd, phi, s1, c1, aab = (small_cols(n, NS) for n in ("ang", "rnd", "phi", "s1", "c1", "aab"))
        nre, nim, fr, fi, t1, t2 = (small_cols(n, NS) for n in ("nre", "nim", "fr", "fi", "t1", "t2"))
        dt_raw = small_cols("dt_raw", 2)
        u_, w_, w2_, pl = (small_cols(n, NW) for n in ("u", "w", "w2", "pl"))
        sp8, sp8n, omka, alam = (small_cols(n, NW) for n in ("sp8", "sp8n", "omka", "alam"))
        pC = small_cols("pC", NQ).rearrange("p (t c) -> p t c", t=NW)
        nmax, rsum, rinv = (small_cols(n, 2 * XH) for n in ("nmax", "rsum", "rinv"))
        assert at[0] <= 512

        banks = [ctx.enter_context(nc.psum_tensor(f"bank{b}", [P, 512], F32)) for b in range(8)]

        def bank(b, *dims):
            names = "abcd"[:len(dims)]
            if len(dims) <= 1:
                return banks[b][:, :]
            return banks[b][:, :].rearrange(f"p ({' '.join(names)}) -> p {' '.join(names)}",
                                            **{x: d for x, d in zip(names[1:], dims[1:])})

        def rota(kind, j, b=0):
            return ROTA_AT[((kind, j), b)] % 4

        s_pre = nc.alloc_semaphore("prologue_loaded")
        s_preT = nc.alloc_semaphore("prologue_turned")
        s_preX = nc.alloc_semaphore("prologue_split")
        s_preA = nc.alloc_semaphore("prologue_act")
        s_preD = nc.alloc_semaphore("prologue_dve")
        s_zero = nc.alloc_semaphore("zeros_written")
        s_end = nc.alloc_semaphore("layer_ended")
        s_go = {e: nc.alloc_semaphore(f"next_layer_{e}") for e in ("pe", "act", "dve", "pool")}
        s_out = nc.alloc_semaphore("output_stored")
        s_head = [nc.alloc_semaphore(f"first_weights_loaded{i}") for i in range(RAW)]

        s_w = [sem(f"weights_loaded{i}") for i in range(RAW)]
        s_piece = sem("piece_multiplied")
        s_hi = sem("weights_hi")
        s_lo = {"dve": sem("weights_lo_dve"), "pool": sem("weights_lo_pool")}
        s_hh = sem("hidden_hi")
        s_hl = sem("hidden_lo")
        s_xTp = sem("xT_lo_from_pool")
        s_mh = sem("merged_hi")
        s_ml = sem("merged_lo")
        s_memTl = sem("memory_lo")
        s_oh = sem("o_hi")
        s_par = sem("parameters_loaded")
        s_raw = sem("s5_matrices_loaded")
        s_lnw = sem("ln_weights_loaded")
        s_memld = sem("memory_loaded")
        s_rowsT = sem("parameter_rows_turned")
        s_pcol = sem("parameter_columns")
        s_silu = sem("silu_done")
        s_h = sem("hidden_done")
        s_lny = sem("ln_residual_read")
        s_lnv = sem("ln_variance")
        s_lnr = sem("ln_rstd")
        s_lnx = sem("ln_normalised_dve")
        s_lnxa = sem("ln_normalised_act")
        s_lnT = sem("ln_turned")
        s_xTa = sem("xT_from_act")
        s_xTd = sem("xT_from_dve")
        s_xg = sem("x_tok_gain_applied")
        s_p1 = sem("prep_dve")
        s_p2 = sem("prep_act")
        s_p3 = sem("prep_pool")
        s_bcT = sem("bc_turned")
        s_bce = sem("bc_evac_act")
        s_rot = sem("rotation_dve")
        s_rots = sem("rotation_act")
        s_z = sem("z_evacuated")
        s_bu = sem("s5_bu")
        s_fwd = sem("s5_rotated")
        s_scan = sem("s5_scanned")
        s_back = sem("s5_rotated_back")
        s_y5 = sem("s5_y")
        s_y5d = sem("s5_y_plus_du")
        s_ys5 = sem("s5_gelu")
        s_conv = sem("lru_conv")
        s_lg = sem("lru_gates_product")
        s_lga = sem("lru_gates_act")
        s_lq = sem("lru_square")
        s_lm = sem("lru_multiplier")
        s_yl = sem("lru_y")
        s_shift = sem("rwkv_shifted")
        s_lora_in = sem("rwkv_lora_input")
        s_lora = sem("rwkv_lora_product")
        s_lora_a = sem("rwkv_lora_act")
        s_kk = sem("rwkv_kk")
        s_sq = sem("rwkv_kk_squared")
        s_ss = sem("rwkv_kk_sums")
        s_nrm = sem("rwkv_kk_norm")
        s_dec = sem("rwkv_decay_sums")
        s_exp = sem("rwkv_exponentials")
        s_ex = sem("rwkv_exponentials_used")
        s_rk = sem("rwkv_rk")
        s_rks = sem("rwkv_rk_scaled")
        s_bon = sem("rwkv_bonus_sums")
        s_ops = sem("rwkv_operands")
        s_tok = sem("rwkv_turned")
        s_toke = sem("rwkv_turned_evac_act")
        s_tokv = sem("rwkv_turned_evac_dve")
        s_G = sem("rwkv_G")
        s_Ge = sem("rwkv_G_masked")
        s_N = sem("rwkv_N")
        s_Nb = sem("rwkv_N_masked")
        s_Wb = sem("rwkv_W_dve")
        s_Wst = sem("rwkv_W_stacked")
        s_Wp = sem("rwkv_W_pool")
        s_tmp = sem("rwkv_W_step")
        s_T = sem("rwkv_solve_turned")
        s_Ta = sem("rwkv_solve_evac_act")
        s_Td = sem("rwkv_solve_evac_dve")
        s_Y = sem("rwkv_Y")
        s_Ye = sem("rwkv_Y_evac")
        s_WY = sem("rwkv_WY")
        s_U = sem("rwkv_U")
        s_Ue = sem("rwkv_U_evac")
        s_Sa = sem("rwkv_Sa")
        s_Sae = sem("rwkv_Sa_evac")
        s_Sn = sem("rwkv_state_product")
        s_S = sem("rwkv_state")
        s_y = sem("rwkv_y")
        s_ye = sem("rwkv_y_evac")
        s_mean = sem("rwkv_mean")
        s_yc = sem("rwkv_centred")
        s_ysq = sem("rwkv_centred_squared")
        s_var = sem("rwkv_variance")
        s_gnr = sem("rwkv_std")
        s_yrw = sem("rwkv_gated")
        s_gact = sem("gates_activated")
        s_glu = sem("glu_sigmoid")
        s_m = sem("merged_banks_read")
        s_acc = sem("token_banks_multiplied")
        s_bonr = sem("rwkv_bonus_read")
        s_dtx = sem("log_dt_rows_spread")
        s_zz = sem("row_zeros_written")
        s_kv = sem("memory_kv_evac")
        s_memT = sem("memory_turned")
        s_memTe = sem("memory_turned_evac")
        s_q = sem("q_evac")
        s_sc = sem("scores")
        s_mx = sem("score_max")
        s_ex2 = sem("softmax_exp")
        s_pn = sem("softmax_normalised")
        s_pT = sem("p_turned")
        s_pTe = sem("p_turned_evac")
        s_o = sem("o_product")
        s_oe = sem("o_evac")
        c_act, c_dve, c_pool = sem("act_chain"), sem("dve_chain"), sem("pool_chain")

        CLEAR = range(sems[0].num, sems[-1].num + 1)
        assert [s.num for s in sems] == list(CLEAR)

        def released(item, b):
            kind, j = item
            if kind in ("g0", "u0"):
                return s_h, j + 1
            if kind in ("g1", "u1"):
                return s_h, NF // 2 + j + 1
            if kind == "rowsT":
                return s_pcol, 1
            if kind == "bcT":
                return (s_bce, b + 1)
            if kind == "memT":
                return s_memTl, b + 1
            if kind == "lnT":
                return (s_xTa, 2 * j + b + 1) if b < 2 else (s_xTd, 2 * j + b - 1)
            if kind == "z":
                return s_z, ZORD.index(j) + 1
            if kind == "gate":
                return s_gact, j + 1
            if kind == "w2":
                return s_glu, 2 * j + b + 1
            if kind == "w1":
                return s_m, 2 * j + b + 1
            if kind == "lru":
                return s_m, 4 + 2 * j + b + 1
            if kind == "rw":
                return s_m, 8 + 2 * j + b + 1
            if kind == "k":
                return s_kv, j + 1
            if kind == "v":
                return s_kv, 4 + j + 1
            if kind == "q":
                return s_q, j + 1
            if kind == "attn":
                return s_oe, j + 1
            raise KeyError(kind)

        def source(l, kind, j, m):
            def rows(w, k0, nk, c0, n):
                part = w[l, bass.ds(k0 * P, nk * P), bass.ds(c0, n)]
                return part.rearrange("(k p) n -> p k n", p=P), nk, n
            if kind in PLAIN:
                w = {"w1": "s5_glu_w1", "w2": "s5_glu_w2", "lru": "lru_w_out", "rw": "rw_w_out"}[kind]
                return rows(io[w], 0, NW, 512 * j + 256 * m, 256)
            if kind in ("d0", "d1", "mix", "wo"):
                w = {"d0": "ffn1_wd", "d1": "ffn2_wd", "mix": "mix_w_out", "wo": "xa_wo"}[kind]
                return rows(io[w], j * 2 + m, 1, 0, D)
            if kind == "v":
                return rows(io["xa_wkv"], ND // 2 * m, ND // 2, D + 256 * j, 256)
            w, c0 = {"g0": ("ffn1_wg", 0), "u0": ("ffn1_wu", 0), "g1": ("ffn2_wg", 0), "u1": ("ffn2_wu", 0),
                     "z": ("w_in", 0), "gate": ("w_in", GATE0), "k": ("xa_wkv", 0),
                     "q": ("xa_wq", 0)}[kind]
            return rows(io[w], 0, ND, j * 256 + (c0 + P * m), P)

        def slot(ring, i, nk, cols):
            return ring[:, i * PIECE:i * PIECE + nk * cols].rearrange("p (k n) -> p k n", k=nk)

        def loaded(eng, n):
            if n < RAW:
                eng.wait_ge(s_head[n], 16)
                eng.sem_clear(s_head[n])
            else:
                eng.wait_ge(s_w[n % RAW], 16 * (n // RAW))

        def raw_flat(n):
            return raw[:, (n % RAW) * PIECE:(n % RAW + 1) * PIECE]

        def split_flat(ring, f):
            return ring[:, (f % SPLIT) * PIECE:(f % SPLIT + 1) * PIECE]

        def split_index(kind, j, m=1, ahead=0):
            return min(SPLIT_AT[INDEX[(kind, j, m)]] + ahead, len(SPLITS) - 1)

        def done_chunk(eng, kind, j):
            eng.wait_ge(s_piece, INDEX[(kind, j, 1)] + 1)

        class Steps:

            def __init__(self, eng, chain):
                self.eng, self.chain, self.n = eng, chain, {}

            def mark(self, ins, s):
                ins.then_inc(s, 1)
                self.n[s.name] = self.n.get(s.name, 0) + 1
                return self.n[s.name]

            def then(self, ins, s=None):
                s = s or self.chain
                self.eng.wait_ge(s, self.mark(ins, s))

        def layer_end(eng, who):
            eng.drain().then_inc(s_end, 1)
            eng.wait_ge(s_go[who], 1)
            eng.sem_clear(s_go[who])

        block = ctx.enter_context(nc.Block())

        @block.sync
        def _(sp):
            sp.dma_start(cst[:, 0:NCONST], consts).then_inc(s_pre, 16)
            sp.dma_start(xtok, io["x"][0].rearrange("(t p) d -> p t d", p=P)).then_inc(s_pre, 16)

            def first_pieces(l):
                for n in range(RAW):
                    kind, j, m = PIECES[n]
                    src, nk, cols = source(l, kind, j, m)
                    sp.dma_start(slot(raw, n, nk, cols), src).then_inc(s_head[n], 16)

            def parameters(l):
                source_of = {"lam_re": "s5_lam_re", "lam_im": "s5_lam_im", "s5_d": "s5_d", "conv_w": "lru_conv_w",
                             "conv_b": "lru_conv_b", "ba": "lru_ba", "bx": "lru_bx", "lam": "lru_lambda",
                             "mu": "rw_mu", "w0": "rw_w0", "a0": "rw_a0", "k_k": "rw_k_k", "k_a": "rw_k_a",
                             "r_k": "rw_r_k", "gn_g": "rw_ln_g", "gn_b": "rw_ln_b"}
                out = []
                for name, (r0, n) in PCOL_A.items():
                    if name == "log_dt":
                        a = io["s5_log_dt"][l].rearrange("(s g) -> s g", g=2)
                        out.append((dt_raw[r0:r0 + n, :], a, s_par))
                        continue
                    a = io[source_of[name]][l]
                    if name in ("lam_re", "lam_im", "r_k"):
                        a = a.rearrange("(n h) c -> n (h c)", n=n)
                    elif name == "conv_w":
                        a = a.rearrange("j (t c) -> (j t) c", c=P)
                    else:
                        a = a.rearrange("(n c) -> n c", c=P)
                    out.append((prow[r0:r0 + n, 0, :], a, s_par))
                for name, (r0, n) in PCOL_B.items():
                    a = io[f"ln{int(name[2]) + 1}_{name[-1]}"][l]
                    out.append((prow[r0 - P:r0 - P + n, 1, :], a.rearrange("(n c) -> n c", c=P), s_par))
                assert len(out) == N_PAR_DMA
                for par in range(2):
                    for g, name in enumerate(("lru_wa", "lru_wx")):
                        out.append((view(wgate, 512 * g, NW, P)[C * par:C * par + C, :, C * par:C * par + C],
                                    io[name][l].rearrange("(t h) i j -> h i t j", h=2)[par], s_raw))
                for g, name in enumerate(("s5_b_re", "s5_b_im")):
                    for h in range(2):
                        out.append((b_raw[g][64 * h:64 * h + 64],
                                    io[name][l].rearrange("(s h) q c -> h q s c", h=2)[h], s_raw))
                for g, name in enumerate(("s5_c_re", "s5_c_im")):
                    out.append((c_raw[g], io[name][l].rearrange("(t g) c q -> (g c) t q", t=NW), s_raw))
                out.append((ups[0:C, 0:W], io["rw_w_up"][l], s_raw))
                out.append((ups[C:P, 0:W], io["rw_a_up"][l], s_raw))
                out.append((ups[:, W:2 * W], io["rw_g_up"][l], s_raw))
                return out

            def layer(l):
                def piece(n, step=0):
                    kind, j, m = PIECES[n]
                    if n - RAW in LO_AT:
                        who, i = LO_AT[n - RAW]
                        sp.wait_ge(s_lo[who], 2 * len(FFN_KINDS) * step + i + 1)
                    else:
                        sp.wait_ge(s_piece, n - RAW + 1)
                    src, nk, cols = source(l, kind, j + step, m)
                    sp.dma_start(slot(raw, n % RAW, nk, cols), src).then_inc(s_w[n % RAW], 16)

                def ffn(i, first, peeled):
                    n0 = INDEX[(f"g{i}", 0, 0)]
                    n1 = n0 + 4 + 2 * len(FFN_KINDS) * peeled
                    for n in range(n0 + first, n1):
                        piece(n)
                        if i == 0:
                            for dst, src, s in params[4 * (n - n0 - first):4 * (n - n0 - first + 1)]:
                                sp.dma_start(dst, src).then_inc(s, 16)
                    with sp.Fori(0, NF // 2 - 1 - peeled) as step:
                        for n in range(n1, n1 + 2 * len(FFN_KINDS)):
                            piece(n, step)
                    n = INDEX[(f"d{i}", NF // 2 - 1, 0)]
                    piece(n)
                    piece(n + 1)

                params = parameters(l)
                ffn(0, RAW, 2)
                assert len(params) <= 4 * (4 + 2 * len(FFN_KINDS) * 2 - RAW)
                for n in range(INDEX[("d0", NF // 2 - 1, 1)] + 1, INDEX[("g1", 0, 0)]):
                    piece(n)
                ffn(1, 0, 0)

            def layer_over():
                sp.wait_ge(s_end, 4)
                sp.sem_clear(CLEAR)
                sp.sem_clear(s_end)
                sp.drain()
                for who in ("pe", "act", "dve", "pool"):
                    sp.sem_inc(s_go[who], 1)

            first_pieces(0)
            sp.wait_ge(s_zero, 1)
            with sp.Fori(0, L - 1) as l:
                layer(l)
                sp.wait_ge(s_lo["dve"], LO_AT[len(PIECES) - 1][1] + 1)
                first_pieces(l + 1)
                layer_over()
            layer(L - 1)
            layer_over()
            sp.dma_start(out[0].rearrange("(t p) d -> p t d", p=P), xtok).then_inc(s_out, 16)
            sp.wait_ge(s_out, 16)

        @block.tensor
        def _(pe):
            mm = nc.tensor.matmul

            def claim(kind, j, b=0):
                r = ROTA_AT[((kind, j), b)]
                if r >= 4:
                    s, v = released(*ROTA[r - 4])
                    pe.wait_ge(s, v)
                return banks[r % 4]

            def take(kind, j, m):
                n = INDEX[(kind, j, m)]
                who, i = LO_AT[n]
                pe.wait_ge(s_lo[who], i + 1)
                _, nk, cols = source(0, kind, j, m)
                return [slot(ring, SPLIT_AT[n] % SPLIT, nk, cols) for ring in (ring_hi, ring_lo)]

            def mm3(o, a, b, first, last, **kw):
                mm(o, a[0], b[0], start=first, stop=False, **kw)
                mm(o, a[0], b[1], start=False, stop=False, **kw)
                return mm(o, a[1], b[0], start=False, stop=last, **kw)

            def half_chunk(kind, j, m, src, ready=None):
                if kind in PLAIN:
                    n = INDEX[(kind, j, m)]
                    loaded(pe, n)
                    w, o = slot(raw, n % RAW, NW, 256), claim(kind, j, m)
                    for c in range(2):
                        for k in range(NW):
                            last = mm(o[:, c * T:(c + 1) * T], w[:, k, c * P:(c + 1) * P], src[:, k, :],
                                      start=(k == 0), stop=(k == NW - 1))
                else:
                    if m == 0:
                        claim(kind, j)
                    o = banks[rota(kind, j)]
                    w = take(kind, j, m)
                    for i, k in enumerate(range(ND) if kind == "k" else (4, 5, 0, 1, 6, 7, 2, 3)):
                        if ready is not None and i % 2 == 0:
                            ready(k // 2)
                        last = mm3(o[:, m * T:(m + 1) * T], [x[:, k, :] for x in w], [x[:, k, :] for x in src],
                                   i == 0, i == ND - 1)
                last.then_inc(s_piece, 1)

            def by_channel(kind, j, src, ready=None):
                half_chunk(kind, j, 0, src, ready)
                half_chunk(kind, j, 1, src)

            def token_piece(kind, j, m, src, first, last_chunk):
                w = take(kind, j, m)
                end = last_chunk and m == 1
                for t in range(NT):
                    for h in range(2):
                        last = mm3(banks[4 + 2 * t + h][:, :], [x[:, 2 * j + m, t * P:(t + 1) * P] for x in src],
                                   [x[:, 0, 512 * h:512 * (h + 1)] for x in w], first and m == 0, end)
                        if end and (t == 0 or h == 0):
                            last.then_inc(s_acc, 1)
                last.then_inc(s_piece, 1)

            def by_token(kind, j, src, first, last_chunk):
                for m in range(2):
                    token_piece(kind, j, m, src, first, last_chunk)

            def ffn(i):
                for kind, j in ffn_items(i):
                    if kind[0] in "gu":
                        by_channel(kind, j, xT, xT_ready(2) if (kind, j) == ("g1", 0) else None)
                    elif kind == "rowsT":
                        o = claim("rowsT", 0)
                        pe.wait_ge(s_par, 16 * N_PAR_DMA)
                        pe.wait_ge(s_dtx, 1)
                        nc.tensor.transpose(o[:, 0:NA], prow[0:NA, 0, :], ident[0:NA, 0:NA])
                        nc.tensor.transpose(o[:, P:P + NB - P], prow[0:NB - P, 1, :], ident[0:NB - P, 0:NB - P])\
                            .then_inc(s_rowsT, 1)
                    elif kind == "bcT":
                        pe.wait_ge(s_p3, 4)
                        for b, src in enumerate(b_bd + c_bd):
                            o = claim("bcT", 0, b)
                            for t in range(NW):
                                last = nc.tensor.transpose(o[:, t * P:(t + 1) * P], src[:, t, :], ident)
                            last.then_inc(s_bcT, 1)
                    else:
                        if i == 1 and j == 0:
                            pe.wait_ge(s_lny, 3 * NT)
                        pe.wait_ge(s_hl, i * (NF // 2) + j + 1)
                        by_token(kind, j, hT, j == 0, j == NF // 2 - 1)

            def ln_turn(n):
                os = [claim("lnT", n, b) for b in range(4)]
                for t in range(NT):
                    pe.wait_ge(s_lnxa, NT * n + t + 1)
                    if t == 1:
                        pe.wait_ge(s_lnx, n + 1)
                    for d in range(ND):
                        last = nc.tensor.transpose(os[d // 2][:, (d % 2) * T + t * P:(d % 2) * T + (t + 1) * P],
                                                   xtok[:, t, d * P:(d + 1) * P], ident)
                    last.then_inc(s_lnT, 1)

            def xT_ready(n):
                def wait(b):
                    if b < 2:
                        pe.wait_ge(s_xTa, 2 * n + b + 1)
                        pe.wait_ge(s_xTp, 2 * n + b + 1)
                    else:
                        pe.wait_ge(s_xTd, 2 * n + b - 1)
                return wait

            pe.wait_ge(s_pre, 32)
            for t in range(NT):
                for d in range(ND):
                    last = nc.tensor.transpose(banks[d // 2][:, (d % 2) * T + t * P:(d % 2) * T + (t + 1) * P],
                                               xtok[:, t, d * P:(d + 1) * P], ident)
            last.then_inc(s_preT, 1)
            pe.wait_ge(s_preX, 2)

            with pe.Fori(0, L) as l:
                ffn(0)
                ln_turn(0)

                zq = list(ZORD)

                def z_chunk():
                    by_channel("z", zq.pop(0), xT, xT_ready(0) if len(zq) == len(ZORD) - 1 else None)

                def s5_in(s):
                    t, q = s // 4, s % 4
                    if s == 0:
                        pe.wait_ge(s_z, 2)
                        pe.wait_ge(s_bce, 4)
                        pe.wait_ge(s_lny, 2)
                    if s >= 2:
                        pe.wait_ge(s_fwd, s - 1)
                    o = bank(4 + s % 2, 2, T)
                    for i in range(2):
                        last = mm(o[:, i, :], view(bT, 512 * i, NW, P)[32 * q:32 * q + 32, t, :],
                                  zu[32 * q:32 * q + 32, t, :], start=True, stop=True)
                    last.then_inc(s_bu, 1)

                def s5_out(s):
                    t, q = s // 4, s % 4
                    if q == 0 and t >= 2:
                        pe.wait_ge(s_y5d, t - 1)
                    pe.wait_ge(s_back, s + 1)
                    o = banks[6 + t % 2][32 * q:32 * q + 32, 0:T]
                    for i in range(2):
                        last = mm(o, view(cT, 512 * i, NW, P)[:, t, 32 * q:32 * q + 32], s5s[s % 2][:, i, :],
                                  start=(i == 0), stop=(i == 1))
                    last.then_inc(s_y5, 1)

                z_chunk()
                z_chunk()
                s5_in(0)
                s5_in(1)
                for s in range(NS):
                    if s % 2 == 0:
                        z_chunk()
                    if s >= 1:
                        s5_out(s - 1)
                    if s + 2 < NS:
                        s5_in(s + 2)
                while zq:
                    z_chunk()
                s5_out(NS - 1)

                def gate(j):
                    by_channel("gate", j, xT)

                gate(0)
                pe.wait_ge(s_y5d, NW)
                pe.wait_ge(s_sq, 1)
                for h in range(2):
                    last = mm(banks[6 + h][:, :], const("heads"), kk_sq[:, 2 * h:2 * h + 2, :], start=True, stop=True)
                last.then_inc(s_ss, 1)
                pe.wait_ge(s_conv, NW)
                pe.wait_ge(s_fwd, NS)
                for g in range(2):
                    if g == 1:
                        half_chunk("gate", 1, 0, xT)
                        pe.wait_ge(s_nrm, 1)
                    for t in range(NW):
                        last = mm(bank(4 + 2 * g + t // 2, 2, T)[:, t % 2, :], view(wgate, 512 * g, NW, P)[:, t, :],
                                  wk[1][:, t, :], start=True, stop=True)
                    last.then_inc(s_lg, 1)
                half_chunk("gate", 1, 1, xT)
                gate(2)
                pe.wait_ge(s_lora_in, 2)
                pe.wait_ge(s_shift, RWT)
                for t in range(NW):
                    if t % 2 == 0:
                        pe.wait_ge(s_lga, 8)
                    last = mm(bank(4 + t // 2, 2, T)[:, t % 2, :], ups[0:C, t * P:(t + 1) * P],
                              wk[7][0:C, 0, :], start=True, stop=True)
                last.then_inc(s_lora, 1)
                for t in range(NW):
                    last = mm(bank(6 + t // 2, 2, T)[:, t % 2, :], ups[C:P, t * P:(t + 1) * P],
                              zrw[C:P, 12, 1:T + 1], start=True, stop=True)
                last.then_inc(s_lora, 1)
                gate(3)
                pe.wait_ge(s_lora_a, 4)
                for t in range(NW):
                    last = mm(bank(4 + t // 2, 2, T)[:, t % 2, :], ups[:, W + t * P:W + (t + 1) * P],
                              wk[7][:, 1, :], start=True, stop=True)
                last.then_inc(s_lora, 1)

                pe.wait_ge(s_ys5, NW)
                by_channel("w1", 0, zu)
                by_channel("w2", 0, zu)
                pe.wait_ge(s_lora_a, 10)
                pe.wait_ge(s_rks, NW)
                for h in range(2):
                    last = mm(banks[4 + h][:, :], const("heads"), wk[7][:, 2 * h:2 * h + 2, :], start=True, stop=True)
                last.then_inc(s_bon, 1)
                pe.wait_ge(s_ops, 1)
                pe.wait_ge(s_bonr, 1)
                for q in range(NQ):
                    last = nc.tensor.transpose(banks[4 + q // 4][:, (q % 4) * P:(q % 4 + 1) * P],
                                               BK[:, q // NC, q % NC, :, :], ident)
                last.then_inc(s_tok, 1)
                half_chunk("w1", 1, 0, zu)
                pe.wait_ge(s_toke, 2)
                pe.wait_ge(s_tokv, 2)
                for q in range(NQ):
                    t, c = q // NC, q % NC
                    a = V_AT + t * (T + 1) + 1 + C * c - C
                    last = nc.tensor.transpose(banks[4 + q // 4][:, (q % 4) * P:(q % 4 + 1) * P],
                                               reg_z[:, a:a + P], ident)
                last.then_inc(s_tok, 1)
                half_chunk("w1", 1, 1, zu)
                for g in range(4):
                    if g == 0:
                        pe.wait_ge(s_toke, 4)
                        pe.wait_ge(s_tokv, 4)
                    if g >= 2:
                        pe.wait_ge(s_Ge, 2 * (g - 1))
                    for i in range(4):
                        q = 4 * g + i
                        for par in range(2):
                            r = slice(C * par, C * par + C)
                            last = mm(banks[4 + 2 * (g % 2) + par][:, i * P:(i + 1) * P], BK[r, q // NC, q % NC, :, :],
                                      AR[r, q // NC, q % NC, :, :], start=True, stop=True)
                    last.then_inc(s_G, 1)
                by_channel("w2", 1, zu)
                pe.wait_ge(s_Ge, 8)
                for q in range(NQ):
                    for par in range(2):
                        r = slice(C * par, C * par + C)
                        last = mm(banks[4 + 2 * par + q // 8][r, (q % 8) * C:(q % 8 + 1) * C],
                                  AR[r, q // NC, q % NC, 0, :], BK[r, q // NC, q % NC, 0, :], start=True, stop=True)
                last.then_inc(s_N, 1)
                gate(4)

                def turn_pairs(src, n=None):
                    for b in range(2):
                        if n is not None:
                            pe.wait_ge(s_Wb, 2 * n + b + 1)
                            pe.wait_ge(s_Wp, 2 * n + b + 1)
                        for q in range(8 * b, 8 * b + 8):
                            last = nc.tensor.transpose(banks[4 + q // 4][:, (q % 4) * P:(q % 4 + 1) * P], src[:, q, :],
                                                       ident)
                        last.then_inc(s_T, 1)

                pe.wait_ge(s_Nb, 8)
                turn_pairs(W_bd)
                fill = [("gate", 5, xT), ("gate", 6, xT), ("gate", 7, xT), ("lru", 0, ly), ("lru", 1, ly)]
                pe.wait_ge(s_Ta, 2)
                pe.wait_ge(s_Td, 1)
                turn_pairs(W_bd, 0)
                for i in range(5):
                    if i == 3:
                        pe.wait_ge(s_yl, NW)
                    pe.wait_ge(s_Wst, i + 1)
                    for b in range(2):
                        pe.wait_ge(s_Ta, 2 * (i + 2) if b else 2 * (i + 2) - 1)
                        for q in range(8 * b, 8 * b + 8):
                            last = mm(banks[4 + b][:, (q % 8) * C:(q % 8 + 1) * C], M_bd[:, q, :], Wst[:, q, :],
                                      start=True, stop=True)
                        last.then_inc(s_Y, 1)
                    kind, j, src = fill[i]
                    half_chunk(kind, j, 0, src)
                    pe.wait_ge(s_Td, i + 2)
                    for b in range(2):
                        pe.wait_ge(s_Ye, 2 * i + b + 1)
                        for q in range(8 * b, 8 * b + 8):
                            last = mm(banks[6 + b][:, (q % 8) * C:(q % 8 + 1) * C], X_bd[:, q, :], Ysb[:, q, :],
                                      start=True, stop=True)
                        last.then_inc(s_WY, 1)
                    half_chunk(kind, j, 1, src)
                    turn_pairs(W_bd, i + 1)

                pe.wait_ge(s_Ta, 14)
                pe.wait_ge(s_Td, 7)
                for c in range(NC):
                    if c >= 1:
                        pe.wait_ge(s_ye, 2 * c)
                    for h in range(8):
                        t, par = h // 2, h % 2
                        q = t * NC + c
                        r = slice(C * par, C * par + C)
                        last = mm(banks[4 + par][r, t * C:(t + 1) * C], G[:, 2 * q + par, 0:C], SV[:, c, h, :],
                                  start=(t == 0), stop=(c == 0), skip_group_check=True)
                    if c >= 1:
                        pe.wait_ge(s_S, c)
                        for h in range(8):
                            t, par = h // 2, h % 2
                            r = slice(C * par, C * par + C)
                            last = mm(banks[4 + par][r, t * C:(t + 1) * C], AR[r, t, c, 0, :], S0[c % 2][r, t, :],
                                      start=False, stop=True, skip_group_check=True)
                    last.then_inc(s_U, 1)
                    half_chunk("gate", 8 + c, 0, xT)
                    pe.wait_ge(s_Ue, 2 * (c + 1))
                    for h in range(8):
                        t, par = h // 2, h % 2
                        last = mm(banks[6][0:C, h * C:(h + 1) * C], X_bd[:, t * NC + c, C * par:C * par + C],
                                  Usb[:, t, :], start=True, stop=True)
                    last.then_inc(s_Sa, 1)
                    half_chunk("gate", 8 + c, 1, xT)
                    pe.wait_ge(s_Sae, c + 1)
                    if c < NC - 1:
                        for h in range(8):
                            t, par = h // 2, h % 2
                            r = slice(C * par, C * par + C)
                            last = mm(banks[7][r, t * C:(t + 1) * C], BKtok[:, t * NC + c, C * par:C * par + C],
                                      SV[:, c, h, :], start=True, stop=True)
                        last.then_inc(s_Sn, 1)
                    for h in range(8):
                        t, par = h // 2, h % 2
                        q = t * NC + c
                        r = slice(C * par, C * par + C)
                        o = banks[4 + par][r, 256 + t * C:256 + (t + 1) * C]
                        last = mm(o, SV[:, c, h, :], G[:, 2 * q + par, C:P], start=(t == 0), stop=(c == 0),
                                  skip_group_check=True)
                    if c >= 1:
                        for h in range(8):
                            t, par = h // 2, h % 2
                            r = slice(C * par, C * par + C)
                            last = mm(banks[4 + par][r, 256 + t * C:256 + (t + 1) * C], S0[c % 2][r, t, :],
                                      AR[r, t, c, 1, :], start=False, stop=True, skip_group_check=True)
                    last.then_inc(s_y, 1)
                pe.wait_ge(s_ye, 2 * NC)
                for h in range(2):
                    last = mm(banks[4 + h][:, :], const("heads"), yT[:, 2 * h:2 * h + 2, :], start=True, stop=True)
                last.then_inc(s_mean, 1)
                pe.wait_ge(s_memld, 16)
                os = [claim("memT", 0, b) for b in range(4)]
                for b in range(4):
                    for d in (2 * b, 2 * b + 1):
                        for t in range(2):
                            last = nc.tensor.transpose(os[b][:, (d % 2) * M + t * P:(d % 2) * M + (t + 1) * P],
                                                       memtok[:, t, d * P:(d + 1) * P], ident)
                    last.then_inc(s_memT, 1)
                def memory_values(j):
                    o = claim("v", j)
                    for m in range(2):
                        w = take("v", j, m)
                        for t in range(2):
                            for k in range(ND // 2):
                                last = mm3(o[:, t * 256:(t + 1) * 256],
                                           [x[:, ND // 2 * m + k, t * P:(t + 1) * P] for x in memT],
                                           [x[:, k, :] for x in w], m == 0 and t == 0 and k == 0,
                                           m == 1 and k == ND // 2 - 1, skip_group_check=True)
                        last.then_inc(s_piece, 1)

                by_channel("k", 0, memT, lambda b: pe.wait_ge(s_memTl, b + 1))
                pe.wait_ge(s_ysq, 1)
                for h in range(2):
                    last = mm(banks[6 + h][:, :], const("heads"), wk[1][:, 2 * h:2 * h + 2, :], start=True, stop=True)
                last.then_inc(s_var, 1)
                for j in range(1, 4):
                    by_channel("k", j, memT)
                memory_values(0)
                pe.wait_ge(s_yrw, 1)
                by_channel("rw", 0, wk[0])
                by_channel("rw", 1, wk[0])
                memory_values(1)
                pe.wait_ge(s_gnr, 1)
                for j in range(4):
                    pe.wait_ge(s_ml, j + 1)
                    by_token("mix", j, merged_r, j == 0, j == 3)
                memory_values(2)
                memory_values(3)
                ln_turn(1)

                def scores(h):
                    pe.wait_ge(s_q, h + 1)
                    if h == 0:
                        pe.wait_ge(s_kv, 8)
                    o = claim("attn", h)
                    for t in range(NT):
                        for d in range(2):
                            last = mm(o[:, t * M:(t + 1) * M], qT[:, 2 * h + d, t * P:(t + 1) * P],
                                      kmT[:, 2 * h + d, :], start=(d == 0), stop=(d == 1))
                    last.then_inc(s_sc, 1)

                def turn_p(h):
                    pe.wait_ge(s_pn, h + 1)
                    for t in range(NT):
                        for m in range(2):
                            last = nc.tensor.transpose(banks[rota("attn", h)][:, m * T + t * P:m * T + (t + 1) * P],
                                                       attn_p[:, h, t, m * P:(m + 1) * P], ident)
                    last.then_inc(s_pT, 1)

                def values(h):
                    pe.wait_ge(s_pTe, h + 1)
                    for d in range(2):
                        for m in range(2):
                            last = mm(banks[rota("attn", h)][:, d * T:(d + 1) * T], vm[:, m, (2 * h + d) * P:(2 * h + d + 1) * P],
                                      attn_pT[:, h, m, :], start=(m == 0), stop=(m == 1))
                    last.then_inc(s_o, 1)

                by_channel("q", 0, xT, xT_ready(1))
                by_channel("q", 1, xT)
                scores(0)
                by_channel("q", 2, xT)
                scores(1)
                by_channel("q", 3, xT)
                turn_p(0)
                scores(2)
                turn_p(1)
                values(0)
                scores(3)

                def project(j, m):
                    pe.wait_ge(s_oe, j + 1)
                    token_piece("wo", j, m, oT, j == 0, j == 3)

                project(0, 0)
                turn_p(2)
                values(1)
                project(0, 1)
                turn_p(3)
                values(2)
                project(1, 0)
                values(3)
                project(1, 1)
                for j in (2, 3):
                    project(j, 0)
                    project(j, 1)
                ln_turn(2)
                ffn(1)
                ln_turn(3)
                layer_end(pe, "pe")

        @block.scalar
        def _(act):
            st = Steps(act, c_act)

            def f(o, i, func, **kw):
                return nc.scalar.activation(o, i, func, **kw)

            hi_at = [0]

            def hi_to(kind, j, m=1, ahead=0):
                while hi_at[0] <= split_index(kind, j, m, ahead):
                    i = hi_at[0]
                    if i >= SPLIT:
                        act.wait_ge(s_piece, SPLITS[i - SPLIT] + 1)
                    loaded(act, SPLITS[i])
                    st.mark(f(split_flat(ring_hi, i), raw_flat(SPLITS[i]), ACT.Copy), s_hi)
                    hi_at[0] += 1

            def normalise(n):
                for t in range(NT):
                    act.wait_ge(s_lnr, NT * n + t + 1)
                    x = xtok[:, t, 512 * t:]
                    st.mark(f(x, x, ACT.Identity, scale=rstd[t], bias=nbias[t]), s_lnxa)

            def ln(n):
                act.wait_ge(s_lnT, NT * n + NT)
                for b in range(2):
                    src = bank(rota("lnT", n, b), 2, T)
                    for m in range(2):
                        d = 2 * b + m
                        ins = f(xf[:, d, :], src[:, m, :], ACT.Identity, scale=pc(f"ln{n}_g", d), bias=pc(f"ln{n}_b", d))
                    st.then(ins)
                    st.mark(f(xT[0][:, 2 * b:2 * b + 2, :], xf[:, 2 * b:2 * b + 2, :], ACT.Copy), s_xTa)

            def silu(i, j):
                hi_to(f"u{i}", j, 0)
                done_chunk(act, f"g{i}", j)
                if i * (NF // 2) + j >= 2:
                    act.wait_ge(s_h, i * (NF // 2) + j - 1)
                st.mark(f(sil[j % 2], banks[rota(f"g{i}", j)][:, :], ACT.Silu), s_silu)

            def hidden_hi(i, j):
                hi_to(f"u{i}", j, 1, ahead=2)
                act.wait_ge(s_h, i * (NF // 2) + j + 1)
                st.mark(f(hT[0][:, 2 * j:2 * j + 2, :].rearrange("p a t -> p (a t)"), htmp[j % 2], ACT.Copy), s_hh)

            def rotation(q, *piece):
                act.wait_ge(s_rot, 4 * q + 1)
                sl = slice(4 * q, 4 * q + 4)
                st.mark(f(sinT[:, sl, :], rot[0], ACT.Sin, scale=float(np.pi)), s_rots)
                hi_to(*piece)
                act.wait_ge(s_rot, 4 * q + 2)
                st.mark(f(cosT[:, sl, :], rot[1], ACT.Sin, scale=-float(np.pi), bias=HALF_PI), s_rots)

            act.wait_ge(s_preT, 1)
            for b in range(2):
                ins = f(xf[:, 2 * b:2 * b + 2, :], bank(b, 2, T), ACT.Copy)
            ins.then_inc(s_preA, 1)
            act.wait_ge(s_preA, 1)
            f(xT[0][:, 0:4, :], xf[:, 0:4, :], ACT.Copy).then_inc(s_preA, 1)

            with act.Fori(0, L) as l:
                def prep1():
                    act.wait_ge(s_pcol, 1)
                    st.mark(f(dt_, pc("log_dt", 0, NS), ACT.Exp), s_p2)
                    act.wait_ge(s_p1, 1)
                    st.mark(f(u_, alam, ACT.Exp, scale=-1.0), s_p2)

                def prep2():
                    act.wait_ge(s_p1, 2)
                    st.mark(f(rho, xr, ACT.Exp), s_p2)
                    st.mark(f(th, xr, ACT.Tanh, scale=0.5), s_p2)

                def prep3():
                    act.wait_ge(s_p1, 3)
                    st.mark(f(s1, ang, ACT.Sin, scale=0.5), s_p2)
                    st.mark(f(c1, aab, ACT.Sin, scale=-0.5, bias=HALF_PI), s_p2)

                def prep_evac():
                    for b in range(4):
                        dst = view(bT if b < 2 else cT, 512 * (b % 2), 512)
                        act.wait_ge(s_bcT, b + 1)
                        ins = f(dst, banks[rota("bcT", 0, b)][:, :], ACT.Copy, scale=-1.0 if b == 3 else 1.0)
                        st.mark(ins, s_bce)

                steps = {2: [prep1], 4: [prep2, prep3], 5: [lambda: rotation(0, "u0", 5, 0)],
                         7: [lambda: rotation(1, "u0", 7, 0)], 9: [prep_evac, lambda: rotation(2, "u0", 9, 0)]}
                for j in range(NF // 2):
                    if j in steps:
                        hi_to("g0", j)
                    for g in steps.get(j, ()):
                        g()
                    silu(0, j)
                    hidden_hi(0, j)
                rotation(3, "d0", NF // 2 - 1, 0)
                def ln_weights(n):
                    if n:
                        act.wait_ge(s_xg, 2 * NT * n)
                    if n == 1:
                        act.wait_ge(s_yrw, 1)
                    for k, x in enumerate("gb"):
                        act.dma_start(lnbc[:, k, :], io[f"ln{n + 1}_{x}"][l].unsqueeze(0).to_broadcast([P, D]))\
                            .then_inc(s_lnw, 16)

                ln_weights(0)
                hi_to("z", ZORD[0])
                normalise(0)
                ln(0)

                dst = {0: zu[:, 0:2, :], 1: zu[:, 2:4, :], 2: lx[:, 0:2, 3:], 3: lx[:, 2:4, 3:],
                       4: ly[:, 0:2, :], 5: ly[:, 2:4, :]}
                dst.update({6 + k: zrw[:, 2 * k:2 * k + 2, 1:] for k in range(7)})
                act.wait_ge(s_bce, 4)
                act.wait_ge(s_rot, 16)
                for j in ZORD:
                    hi_to("z", j, ahead=1)
                    done_chunk(act, "z", j)
                    func = ACT.Gelu_apprx_tanh if j in (4, 5) else ACT.Copy
                    st.mark(f(dst[j], bank(rota("z", j), 2, T), func), s_z)
                hi_to("gate", 0)
                act.wait_ge(s_kk, 1)
                st.mark(f(kk_sq, kk, ACT.Square), s_sq)
                def gate_evac(j):
                    done_chunk(act, "gate", j)
                    if j >= 4:
                        act.wait_ge(s_m, j - 3)
                    st.mark(f(gates[:, 2 * (j % 4):2 * (j % 4) + 2, :], bank(rota("gate", j), 2, T), ACT.Sigmoid),
                            s_gact)

                hi_to("gate", 1, 0)
                gate_evac(0)
                hi_to("gate", 1)
                act.wait_ge(s_ss, 1)
                for h in range(2):
                    ins = f(kk_norm[:, 2 * h:2 * h + 2, :], bank(6 + h, 2, T), ACT.Sqrt, bias=TINY)
                st.mark(ins, s_nrm)
                hi_to("gate", 2, 0)
                for g in range(2):
                    act.wait_ge(s_lg, g + 1)
                    for t in range(NW):
                        st.mark(f(wk[2 + g][:, t, :], bank(4 + 2 * g + t // 2, 2, T)[:, t % 2, :], ACT.Sigmoid,
                                  bias=pc("bx" if g else "ba", t)), s_lga)
                hi_to("gate", 2)
                act.wait_ge(s_shift, RWT)
                st.mark(f(wk[7][:, 1, :], zrw[:, 13, 1:], ACT.Sigmoid), s_lora_in)
                st.mark(f(wk[7][0:C, 0, :], zrw[0:C, 12, 1:], ACT.Tanh), s_lora_in)
                gate_evac(1)
                act.wait_ge(s_lga, 8)
                for t in range(NW):
                    f(wk[4][:, t, :], wk[2][:, t, :], ACT.Exp, scale=sp8n[:, t:t + 1])
                    st.mark(f(wk[5][:, t, :], wk[2][:, t, :], ACT.Tanh, scale=sp8[:, t:t + 1]), s_lga)
                hi_to("gate", 3)
                act.wait_ge(s_lq, 1)
                st.mark(f(wk[5], wk[5], ACT.Sqrt), s_lm)
                for t in range(NW):
                    act.wait_ge(s_y5d, t + 1)
                    st.mark(f(zu[:, t, :], zu[:, t, :], ACT.Gelu_apprx_tanh), s_ys5)
                act.wait_ge(s_yl, NW)
                for g in range(2):
                    act.wait_ge(s_lora, g + 1)
                    for t in range(NW):
                        st.mark(f(wk[1 + g][:, t, :], bank(4 + 2 * g + t // 2, 2, T)[:, t % 2, :], ACT.Sigmoid,
                                  bias=pc("a0" if g else "w0", t)), s_lora_a)
                gate_evac(2)
                act.wait_ge(s_lora, 3)
                for h in range(2):
                    st.mark(f(gRW[:, 2 * h:2 * h + 2, :], bank(4 + h, 2, T), ACT.Copy), s_lora_a)
                gate_evac(3)
                act.wait_ge(s_dec, 1)
                st.mark(f(wk[6], wk[3], ACT.Exp, scale=EDEC), s_exp)
                st.mark(f(wk[0], wk[1], ACT.Exp, scale=-EDEC), s_exp)
                act.wait_ge(s_ex, 1)
                st.mark(f(wk[0], wk[3], ACT.Exp, scale=-EDEC), s_exp)
                act.wait_ge(s_rk, 1)
                act.wait_ge(s_lora, 3)
                for t in range(NW):
                    st.mark(f(wk[7][:, t, :], wk[7][:, t, :], ACT.Copy, scale=pc("r_k", t)), s_rks)

                def glu_sigmoid(j):
                    done_chunk(act, "w2", j)
                    for b in range(2):
                        if j:
                            act.wait_ge(s_m, b + 1)
                        else:
                            act.wait_ge(s_bon, 1)
                        st.mark(f(mtmp[:, 2 * b:2 * b + 2, :], bank(rota("w2", j, b), 2, T), ACT.Sigmoid), s_glu)

                glu_sigmoid(0)
                act.wait_ge(s_tok, 1)
                act.wait_ge(s_back, NS)
                for b in range(2):
                    st.mark(f(BKtok[:, 4 * b:4 * b + 4, :], bank(4 + b, 4, P), ACT.Copy), s_toke)
                act.wait_ge(s_tok, 2)
                for b in range(2):
                    st.mark(f(SV[C:P, :, 2 * b:2 * b + 2, :], bank(4 + b, 4, 2, C)[C:P], ACT.Copy), s_toke)
                hi_to("gate", 4, 0)
                glu_sigmoid(1)
                hi_to("gate", 5, 0)
                gate_evac(4)

                def turned(dst, n):
                    act.wait_ge(s_T, 2 * n - 1)
                    for b in range(2):
                        st.mark(f(dst[:, 4 * b:4 * b + 4, :], bank(4 + b, 4, P), ACT.Copy), s_Ta)

                turned(M_bd, 1)
                turned(X_bd, 2)
                for i in range(5):
                    for b in range(2):
                        act.wait_ge(s_Y, 2 * i + b + 1)
                        st.mark(f(Ysb[:, 8 * b:8 * b + 8, :], bank(4 + b, 8, C), ACT.Copy), s_Ye)
                    if i < 3:
                        hi_to("gate", 5 + i)
                    if i < 2:
                        hi_to("gate", 6 + i, 0)
                    if i < 3:
                        gate_evac(5 + i)
                    if i == 4:
                        hi_to("gate", 8)
                    turned(X_bd, i + 3)
                act.dma_start(memtok, io["mem"][0].rearrange("(t p) d -> p t d", p=P)).then_inc(s_memld, 16)
                for c in range(NC):
                    hi_to("gate", 8 + c)
                    act.wait_ge(s_Sa, c + 1)
                    st.mark(f(SV[0:C, c, :, :], bank(6, 8, C)[0:C], ACT.Copy), s_Sae)
                    hi_to("gate", 8 + c, ahead=1)
                    gate_evac(8 + c)
                    act.wait_ge(s_y, c + 1)
                    for par in range(2):
                        r = slice(C * par, C * par + C)
                        st.mark(f(yT[r, :, C * c:C * c + C], bank(4 + par, 2, NW, C)[r, 1], ACT.Copy), s_ye)
                hi_to("k", 0)
                for b in range(4):
                    act.wait_ge(s_memT, b + 1)
                    st.mark(f(memT[0][:, 2 * b:2 * b + 2, :], bank(rota("memT", 0, b), 2, M), ACT.Copy), s_memTe)

                def k_evac(j):
                    done_chunk(act, "k", j)
                    st.mark(f(kmT[:, 2 * j:2 * j + 2, :], bank(rota("k", j), 2, M), ACT.Copy), s_kv)

                def v_evac(j):
                    done_chunk(act, "v", j)
                    st.mark(f(vm[:, :, 256 * j:256 * j + 256], bank(rota("v", j), 2, 256), ACT.Copy), s_kv)

                def merged_hi(j):
                    act.wait_ge(s_m, 8 + j + 1)
                    st.mark(f(merged_r[0][:, 2 * j:2 * j + 2, :], merged[:, 2 * j:2 * j + 2, :], ACT.Copy), s_mh)

                act.wait_ge(s_yc, 1)
                st.mark(f(wk[1], wk[0], ACT.Square), s_ysq)
                hi_to("k", 1)
                act.wait_ge(s_var, 1)
                for h in range(2):
                    ins = f(wk[2][:, 2 * h:2 * h + 2, :], bank(6 + h, 2, T), ACT.Sqrt, bias=GNE, scale=1.0 / C)
                st.mark(ins, s_gnr)
                k_evac(0)
                for j in range(1, 4):
                    hi_to("k", j, ahead=1)
                    k_evac(j)
                hi_to("v", 0)
                v_evac(0)
                ln_weights(1)
                hi_to("v", 1, 0)
                merged_hi(0)
                merged_hi(1)
                hi_to("v", 1)
                merged_hi(2)
                merged_hi(3)
                hi_to("mix", 0)
                v_evac(1)
                hi_to("v", 2, ahead=1)
                v_evac(2)
                hi_to("v", 3)
                normalise(1)
                hi_to("q", 0, 0)
                v_evac(3)
                hi_to("q", 0)
                ln(1)
                def softmax_exp(h):
                    act.wait_ge(s_mx, h + 1)
                    for t in range(NT):
                        k = NT * h + t
                        ins = f(attn_p[:, h, t, :], banks[rota("attn", h)][:, t * M:(t + 1) * M], ACT.Exp, bias=nmax[:, k:k + 1],
                                scale=1.0 / 16.0, accum_out=rsum[:, k:k + 1])
                    st.mark(ins, s_ex2)

                def q_evac(j):
                    done_chunk(act, "q", j)
                    st.mark(f(qT[:, 2 * j:2 * j + 2, :], bank(rota("q", j), 2, T), ACT.Copy), s_q)

                def p_evac(h):
                    act.wait_ge(s_pT, h + 1)
                    st.mark(f(attn_pT[:, h, :, :], bank(rota("attn", h), 2, T), ACT.Copy), s_pTe)

                def o_hi(h):
                    act.wait_ge(s_o, h + 1)
                    st.mark(f(oT[0][:, 2 * h:2 * h + 2, :], bank(rota("attn", h), 2, T), ACT.Copy), s_oh)

                hi_to("q", 1, 0)
                q_evac(0)
                hi_to("q", 2, 0)
                q_evac(1)
                hi_to("q", 2)
                softmax_exp(0)
                hi_to("q", 3, 0)
                q_evac(2)
                hi_to("q", 3)
                softmax_exp(1)
                hi_to("wo", 0, 0)
                q_evac(3)
                hi_to("wo", 0)
                p_evac(0)
                softmax_exp(2)
                p_evac(1)
                o_hi(0)
                softmax_exp(3)
                hi_to("wo", 1, 0)
                p_evac(2)
                o_hi(1)
                hi_to("wo", 1)
                p_evac(3)
                o_hi(2)
                hi_to("wo", 2, 0)
                o_hi(3)
                ln_weights(2)
                hi_to("g1", 0)
                normalise(2)
                ln(2)
                for j in range(NF // 2):
                    silu(1, j)
                    hidden_hi(1, j)
                ln_weights(3)
                hi_to("d1", NF // 2 - 1)
                normalise(3)
                ln(3)
                layer_end(act, "act")

        @block.vector
        def _(dve):
            st = Steps(dve, c_dve)
            v = nc.vector
            tt, ts, stt = v.tensor_tensor, v.tensor_scalar, v.scalar_tensor_tensor

            lo_at = [0]

            def lo_to(kind, j, m=1, ahead=0):
                while lo_at[0] <= split_index(kind, j, m, ahead):
                    i = lo_at[0]
                    if LO_AT[SPLITS[i]][0] == "dve":
                        dve.wait_ge(s_hi, i + 1)
                        st.mark(tt(split_flat(ring_lo, i), raw_flat(SPLITS[i]), split_flat(ring_hi, i), ALU.subtract),
                                s_lo["dve"])
                    lo_at[0] += 1

            def ln(n, kind, j, scale, after, within=()):
                if n:
                    dve.wait_ge(s_xg, 2 * NT * n)
                for t in range(NT):
                    for h in range(2):
                        if t == 0 or h == 0:
                            dve.wait_ge(s_acc, 3 * n + 2 * t + h + 1)
                        else:
                            done_chunk(dve, kind, j)
                        x = xtok[:, t, 512 * h:512 * h + 512]
                        ins = stt(x, banks[4 + 2 * t + h][:, :], scale, x, ALU.mult, ALU.add)
                        if h == 1:
                            st.then(ins, s_lny)
                        else:
                            st.then(ins)
                    if within and t == 1:
                        lo_to(*within[1])
                    for h in range(2):
                        st.then(v.bn_stats(stats[t][:, 6 * h:6 * h + 6], xtok[:, t, 512 * h:512 * h + 512]))
                    st.then(v.bn_aggr(mv[t], stats[t]))
                    st.mark(ts(vare[t], mv[t][:, 1:2], LNE, None, ALU.add), s_lnv)
                    if within:
                        lo_to(*within[2 * t])
                dve.wait_ge(s_lnr, NT * n + NT)
                x = xtok[:, 1, 0:512]
                st.mark(ts(x, x, mv[1][:, 0:1], rstd[1], ALU.subtract, ALU.mult), s_lnx)
                for piece in after:
                    lo_to(*piece)
                dve.wait_ge(s_lnT, NT * n + NT)
                for b in range(2, 4):
                    src, sl = bank(rota("lnT", n, b), 2, T), slice(2 * b, 2 * b + 2)
                    for m in range(2):
                        d = 2 * b + m
                        ins = ts(xf[:, d, :], src[:, m, :], pc(f"ln{n}_g", d), pc(f"ln{n}_b", d), ALU.mult, ALU.add)
                    st.then(ins)
                    st.then(v.tensor_copy(xT[0][:, sl, :], xf[:, sl, :]))
                    st.mark(tt(xT[1][:, sl, :], xf[:, sl, :], xT[0][:, sl, :], ALU.subtract), s_xTd)

            def hidden(i, j):
                lo_to(f"u{i}", j, 1, 1)
                dve.wait_ge(s_silu, i * (NF // 2) + j + 1)
                if i * (NF // 2) + j >= 2:
                    dve.wait_ge(s_hl, i * (NF // 2) + j - 1)
                done_chunk(dve, f"u{i}", j)
                st.mark(tt(htmp[j % 2], sil[j % 2], banks[rota(f"u{i}", j)][:, :], ALU.mult), s_h)

            dve.wait_ge(s_preT, 1)
            for b in range(2, 4):
                ins = v.tensor_copy(xf[:, 2 * b:2 * b + 2, :], bank(b, 2, T))
            ins.then_inc(s_preD, 1)
            dve.wait_ge(s_preD, 1)
            v.tensor_copy(xT[0][:, 4:8, :], xf[:, 4:8, :]).then_inc(s_preD, 1)
            dve.wait_ge(s_preD, 2)
            tt(xT[1][:, 4:8, :], xf[:, 4:8, :], xT[0][:, 4:8, :], ALU.subtract).then_inc(s_preX, 1)

            def prep():
                dve.wait_ge(s_rowsT, 1)
                o = banks[rota("rowsT", 0)]
                v.tensor_copy(pcol[:, 0:NA], o[:, 0:NA])
                st.then(v.tensor_copy(pcol[:, P:NB], o[:, P:NB]), s_pcol)
                lam = pc("lam", 0, NW)
                st.then(stt(alam, lam, -1.0, lam, ALU.mult, ALU.max), s_p1)

            def prep_a():
                lre, lim, lam = pc("lam_re", 0, NS), pc("lam_im", 0, NS), pc("lam", 0, NW)
                dve.wait_ge(s_p2, 1)
                st.then(tt(ang, lim, dt_, ALU.mult))
                st.then(tt(xr, lre, dt_, ALU.mult), s_p1)
                st.then(ts(rnd, ang, 1.0 / TWO_PI, MAGIC, ALU.mult, ALU.add))
                st.then(ts(rnd, rnd, MAGIC, None, ALU.subtract))
                for part in (PI_A, PI_B, PI_C):
                    st.then(stt(ang, rnd, -part, ang, ALU.mult, ALU.add))
                st.then(stt(aab, ang, -1.0, ang, ALU.mult, ALU.max), s_p1)
                st.then(ts(phi, ang, 1.0 / TWO_PI, None, ALU.mult))
                lo_to("g0", 3)
                dve.wait_ge(s_p2, 2)
                st.then(ts(w_, u_, 2.0, None, ALU.add))
                st.then(v.reciprocal(w_, w_))
                st.then(tt(w_, w_, u_, ALU.mult))
                st.then(tt(w2_, w_, w_, ALU.mult))
                st.then(ts(pl, w2_, 1.0 / 19.0, None, ALU.mult))
                for k in range(17, 1, -2):
                    st.then(stt(pl, pl, 1.0 / k, w2_, ALU.add, ALU.mult))
                st.then(stt(pl, pl, 1.0, w_, ALU.add, ALU.mult))
                lo_to("u0", 3, 0)
                st.then(ts(u_, lam, -1.0, 0.0, ALU.mult, ALU.max))
                st.then(stt(pl, pl, 2.0, u_, ALU.mult, ALU.add))
                v.tensor_scalar(sp8, pl, 8.0, None, ALU.mult)
                v.tensor_scalar(sp8n, pl, -8.0, None, ALU.mult)
                st.then(ts(omka, pc("k_a", 0, NW), -1.0, 1.0, ALU.mult, ALU.add))

            def prep_b():
                lre, lim = pc("lam_re", 0, NS), pc("lam_im", 0, NS)
                dve.wait_ge(s_p2, 6)
                st.then(stt(em, rho, 1.0, th, ALU.add, ALU.mult))
                st.then(tt(t1, s1, s1, ALU.mult))
                st.then(ts(t2, t1, -2.0, 1.0, ALU.mult, ALU.add))
                st.then(tt(t2, em, t2, ALU.mult))
                st.then(stt(nre, t1, -2.0, t2, ALU.mult, ALU.add))
                st.then(stt(t1, s1, 2.0, c1, ALU.mult, ALU.mult))
                lo_to("u0", 5)
                st.then(tt(nim, rho, t1, ALU.mult))
                st.then(tt(t1, lre, lre, ALU.mult))
                st.then(tt(t2, lim, lim, ALU.mult))
                st.then(tt(den, t1, t2, ALU.add))
                st.then(v.reciprocal(den, den))
                lo_to("u0", 5, 1, 1)
                st.then(tt(t1, nre, lre, ALU.mult))
                st.then(tt(t2, nim, lim, ALU.mult))
                st.then(tt(t1, t1, t2, ALU.add))
                st.then(tt(fr, t1, den, ALU.mult))
                st.then(tt(t1, nim, lre, ALU.mult))
                st.then(tt(t2, nre, lim, ALU.mult))
                st.then(tt(t1, t1, t2, ALU.subtract))
                st.then(tt(fi, t1, den, ALU.mult), s_p1)

            def rotation_angle(q):
                j, sl = 2 * q + 4, slice(4 * q, 4 * q + 4)
                time = const("time").unsqueeze(1).to_broadcast([P, 4, T])
                turns = phi[:, sl].unsqueeze(2).to_broadcast([P, 4, T])
                st.then(tt(rot[0], time, turns, ALU.mult))
                st.then(ts(rot[1], rot[0], MAGIC, None, ALU.add))
                lo_to("g0", j)
                st.then(ts(rot[1], rot[1], MAGIC, None, ALU.subtract))
                st.then(tt(rot[0], rot[0], rot[1], ALU.subtract), s_rot)
                lo_to("u0", j, 0)
                st.then(stt(rot[1], rot[0], -1.0, rot[0], ALU.mult, ALU.max), s_rot)

            def rotation_combine(q, before, within):
                sl = slice(4 * q, 4 * q + 4)
                lo_to(*before)
                lo_to(*within)
                dve.wait_ge(s_rots, 2 * q + 2)
                st.then(stt(rot[2], sinT[:, sl, :], -2.0, sinT[:, sl, :], ALU.mult, ALU.mult))
                st.then(stt(sinT[:, sl, :], sinT[:, sl, :], 2.0, cosT[:, sl, :], ALU.mult, ALU.mult), s_rot)
                st.then(ts(cosT[:, sl, :], rot[2], 1.0, None, ALU.add), s_rot)

            with dve.Fori(0, L) as l:
                st.n.clear()
                for j in range(NF // 2):
                    lo_to("g0", j, 0)
                    if j == 2:
                        prep()
                    if j == 3:
                        prep_a()
                    if j in (4, 6, 8, 10):
                        rotation_angle((j - 4) // 2)
                    if j in (5, 7, 9):
                        rotation_combine((j - 5) // 2, ("g0", j), ("u0", j, 0))
                    if j == 5:
                        prep_b()
                    hidden(0, j)
                rotation_combine(3, ("d0", NF // 2 - 2), ("d0", NF // 2 - 1, 0))
                lo_to("d0", NF // 2 - 1)
                lo_to("z", ZORD[0], 0)
                ln(0, "d0", NF // 2 - 1, 0.5 / ALPHA, [("z", ZORD[0])])

                def s5_forward(s):
                    dve.wait_ge(s_bu, s + 1)
                    src = bank(4 + s % 2, 2, T)
                    cs = cosT[:, s:s + 1, :].to_broadcast([P, 2, T])
                    sn = sinT[:, s:s + 1, :].to_broadcast([P, 2, T])
                    tt(s5m[:, 0, :, :], src, cs, ALU.mult)
                    st.then(tt(s5m[:, 1, :, :], src, sn, ALU.mult), s_fwd)
                    tt(s5v[:, 0, :], s5m[:, 0, 0, :], s5m[:, 1, 1, :], ALU.add)
                    st.then(tt(s5v[:, 1, :], s5m[:, 0, 1, :], s5m[:, 1, 0, :], ALU.subtract))
                    if s >= 2:
                        dve.wait_ge(s_back, s - 1)
                    for i in range(2):
                        ins = v.tensor_tensor_scan(s5z[s % 2][:, i, :], rho[:, s:s + 1].to_broadcast([P, T]),
                                                   s5v[:, i, :], 0.0, ALU.mult, ALU.add)
                    st.then(ins, s_scan)

                def s5_skip(t):
                    dve.wait_ge(s_y5, 4 * t + 4)
                    st.then(stt(zu[:, t, :], zu[:, t, :], pc("s5_d", t), banks[6 + t % 2][:, 0:T], ALU.mult, ALU.add),
                            s_y5d)

                lo_to("z", ZORD[1])
                dve.wait_ge(s_xg, 2 * NT)
                for s in range(NS):
                    lo_to("z", ZORD[2 + s // 2], s % 2)
                    s5_forward(s)
                    if s >= 6 and s % 4 == 2:
                        s5_skip((s - 6) // 4)

                def shift(a, n):
                    before = wk[6][:, 0:n, :]
                    st.then(tt(before, zrw[:, a:a + n, 0:T], zrw[:, a:a + n, 1:T + 1], ALU.subtract))
                    for t in range(n):
                        ins = stt(zrw[:, a + t, 1:T + 1], before[:, t, :], pc("mu", a + t), zrw[:, a + t, 1:T + 1],
                                  ALU.mult, ALU.add)
                        st.then(ins, s_shift)

                xc = wk[1]

                def convolve(t):
                    st.then(ts(xc[:, t, :], lx[:, t, 0:T], pc("conv_w", t), pc("conv_b", t), ALU.mult, ALU.add))
                    for k in range(1, 4):
                        ins = stt(xc[:, t, :], lx[:, t, k:k + T], pc("conv_w", 4 * k + t), xc[:, t, :], ALU.mult, ALU.add)
                        if k == 3:
                            st.then(ins, s_conv)
                        else:
                            st.then(ins)

                dve.wait_ge(s_z, 9)
                dve.wait_ge(s_zz, 2)
                lo_to("z", ZORD[10], 0)
                shift(12, 2)
                lo_to("z", ZORD[10])
                shift(4, 2)
                lo_to("z", ZORD[11], 0)
                shift(6, 2)
                lo_to("z", ZORD[11])
                dve.wait_ge(s_z, 11)
                convolve(0)
                lo_to("z", ZORD[12], 0)
                convolve(1)
                lo_to("z", ZORD[12])
                convolve(2)
                convolve(3)
                s5_skip(NW - 1)
                for t in range(NW):
                    ins = ts(kk[:, t, :], zrw[:, 4 + t, 1:T + 1], pc("k_k", t), None, ALU.mult)
                st.then(ins, s_kk)
                shift(0, 4)
                shift(8, 4)
                dve.wait_ge(s_nrm, 1)
                st.then(v.reciprocal(kk_norm, kk_norm))
                st.then(tt(kk, kk, kk_norm, ALU.mult))
                dve.wait_ge(s_lga, 12)
                a_, th_, gi_, h_ = wk[4], wk[5], wk[3], wk[6]
                st.then(tt(h_, a_, a_, ALU.mult))
                st.then(stt(th_, h_, 1.0, th_, ALU.add, ALU.mult), s_lq)
                st.then(tt(gi_, gi_, xc, ALU.mult))
                dve.wait_ge(s_lm, 1)
                st.then(tt(gi_, gi_, th_, ALU.mult))
                for t in range(NW):
                    st.then(v.tensor_tensor_scan(h_[:, t, :], a_[:, t, :], gi_[:, t, :], 0.0, ALU.mult, ALU.add))
                    st.then(tt(ly[:, t, :], h_[:, t, :], ly[:, t, :], ALU.mult), s_yl)

                r_, k_, v_ = (zrw[:, a:a + 4, 1:T + 1] for a in (0, 4, 8))
                sw, ra, dec, rk = wk[1], wk[2], wk[3], wk[7]
                dve.wait_ge(s_lora_a, 4)
                for t in range(NW):
                    ins = v.tensor_tensor_scan(dec[:, t, :], const("reset"), sw[:, t, :], 0.0, ALU.mult, ALU.add)
                st.then(ins)
                st.then(tt(sw, dec, sw, ALU.subtract), s_dec)
                dve.wait_ge(s_lora_a, 8)
                dve.wait_ge(s_lora, 3)
                for t in range(NW):
                    ins = ts(rk[:, t, :], ra[:, t, :], pc("k_a", t), omka[:, t:t + 1], ALU.mult, ALU.add)
                st.then(ins)
                st.then(tt(k_, k_, rk, ALU.mult))
                st.then(tt(rk, r_, k_, ALU.mult), s_rk)
                st.then(stt(ra, kk, -1.0, ra, ALU.mult, ALU.mult))
                def split(x):
                    return x.rearrange("p t (c s) -> p t c s", c=NC)

                dve.wait_ge(s_exp, 1)
                dve.wait_ge(s_y5d, NW)
                eN = wk[6]
                for t in range(NW):
                    tt(BK[:, t, :, 0, :], ra[:, t, :].rearrange("p (c s) -> p c s", c=NC),
                       eN[:, t, :].rearrange("p (c s) -> p c s", c=NC), ALU.mult)
                    tt(BK[:, t, :, 1, :], k_[:, t, :].rearrange("p (c s) -> p c s", c=NC),
                       eN[:, t, :].rearrange("p (c s) -> p c s", c=NC), ALU.mult)
                dve.wait_ge(s_exp, 2)
                for t in range(NW):
                    ins = tt(AR[:, t, :, 0, :], kk[:, t, :].rearrange("p (c s) -> p c s", c=NC),
                             wk[0][:, t, :].rearrange("p (c s) -> p c s", c=NC), ALU.mult)
                st.then(ins, s_ex)
                dve.wait_ge(s_exp, 3)
                for t in range(NW):
                    ins = tt(AR[:, t, :, 1, :], r_[:, t, :].rearrange("p (c s) -> p c s", c=NC),
                             wk[0][:, t, :].rearrange("p (c s) -> p c s", c=NC), ALU.mult)
                st.then(v.tensor_copy(pC, split(wk[0])[:, :, :, C - 1]), s_ops)
                dve.wait_ge(s_bon, 1)
                for h in range(2):
                    ins = tt(bonus[:, 2 * h:2 * h + 2, :], bank(4 + h, 2, T), v_[:, 2 * h:2 * h + 2, :], ALU.mult)
                st.then(ins, s_bonr)

                def merge(k):
                    j, b = (k % 4) // 2, k % 2
                    sl = slice(2 * (k % 4), 2 * (k % 4) + 2)
                    tmp = mtmp[:, 2 * b:2 * b + 2, :]
                    if k < 4:
                        dve.wait_ge(s_gact, k + 1)
                        dve.wait_ge(s_glu, k + 1)
                        done_chunk(dve, "w1", j)
                        st.then(tt(tmp, tmp, bank(rota("w1", j, b), 2, T), ALU.mult))
                        st.then(tt(merged[:, sl, :], tmp, gates[:, sl, :], ALU.mult), s_m)
                        return
                    kind = "lru" if k < 8 else "rw"
                    dve.wait_ge(s_gact, k + 1)
                    done_chunk(dve, kind, j)
                    st.then(tt(tmp, gates[:, sl, :], bank(rota(kind, j, b), 2, T), ALU.mult))
                    st.then(tt(merged[:, sl, :], merged[:, sl, :], tmp, ALU.add), s_m)

                merge(0)
                merge(1)
                dve.wait_ge(s_tok, 1)
                dve.wait_ge(s_back, NS)
                for b in range(2, 4):
                    st.mark(v.tensor_copy(BKtok[:, 4 * b:4 * b + 4, :], bank(4 + b, 4, P)), s_tokv)
                dve.wait_ge(s_tok, 2)
                for b in range(2, 4):
                    st.mark(v.tensor_copy(SV[C:P, :, 2 * b:2 * b + 2, :], bank(4 + b, 4, 2, C)[C:P]), s_tokv)
                G4 = G.rearrange("p (q h) s -> p q h s", h=2)
                for g in range(4):
                    dve.wait_ge(s_G, g + 1)
                    for par in range(2):
                        st.mark(tt(G4[:, 4 * g:4 * g + 4, par, :], bank(4 + 2 * (g % 2) + par, 4, P),
                                   const("maskG").unsqueeze(1).to_broadcast([P, 4, P]), ALU.mult), s_Ge)
                merge(2)
                merge(3)
                dve.wait_ge(s_N, 1)
                dve.wait_ge(s_p3, 5)
                for par in range(2):
                    r = slice(C * par, C * par + C)
                    for hf in range(2):
                        src = bank(4 + 2 * par + hf, 8, C)[r]
                        for name, dst in (("strict", W_bd[r, 8 * hf:8 * hf + 8, C * par:C * par + C]),
                                          ("off1", Wst[r, 8 * hf:8 * hf + 8, :])):
                            m = const(name)[r].unsqueeze(1).to_broadcast([C, 8, C])
                            ins = tt(dst, src, m, ALU.mult)
                            st.mark(ins, s_Nb)
                dve.wait_ge(s_Nb, 8)
                st.then(tt(Wst, Wst, const("eye2").unsqueeze(1).to_broadcast([P, NQ, C]), ALU.add), s_Wst)
                dve.wait_ge(s_T, 2)
                for b in range(2):
                    sl = slice(8 * b, 8 * b + 8)
                    st.mark(v.tensor_copy(W_bd[0:C, sl, 0:C], Wst[0:C, sl]), s_Wb)

                def turned(dst, n):
                    dve.wait_ge(s_T, 2 * n)
                    for b in range(2, 4):
                        ins = v.tensor_copy(dst[:, 4 * b:4 * b + 4, :], bank(4 + b, 4, P))
                    st.then(ins, s_Td)

                turned(M_bd, 1)
                turned(X_bd, 2)
                for i in range(5):
                    for b in range(2):
                        dve.wait_ge(s_WY, 2 * i + b + 1)
                        m = const(f"off{2 << i}").unsqueeze(1).to_broadcast([P, 8, C])
                        sl = slice(8 * b, 8 * b + 8)
                        st.then(tt(tmpB[:, sl, :], bank(6 + b, 8, C), m, ALU.mult), s_tmp)
                        st.mark(tt(W_bd[0:C, sl, 0:C], Wst[0:C, sl], tmpB[0:C, sl], ALU.add), s_Wb)
                    dve.wait_ge(s_Wb, 2 * (i + 2))
                    dve.wait_ge(s_Wp, 2 * (i + 2))
                    st.then(tt(Wst, Wst, tmpB, ALU.add), s_Wst)
                    turned(X_bd, i + 3)
                    if i == 4:
                        for k in range(4, 8):
                            merge(k)
                for c in range(NC):
                    dve.wait_ge(s_U, c + 1)
                    for par in range(2):
                        r = slice(C * par, C * par + C)
                        st.mark(v.tensor_copy(Usb[r], bank(4 + par, 2, NW, C)[r, 0]), s_Ue)
                    if c < NC - 1:
                        dve.wait_ge(s_Sn, c + 1)
                        pcb = pC[:, :, c:c + 1].to_broadcast([P, NW, C])
                        src, new = bank(7, 2, NW, C)[:, 0], S0[(c + 1) % 2]
                        if c:
                            st.then(tt(new, src, S0[c % 2], ALU.add))
                            st.then(tt(new, new, pcb, ALU.mult), s_S)
                        else:
                            st.then(tt(new, src, pcb, ALU.mult), s_S)
                lo_to("k", 0)
                dve.wait_ge(s_mean, 1)
                yc, sd = wk[0], wk[2]
                for h in range(2):
                    ins = stt(yc[:, 2 * h:2 * h + 2, :], bank(4 + h, 2, T), -1.0 / C, yT[:, 2 * h:2 * h + 2, :],
                              ALU.mult, ALU.add)
                st.then(ins, s_yc)
                for b in range(4):
                    dve.wait_ge(s_memTe, b + 1)
                    sl = slice(2 * b, 2 * b + 2)
                    st.mark(tt(memT[1][:, sl, :], bank(rota("memT", 0, b), 2, M), memT[0][:, sl, :], ALU.subtract),
                            s_memTl)
                lo_to("k", 1)
                dve.wait_ge(s_gnr, 1)
                for h in range(2):
                    st.then(v.reciprocal(sd[:, 2 * h:2 * h + 2, :], sd[:, 2 * h:2 * h + 2, :]))
                    lo_to("k", 2, h)
                st.then(tt(yc, yc, sd, ALU.mult))
                for t in range(NW):
                    ins = ts(yc[:, t, :], yc[:, t, :], pc("gn_g", t), pc("gn_b", t), ALU.mult, ALU.add)
                st.then(ins)
                lo_to("k", 3, 0)
                st.then(tt(yc, yc, bonus, ALU.add))
                st.then(tt(yc, yc, gRW, ALU.mult), s_yrw)

                def merged_lo(j):
                    dve.wait_ge(s_mh, j + 1)
                    sl = slice(2 * j, 2 * j + 2)
                    st.mark(tt(merged_r[1][:, sl, :], merged[:, sl, :], merged_r[0][:, sl, :], ALU.subtract), s_ml)

                lo_to("v", 1, 0)
                merge(8)
                merge(9)
                merged_lo(0)
                merged_lo(1)
                lo_to("v", 1)
                merge(10)
                merge(11)
                lo_to("mix", 0, 0)
                merged_lo(2)
                lo_to("mix", 0)
                merged_lo(3)
                lo_to("v", 2, 0)
                ln(1, "mix", 3, 1.0 / ALPHA, [("q", 0)], [("v", 2), ("v", 3, 0), ("v", 3)])

                def score_max(h):
                    dve.wait_ge(s_sc, h + 1)
                    k = slice(NT * h, NT * h + NT)
                    st.then(v.tensor_reduce(nmax[:, k], bank(rota("attn", h), NT, M), AX.X, ALU.max))
                    st.then(ts(nmax[:, k], nmax[:, k], -1.0 / 16.0, None, ALU.mult), s_mx)

                def normalise(h):
                    dve.wait_ge(s_ex2, h + 1)
                    k = slice(NT * h, NT * h + NT)
                    st.then(v.reciprocal(rinv[:, k], rsum[:, k]))
                    for t in range(NT):
                        ins = ts(attn_p[:, h, t, :], attn_p[:, h, t, :], rinv[:, NT * h + t:NT * h + t + 1], None,
                                 ALU.mult)
                    st.then(ins, s_pn)

                def o_evac(h):
                    dve.wait_ge(s_o, h + 1)
                    dve.wait_ge(s_oh, h + 1)
                    sl = slice(2 * h, 2 * h + 2)
                    st.mark(tt(oT[1][:, sl, :], bank(rota("attn", h), 2, T), oT[0][:, sl, :], ALU.subtract), s_oe)

                lo_to("q", 2, 0)
                score_max(0)
                lo_to("q", 3, 0)
                score_max(1)
                lo_to("q", 3)
                normalise(0)
                normalise(1)
                lo_to("wo", 0, 0)
                score_max(2)
                lo_to("wo", 0)
                normalise(2)
                o_evac(0)
                score_max(3)
                normalise(3)
                lo_to("wo", 1, 0)
                o_evac(1)
                lo_to("wo", 1)
                o_evac(2)
                lo_to("wo", 2, 0)
                o_evac(3)
                lo_to("g1", 0, 0)
                ln(2, "wo", 3, 1.0 / ALPHA, [("g1", 0)])
                for j in range(NF // 2):
                    hidden(1, j)
                lo_to("d1", NF // 2 - 1)
                ln(3, "d1", NF // 2 - 1, 0.5 / ALPHA, [])
                dve.wait_ge(s_lnw, 32 * 4)
                for k, op in enumerate((ALU.mult, ALU.add)):
                    st.then(tt(xtok[:, 1, :], xtok[:, 1, :], lnbc[:, k, :], op))
                layer_end(dve, "dve")

        @block.gpsimd
        def _(pool):
            st = Steps(pool, c_pool)
            g = nc.gpsimd
            tt = g.tensor_tensor
            g.memset(wgate[:, :], 0.0).then_inc(s_zero, 1)

            def ln(n):
                for t in range(NT):
                    pool.wait_ge(s_lnv, NT * n + t + 1)
                    st.then(tt(rstd[t], vare[t], NEG_HALF, ALU.pow))
                    st.then(g.tensor_scalar(nbias[t], mv[t][:, 0:1], rstd[t], -1.0, ALU.mult, ALU.mult), s_lnr)
                pool.wait_ge(s_lnw, 32 * (n + 1))
                for b in range(2):
                    pool.wait_ge(s_xTa, 2 * n + b + 1)
                    sl = slice(2 * b, 2 * b + 2)
                    st.mark(tt(xT[1][:, sl, :], xf[:, sl, :], xT[0][:, sl, :], ALU.subtract), s_xTp)
                for t in range(NT if n < 3 else 1):
                    pool.wait_ge(s_lnT, NT * n + t + 1)
                    st.then(tt(xtok[:, t, :], xtok[:, t, :], lnbc[:, 0, :], ALU.mult), s_xg)
                    st.then(tt(xtok[:, t, :], xtok[:, t, :], lnbc[:, 1, :], ALU.add), s_xg)

            def gate_lo(j, m):
                n = INDEX[("gate", j, m)]
                i = SPLIT_AT[n]
                pool.wait_ge(s_hi, i + 1)
                st.then(tt(split_flat(ring_lo, i), raw_flat(n), split_flat(ring_hi, i), ALU.subtract), s_lo["pool"])

            def hidden_lo(i, j):
                pool.wait_ge(s_hh, i * (NF // 2) + j + 1)
                hi, lo = (x[:, 2 * j:2 * j + 2, :].rearrange("p a t -> p (a t)") for x in hT)
                st.mark(tt(lo, htmp[j % 2], hi, ALU.subtract), s_hl)

            pool.wait_ge(s_preA, 2)
            tt(xT[1][:, 0:4, :], xf[:, 0:4, :], xT[0][:, 0:4, :], ALU.subtract).then_inc(s_preX, 1)
            pool.wait_ge(s_preX, 2)

            with pool.Fori(0, L) as l:
                st.n.clear()
                pool.wait_ge(s_zero, 1)
                pool.wait_ge(s_par, 16 * N_PAR_DMA)
                r0 = PCOL_A["log_dt"][0]
                g.tensor_copy(prow[r0:r0 + NS, 0, :].rearrange("s (g q) -> s g q", g=2),
                              dt_raw[r0:r0 + NS, :].unsqueeze(2).to_broadcast([NS, 2, 64])).then_inc(s_dtx, 1)
                pool.wait_ge(s_dtx, 1)
                for j in range(5):
                    hidden_lo(0, j)
                pool.wait_ge(s_raw, 16 * 13)
                pool.wait_ge(s_p1, 4)
                half_s, half_c = const("half_state"), const("half_chan")
                frb, fib = (x.unsqueeze(2).to_broadcast([P, NS, 16]) for x in (fr, fi))
                for i in range(2):
                    a, b = (frb, fib) if i == 0 else (fib, frb)
                    st.then(tt(bt_tmp[0], b_raw[0], a, ALU.mult))
                    st.then(tt(bt_tmp[1], b_raw[1], b, ALU.mult))
                    st.then(tt(bt_tmp[0], bt_tmp[0], bt_tmp[1], ALU.subtract if i == 0 else ALU.add))
                    for h in range(2):
                        dst = b_bd[i].rearrange("p t (s h c) -> p (t s) h c", s=4, h=2)[:, :, h, :]
                        ins = tt(dst, bt_tmp[0], half_s[:, h:h + 1].unsqueeze(2).to_broadcast([P, NS, 16]), ALU.mult)
                    st.then(ins, s_p3)
                    hidden_lo(0, 5 + i)
                for i in range(2):
                    for h in range(2):
                        ins = tt(c_bd[i][:, :, 64 * h:64 * h + 64], c_raw[i],
                                 half_c[:, h:h + 1].unsqueeze(2).to_broadcast([P, NW, C]), ALU.mult)
                    st.then(ins, s_p3)
                    hidden_lo(0, 7 + i)
                for j in range(9, NF // 2):
                    hidden_lo(0, j)
                ln(0)
                pool.wait_ge(s_bce, 4)
                pool.wait_ge(s_rot, 16)
                st.then(g.memset(zrw[:, :, 0:1], 0.0), s_zz)
                st.then(g.memset(lx[:, :, 0:3], 0.0), s_zz)
                for s in range(NS):
                    pool.wait_ge(s_scan, s + 1)
                    z = s5z[s % 2]
                    cs = cosT[:, s:s + 1, :].to_broadcast([P, 2, T])
                    sn = sinT[:, s:s + 1, :].to_broadcast([P, 2, T])
                    tt(s5n[:, 0, :, :], z, cs, ALU.mult)
                    st.then(tt(s5n[:, 1, :, :], z, sn, ALU.mult))
                    if s >= 2:
                        pool.wait_ge(s_y5, s - 1)
                    tt(s5s[s % 2][:, 0, :], s5n[:, 0, 0, :], s5n[:, 1, 1, :], ALU.subtract)
                    st.then(tt(s5s[s % 2][:, 1, :], s5n[:, 0, 1, :], s5n[:, 1, 0, :], ALU.add), s_back)
                for j in range(4):
                    for m in range(2):
                        gate_lo(j, m)
                pool.wait_ge(s_ops, 1)
                st.then(g.memset(W_bd[0:C, :, C:P], 0.0))
                st.then(g.memset(W_bd[C:P, :, 0:C], 0.0), s_p3)
                gate_lo(4, 0)
                gate_lo(4, 1)
                for i in range(6):
                    if i == 5:
                        gate_lo(8, 0)
                    r = slice(C, P)
                    for b in range(2):
                        sl = slice(8 * b, 8 * b + 8)
                        if i == 0:
                            pool.wait_ge(s_Wst, 1)
                            pool.wait_ge(s_T, 2)
                            st.then(g.tensor_copy(W_bd[r, sl, C:P], Wst[r, sl]), s_Wp)
                        else:
                            pool.wait_ge(s_tmp, 2 * (i - 1) + b + 1)
                            st.then(tt(W_bd[r, sl, C:P], Wst[r, sl], tmpB[r, sl], ALU.add), s_Wp)
                    if i < 3:
                        gate_lo(5 + i, 0)
                        gate_lo(5 + i, 1)
                gate_lo(8, 1)
                for j in range(9, 12):
                    gate_lo(j, 0)
                    gate_lo(j, 1)
                ln(1)
                ln(2)
                for j in range(NF // 2):
                    hidden_lo(1, j)
                ln(3)
                layer_end(pool, "pool")


N_PAR_DMA = len(ROWS_A) + len(ROWS_B)
_INS = ['x', 'mem', 'ffn1_wg', 'ffn1_wu', 'ffn1_wd', 'ln1_g', 'ln1_b', 'w_in', 's5_lam_re', 's5_lam_im', 's5_log_dt',
        's5_b_re', 's5_b_im', 's5_c_re', 's5_c_im', 's5_d', 's5_glu_w1', 's5_glu_w2', 'lru_conv_w', 'lru_conv_b',
        'lru_wa', 'lru_ba', 'lru_wx', 'lru_bx', 'lru_lambda', 'lru_w_out', 'rw_mu', 'rw_w0', 'rw_w_up', 'rw_a0',
        'rw_a_up', 'rw_g_up', 'rw_k_k', 'rw_k_a', 'rw_r_k', 'rw_ln_g', 'rw_ln_b', 'rw_w_out', 'mix_w_out', 'ln2_g',
        'ln2_b', 'xa_wq', 'xa_wkv', 'xa_wo', 'ln3_g', 'ln3_b', 'ffn2_wg', 'ffn2_wu', 'ffn2_wd', 'ln4_g', 'ln4_b']


def kernel(**inputs):
    import concourse.bacc as _bacc
    from concourse.bass_utils import run_bass_kernel_spmd as _run

    nc = _bacc.Bacc("TRN2", target_bir_lowering=False, num_devices=1)
    arrays, io = {}, {}
    for name in _INS:
        a = np.ascontiguousarray(inputs[name])
        arrays[f"in_{name}_dram"] = a
        io[name] = nc.dram_tensor(f"in_{name}_dram", a.shape, mybir.dt.from_np(a.dtype), kind="ExternalInput").ap()
    c = constants()
    arrays["constants_dram"] = c
    consts = nc.dram_tensor("constants_dram", c.shape, F32, kind="ExternalInput").ap()
    out = nc.dram_tensor("out_0_dram", (1, T, D), F32, kind="ExternalOutput").ap()
    trunk(nc, io, consts, out)
    r = _run(nc, [arrays], core_ids=[0])
    return r.results[0]["out_0_dram"]
```
